# Optimizing a Trainium2 kernel written in Bass

```python
import math
import jax, jax.numpy as jnp
from jax import lax
import numpy as np

D_MODEL = 1024
BATCH = 1
SEQ = 2048
DEPTH = 1
DEC_BATCH = 8
DEC_SEQ = 4
PAST_LEN = 2048
PAGE_SIZE = 128

DN_HEADS = 4
DN_DK = 128
DN_DV = 128
QK_W = DN_HEADS * DN_DK
DN_WIDTH = DN_HEADS * DN_DV
CONV_W = 4
CONV_CH = 2 * QK_W + DN_WIDTH
DN_CHUNK = 64
SW_HEADS = 8
SW_HD = 64
SW_WIDTH = SW_HEADS * SW_HD
DILATIONS = ((128, 1), (512, 4), (2048, 16))
WIN_MAX = 2048
D_MIX = DN_WIDTH + SW_WIDTH
D_IN = CONV_CH + DN_WIDTH + 2 * DN_HEADS + 3 * SW_WIDTH + SW_WIDTH
NORM_EPS = 1e-6

kernel_name = 'hymba_gdn_dilated_swa_step'

def rmsnorm(x, g):
    xf = x.astype(jnp.float32)
    xf = xf * lax.rsqrt(jnp.mean(xf * xf, axis=-1, keepdims=True) + NORM_EPS)
    return xf.astype(x.dtype) * g

def l2normalize(x):
    xf = x.astype(jnp.float32)
    return xf * lax.rsqrt(jnp.sum(xf * xf, axis=-1, keepdims=True) + NORM_EPS)

def causal_short_conv(x_ext, w):
    L = x_ext.shape[1] - (CONV_W - 1)
    y = w[0] * x_ext[:, 0:L]
    for j in range(1, CONV_W):
        y = y + w[j] * x_ext[:, j:j + L]
    return jax.nn.silu(y)

def gated_delta_rule(q, k, v, g, beta, s0):
    B_, L, H, _ = q.shape
    dv = v.shape[-1]
    C = min(DN_CHUNK, L)
    n = -(-L // C)
    pad = n * C - L
    f32 = jnp.float32

    def blocks(t):
        t = jnp.pad(t.astype(f32), [(0, 0), (0, pad)] + [(0, 0)] * (t.ndim - 2))
        t = jnp.moveaxis(t, 1, 2)
        return t.reshape(t.shape[:2] + (n, C) + t.shape[3:])

    q, k, v, g, beta = (blocks(t) for t in (q, k, v, g, beta))
    gc = jnp.cumsum(g, axis=-1)
    incl = jnp.tril(jnp.ones((C, C), dtype=bool))
    strict = jnp.tril(jnp.ones((C, C), dtype=bool), -1)
    decay = jnp.exp(jnp.where(incl, gc[..., :, None] - gc[..., None, :], -jnp.inf))
    kb = k * beta[..., None]
    a_mat = jnp.where(strict, jnp.einsum('bhnid,bhnjd->bhnij', kb, k) * decay, 0.0)
    rhs = jnp.concatenate([v * beta[..., None], kb * jnp.exp(gc)[..., None]], axis=-1)
    sol = lax.linalg.triangular_solve(jnp.eye(C, dtype=f32) + a_mat, rhs,
                                      left_side=True, lower=True, unit_diagonal=True)
    u, w = sol[..., :dv], sol[..., dv:]
    attn = jnp.einsum('bhnid,bhnjd->bhnij', q, k) * decay
    q_dec = q * jnp.exp(gc)[..., None]
    k_dec = k * jnp.exp(gc[..., -1:] - gc)[..., None]
    g_last = jnp.exp(gc[..., -1])

    def step(S, xs):
        u_c, w_c, q_c, k_c, a_c, gl = xs
        v_new = u_c - jnp.einsum('bhck,bhkv->bhcv', w_c, S)
        o_c = jnp.einsum('bhck,bhkv->bhcv', q_c, S) + jnp.einsum('bhij,bhjv->bhiv', a_c, v_new)
        S = S * gl[..., None, None] + jnp.einsum('bhck,bhcv->bhkv', k_c, v_new)
        return S, o_c

    xs = tuple(jnp.moveaxis(t, 2, 0) for t in (u, w, q_dec, k_dec, attn, g_last))
    S, o = lax.scan(step, s0.astype(f32), xs)
    o = jnp.moveaxis(o, 0, 2).reshape(B_, H, n * C, dv)[:, :, :L]
    return jnp.moveaxis(o, 2, 1), S

def banded_window_attn(q, k, v, steps):
    N, n, H, hd = q.shape
    blk = steps
    nb = -(-n // blk)
    pad = nb * blk - n
    f32 = jnp.float32

    def to_blocks(t):
        t = jnp.pad(t, ((0, 0), (0, pad), (0, 0), (0, 0)))
        return t.reshape(N, nb, blk, H, hd)

    qb, kb, vb = to_blocks(q), to_blocks(k), to_blocks(v)
    prev = lambda t: jnp.pad(t, ((0, 0), (1, 0), (0, 0), (0, 0), (0, 0)))[:, :-1]
    kk = jnp.concatenate([prev(kb), kb], axis=2)
    vv = jnp.concatenate([prev(vb), vb], axis=2)
    s = jnp.einsum('ncqhd,nckhd->nchqk', qb, kk).astype(f32) * (hd ** -0.5)
    qi = jnp.arange(blk)[:, None]
    kj = jnp.arange(2 * blk)[None, :]
    band = (kj >= blk + qi - steps) & (kj <= blk + qi)
    has_prev = (jnp.arange(nb) > 0)[:, None, None] | (kj >= blk)[None]
    mask = band[None] & has_prev
    s = jnp.where(mask[None, :, None], s, -jnp.inf)
    m = jnp.max(s, axis=-1)
    p = jnp.exp(s - m[..., None])
    l = jnp.sum(p, axis=-1)
    num = jnp.einsum('nchqk,nckhd->ncqhd', p, vv.astype(f32)).reshape(N, nb * blk, H, hd)[:, :n]
    m = jnp.moveaxis(m, 2, 3).reshape(N, nb * blk, H)[:, :n]
    l = jnp.moveaxis(l, 2, 3).reshape(N, nb * blk, H)[:, :n]
    return num, m, l

def dilated_branch_prompt(q, k, v, steps, d):
    B_, S_, H, hd = q.shape
    n = S_ // d
    to_sub = lambda t: t.reshape(B_, n, d, H, hd).transpose(0, 2, 1, 3, 4).reshape(B_ * d, n, H, hd)
    num, m, l = banded_window_attn(to_sub(q), to_sub(k), to_sub(v), steps)
    num = num.reshape(B_, d, n, H, hd).transpose(0, 2, 1, 3, 4).reshape(B_, S_, H, hd)
    m = m.reshape(B_, d, n, H).transpose(0, 2, 1, 3).reshape(B_, S_, H)
    l = l.reshape(B_, d, n, H).transpose(0, 2, 1, 3).reshape(B_, S_, H)
    return num, m, l

def dilated_branch_sample(q, k_ext, v_ext, steps, d):
    T = q.shape[1]
    hd = q.shape[-1]
    lbuf = k_ext.shape[1] - T
    idx = lbuf + jnp.arange(T)[:, None] - d * jnp.arange(steps + 1)[None, :]
    valid = idx >= 0
    idx = jnp.maximum(idx, 0)
    kg = jnp.take(k_ext, idx, axis=1)
    vg = jnp.take(v_ext, idx, axis=1)
    s = jnp.einsum('bthd,btjhd->bthj', q, kg).astype(jnp.float32) * (hd ** -0.5)
    s = jnp.where(valid[None, :, None, :], s, -jnp.inf)
    m = jnp.max(s, axis=-1)
    p = jnp.exp(s - m[..., None])
    l = jnp.sum(p, axis=-1)
    num = jnp.einsum('bthj,btjhd->bthd', p, vg.astype(jnp.float32))
    return num, m, l

def merge_dilations(parts):
    ms = jnp.stack([m for _, m, _ in parts])
    mx = jnp.max(ms, axis=0)
    wts = jnp.exp(ms - mx)
    num = sum(wts[i][..., None] * parts[i][0] for i in range(len(parts)))
    den = sum(wts[i] * parts[i][2] for i in range(len(parts)))
    return num / den[..., None]

def hybrid_layer(x, conv_prefix, s0, k_win, v_win, norm_g, w_in, conv_w, a_log, dt_bias, dn_norm_g, w_out):
    B_, L, _ = x.shape
    f32 = jnp.float32
    h = rmsnorm(x, norm_g)
    proj = jnp.einsum('bld,de->ble', h, w_in)
    o0 = CONV_CH
    o1 = o0 + DN_WIDTH
    o2 = o1 + DN_HEADS
    o3 = o2 + DN_HEADS
    o4 = o3 + 3 * SW_WIDTH
    qkv_raw, z_a, a_in, b_in = proj[..., :o0], proj[..., o0:o1], proj[..., o1:o2], proj[..., o2:o3]
    qkv_b, z_b = proj[..., o3:o4], proj[..., o4:]

    x_ext = jnp.concatenate([conv_prefix.astype(x.dtype), qkv_raw], axis=1)
    qkv = causal_short_conv(x_ext, conv_w)
    new_conv = x_ext[:, -(CONV_W - 1):]
    qa, ka, va = jnp.split(qkv, [QK_W, 2 * QK_W], axis=-1)
    qa = l2normalize(qa.reshape(B_, L, DN_HEADS, DN_DK)) * (DN_DK ** -0.5)
    ka = l2normalize(ka.reshape(B_, L, DN_HEADS, DN_DK))
    va = va.reshape(B_, L, DN_HEADS, DN_DV)
    g = -jnp.exp(a_log.astype(f32)) * jax.nn.softplus(a_in.astype(f32) + dt_bias.astype(f32))
    beta = jax.nn.sigmoid(b_in.astype(f32))
    o_a, s_new = gated_delta_rule(qa, ka, va, g, beta, s0)
    o_a = rmsnorm(o_a.astype(x.dtype), dn_norm_g) * jax.nn.silu(z_a.reshape(B_, L, DN_HEADS, DN_DV))

    qb, kb, vb = (t.reshape(B_, L, SW_HEADS, SW_HD) for t in jnp.split(qkv_b, 3, axis=-1))
    if k_win is None:
        parts = [dilated_branch_prompt(qb, kb, vb, w // d, d) for w, d in DILATIONS]
        keep = min(WIN_MAX, L)
        new_k, new_v = kb[:, L - keep:], vb[:, L - keep:]
    else:
        k_ext = jnp.concatenate([k_win.astype(x.dtype), kb], axis=1)
        v_ext = jnp.concatenate([v_win.astype(x.dtype), vb], axis=1)
        parts = [dilated_branch_sample(qb, k_ext, v_ext, w // d, d) for w, d in DILATIONS]
        keep = k_win.shape[1]
        new_k, new_v = k_ext[:, -keep:], v_ext[:, -keep:]
    o_b = merge_dilations(parts).astype(x.dtype) * jax.nn.silu(z_b.reshape(B_, L, SW_HEADS, SW_HD))

    mix = jnp.concatenate([o_a.reshape(B_, L, DN_WIDTH), o_b.reshape(B_, L, SW_WIDTH)], axis=-1)
    y = x + jnp.einsum('ble,ed->bld', mix, w_out)
    return y, new_conv, s_new.astype(x.dtype), new_k, new_v

def setup_inputs(seed: int = 0) -> dict:
    key = jax.random.key(seed)
    ks = jax.random.split(key, 16)
    lbuf = min(WIN_MAX, PAST_LEN)
    nrm = jax.random.normal
    x_prompt = nrm(ks[0], (BATCH, SEQ, D_MODEL), jnp.float32)
    x_sample = nrm(ks[1], (DEC_BATCH, DEC_SEQ, D_MODEL), jnp.float32)
    state_conv = nrm(ks[2], (DEPTH, DEC_BATCH, CONV_W - 1, CONV_CH), jnp.float32)
    state_delta = 0.1 * nrm(ks[3], (DEPTH, DEC_BATCH, DN_HEADS, DN_DK, DN_DV), jnp.float32)
    cache_k_win = nrm(ks[4], (DEPTH, DEC_BATCH, lbuf, SW_HEADS, SW_HD), jnp.float32)
    cache_v_win = nrm(ks[5], (DEPTH, DEC_BATCH, lbuf, SW_HEADS, SW_HD), jnp.float32)
    norm_g = 1.0 + 0.01 * nrm(ks[6], (DEPTH, D_MODEL), jnp.float32)
    final_norm_g = 1.0 + 0.01 * nrm(ks[7], (D_MODEL,), jnp.float32)
    w_in = nrm(ks[8], (DEPTH, D_MODEL, D_IN), jnp.float32) * (D_MODEL ** -0.5)
    conv_w = nrm(ks[9], (DEPTH, CONV_W, CONV_CH), jnp.float32) * (CONV_W ** -0.5)
    a_log = jnp.log(jax.random.uniform(ks[10], (DEPTH, DN_HEADS), jnp.float32, 1.0, 16.0))
    dt = jnp.exp(jax.random.uniform(ks[11], (DEPTH, DN_HEADS), jnp.float32, math.log(1e-3), math.log(1e-1)))
    dt_bias = dt + jnp.log(-jnp.expm1(-dt))
    dn_norm_g = 1.0 + 0.01 * nrm(ks[12], (DEPTH, DN_DV), jnp.float32)
    w_out = nrm(ks[13], (DEPTH, D_MIX, D_MODEL), jnp.float32) * (D_MIX ** -0.5)
    return {'x_prompt': x_prompt, 'x_sample': x_sample, 'state_conv': state_conv,
            'state_delta': state_delta, 'cache_k_win': cache_k_win, 'cache_v_win': cache_v_win,
            'norm_g': norm_g, 'final_norm_g': final_norm_g, 'w_in': w_in, 'conv_w': conv_w,
            'a_log': a_log, 'dt_bias': dt_bias, 'dn_norm_g': dn_norm_g, 'w_out': w_out}

def reference(x_prompt, x_sample, state_conv, state_delta, cache_k_win, cache_v_win,
              norm_g, final_norm_g, w_in, conv_w, a_log, dt_bias, dn_norm_g, w_out):
    yp, ys = x_prompt, x_sample
    bp = x_prompt.shape[0]
    p_conv, p_delta, p_k, p_v = [], [], [], []
    s_conv, s_delta, s_k, s_v = [], [], [], []
    for l in range(DEPTH):
        weights = (norm_g[l], w_in[l], conv_w[l], a_log[l], dt_bias[l], dn_norm_g[l], w_out[l])
        zero_conv = jnp.zeros((bp, CONV_W - 1, CONV_CH), x_prompt.dtype)
        zero_state = jnp.zeros((bp, DN_HEADS, DN_DK, DN_DV), jnp.float32)
        yp, c, s, k, v = hybrid_layer(yp, zero_conv, zero_state, None, None, *weights)
        p_conv.append(c); p_delta.append(s); p_k.append(k); p_v.append(v)
        ys, c, s, k, v = hybrid_layer(ys, state_conv[l], state_delta[l], cache_k_win[l], cache_v_win[l], *weights)
        s_conv.append(c); s_delta.append(s); s_k.append(k); s_v.append(v)
    y_prompt = rmsnorm(yp, final_norm_g)
    y_sample = rmsnorm(ys, final_norm_g)
    new_conv_prompt = jnp.stack(p_conv)
    new_delta_prompt = jnp.stack(p_delta)
    new_k_win_prompt = jnp.stack(p_k)
    new_v_win_prompt = jnp.stack(p_v)
    new_conv_sample = jnp.stack(s_conv)
    new_delta_sample = jnp.stack(s_delta)
    new_k_win_sample = jnp.stack(s_k)
    new_v_win_sample = jnp.stack(s_v)
    return (y_prompt, y_sample, new_conv_prompt, new_delta_prompt, new_k_win_prompt, new_v_win_prompt,
            new_conv_sample, new_delta_sample, new_k_win_sample, new_v_win_sample)


_drawn_inputs = setup_inputs


def setup_inputs(seed=0):
    import zlib

    import numpy as np

    out = dict(_drawn_inputs(seed))
    spreads = {}
    factors = {'norm_g': 3.386, 'final_norm_g': 5.718, 'dn_norm_g': 8.0}
    for name, (base, spread) in spreads.items():
        noise = np.random.default_rng([zlib.crc32(name.encode()), seed]).standard_normal(out[name].shape)
        drawn = base * np.exp(spread * noise) if base else spread * noise
        out[name] = __import__('jax').numpy.asarray(drawn.astype(out[name].dtype))
    for name, factor in factors.items():
        out[name] = (out[name] * factor).astype(out[name].dtype)
    return out
```

```python
from contextlib import ExitStack

import concourse.bass as bass
from concourse import mybir

F32 = mybir.dt.float32
F32R = mybir.dt.float32r
BF16 = mybir.dt.bfloat16
I32 = mybir.dt.int32
ALU = mybir.AluOpType
ACT = mybir.ActivationFunctionType
AX = mybir.AxisListType

P = 128
D_MODEL = 1024
SEQ = 2048
DEC_BATCH = 8
DEC_SEQ = 4
NS = DEC_BATCH * DEC_SEQ
PAST = 2048
CONV_W = 4
TAIL = CONV_W - 1
DN_HEADS = 4
DK = 128
QK_W = DN_HEADS * DK
CONV_CH = 3 * QK_W
SW_HEADS = 8
HD = 64
SW_WIDTH = SW_HEADS * HD
EPS = 1e-6
KT = D_MODEL // P
CHUNK = 512
NCH = SEQ // CHUNK
NT = SEQ // P
KINDS = ("q", "k", "v", "za", "wq", "wk", "wv", "zb")
NK = len(KINDS)
O_AB = CONV_CH + QK_W
O_WIN = O_AB + 2 * DN_HEADS
COLS = (0, QK_W, 2 * QK_W, CONV_CH, O_WIN, O_WIN + SW_WIDTH, O_WIN + 2 * SW_WIDTH, O_WIN + 3 * SW_WIDTH)
NJ = QK_W // P
NTILES = NK * NJ
POSTED = ("q", "k", "v", "wk", "wv")
TURNED = ("k", "v", "wk", "wv")


def flat(t):
    return t.rearrange("p a b -> p (a b)")


def constants(nc, env, ctx):
    sb = lambda n, s, d=F32: ctx.enter_context(nc.sbuf_tensor(n, s, d))
    env.ident = sb("ident", [P, P])
    env.ones = sb("ones", [P, P])
    env.sam = sb("sam", [P, NK, NJ, NS])
    env.ab_tok = sb("ab_tok", [P, NT + 1, 8])
    env.ssq = sb("ssq", [P, NT, 2, NJ])
    env.conv_tail = sb("conv_tail", [P, 3 * NJ, TAIL])
    env.conv_wt = sb("conv_wt", [P, 3 * NJ, CONV_W])
    env.g_in = sb("g_in", [P, KT])


def project(nc, env, D):
    with ExitStack() as ctx:
        sb = lambda n, s, d=F32: ctx.enter_context(nc.sbuf_tensor(n, s, d))
        ps = lambda n: ctx.enter_context(nc.psum_tensor(n, [P, CHUNK], F32))
        sem = env.sem
        ident, ones, sam, ab_tok, ssq, g_in = env.ident, env.ones, env.sam, env.ab_tok, env.ssq, env.g_in
        conv_tail, conv_wt = env.conv_tail, env.conv_wt

        TOK = SEQ + NS
        hT_hi = sb("hT_hi", [P, KT, TOK], F32R)
        hT_lo = sb("hT_lo", [P, KT, TOK], F32R)
        w_raw = sb("w_raw", [P, 2, KT, P])
        w_hi = [sb(f"w_hi{s}", [P, KT, P], F32R) for s in range(2)]
        w_lo = [sb(f"w_lo{s}", [P, KT, P], F32R) for s in range(2)]
        raw = sb("raw", [P, TAIL + SEQ])
        acc = sb("acc", [P, 2, CHUNK])
        sil = sb("sil", [P, NCH, CHUNK])
        sq = sb("sq", [P, 2, CHUNK])
        hi = sb("hi", [P, 2, CHUNK], F32R)
        lo = sb("lo", [P, 2, CHUNK], F32R)
        xr = sb("xr", [P, 2, D_MODEL])
        tmp = acc
        tok, zr = (xr[:, s, :].rearrange("p (a b) -> p a b", a=2) for s in range(2))
        junk = flat(sil[:, 0:2, :])
        stat = sb("stat", [P, 2, 4])
        abT = flat(sil)[0:2 * DN_HEADS, :]
        ab_sam = sb("ab_sam", [2 * DN_HEADS, NS])

        pj = [ps(f"pj{c}") for c in range(NCH)]
        tp = [ps(f"tp{c}") for c in range(2)]
        p_sam = ps("p_sam")
        p_ssq = ps("p_ssq")

        ident_set, ident_done, ones_done, consts_in = (sem(n) for n in ("ident_set", "ident_done", "ones_done", "consts_in"))
        w_loaded, x_loaded = [sem(f"w_loaded{s}") for s in range(2)], [sem(f"x_loaded{s}") for s in range(2)]
        sq_summed, ms_done, root_done, inv_done, xn_done = (sem(n) for n in ("sq_summed", "ms_done", "root_done", "inv_done", "xn_done"))
        xT_done, tmp_done, hT_hi_done, hT_lo_done = (sem(n) for n in ("xT_done", "tmp_done", "hT_hi_done", "hT_lo_done"))
        w_hi_done, w_lo_done, pj_done, sam_mm, sam_free = (sem(n) for n in ("w_hi_done", "w_lo_done", "pj_done", "sam_mm", "sam_free"))
        pj_free = [sem(f"pj_free{c}") for c in range(NCH)]
        chain, conv_done, sil_done, sq_done = (sem(n) for n in ("chain", "conv_done", "sil_done", "sq_done"))
        post_done, tok_done, ssq_read, hi_done, w_f32_done = (sem(n) for n in ("post_done", "tok_done", "ssq_read", "hi_done", "w_f32_done"))
        sil_stored = [sem(f"sil_stored{c}") for c in range(NCH)]
        tok_stored, hi_stored, lo_stored, z_stored = ([sem(f"{n}{s}") for s in range(2)] for n in ("tok_stored", "hi_stored", "lo_stored", "z_stored"))
        seen = sem("seen")
        shifted, tail_done, tail_stored = sem("shifted"), sem("tail_done"), sem("tail_stored")
        raw_head, ab_evac, ab_turned = sem("raw_head"), sem("ab_evac"), sem("ab_turned")
        block = ctx.enter_context(nc.Block())

        X_CREDIT = 4
        TMP_CREDIT = 2
        W_CREDIT = 2
        CONV_CREDIT = 4
        SIL_CREDIT = 2
        POST_CREDIT = 4
        TOK_CREDIT = 2
        SSQ_CREDIT = 1

        def lagged(y, c):
            return (KINDS[y], c - 2) if c >= 2 else (KINDS[y - 1] if y else None, c + 2)

        def posts_before(j, kind, c):
            return 4 * (len(POSTED) * j + POSTED.index(kind)) + c

        def turned_before(j, kind, c):
            return 4 * (len(TURNED) * j + TURNED.index(kind)) + c

        @block.sync
        def _(sp):
            with nc.allow_non_contiguous_dma(reason="a few weights, once"):
                sp.dma_start(g_in[:], D.norm_g.rearrange("(k p) -> p k", p=P)).then_inc(consts_in, 16)
                for r in range(CONV_W):
                    sp.dma_start(conv_wt[:, :, r], D.conv_w[r].rearrange("(t p) -> p t", p=P)).then_inc(consts_in, 16)
            with sp.Fori(0, NT // 2) as i:
                for s in range(2):
                    n = 2 * i + s
                    sp.wait_ge(xT_done, 2 * n + 2)
                    sp.dma_start(xr[:, s, :], D.x[bass.ds(P * n, P), :]).then_inc(x_loaded[s], 16)
            sp.wait_ge(xT_done, 2 * NT + 2)
            sp.dma_start(xr[0:NS, 0, :], D.x_sample).then_inc(x_loaded[0], 16)

            def load_w(j, y):
                src = D.w_in[:, bass.ds(P * j + COLS[y], P)].rearrange("(k p) c -> p k c", p=P)
                sp.dma_start(w_raw[:, y % 2], src).then_inc(w_loaded[y % 2], 16)

            for s in range(2):
                for stored in (hi_stored, lo_stored, z_stored, tok_stored):
                    sp.sem_inc(stored[s], 16)
                load_w(0, s)

            def store_turned(j, kind, c):
                sp.wait_ge(tok_done, TOK_CREDIT + turned_before(j, kind, c) + 1)
                sp.sem_inc(seen, 1)
                dst = {"k": D.k_tok, "v": D.v_tok, "wk": D.new_k, "wv": D.new_v}[kind]
                dst = dst[CHUNK * c:CHUNK * (c + 1), bass.ds(P * j, P)].rearrange("(b p) d -> p b d", p=P)
                sp.dma_start(dst, tok[:, c % 2, :].rearrange("p (b d) -> p b d", b=4)).then_inc(tok_stored[c % 2], 16)

            with sp.Fori(0, NJ) as j:
                for y, kind in enumerate(KINDS):
                    sp.wait_ge(w_lo_done, W_CREDIT + NK * j + y + 1)
                    load_w(j + (y + 2) // NK, (y + 2) % NK)
                    rows = bass.ds(P * j, P)
                    for c in range(NCH):
                        cs = slice(CHUNK * c, CHUNK * (c + 1))
                        if kind in ("q", "k"):
                            sp.wait_ge(sil_done, SIL_CREDIT + 4 * (3 * j + y) + c + 1)
                            sp.dma_start(D.qk_ch[y, rows, cs], sil[:, c, :]).then_inc(sil_stored[c], 16)
                        if kind in ("za", "zb"):
                            sp.wait_ge(pj_free[c], NK * j + y + 2)
                            sp.dma_start(D.z_ch[int(kind == "zb"), rows, cs], zr[:, c % 2, :]).then_inc(z_stored[c % 2], 16)
                        if kind in ("wq", "wk"):
                            q = int(kind == "wk")
                            sp.wait_ge(hi_done, 4 * (2 * j + q) + c + 1)
                            sp.dma_start(D.wqk[q, 0, rows, cs], hi[:, c % 2, :].bitcast(F32)).then_inc(hi_stored[c % 2], 16)
                            sp.wait_ge(pj_free[c], NK * j + y + 2)
                            sp.dma_start(D.wqk[q, 1, rows, cs], lo[:, c % 2, :].bitcast(F32)).then_inc(lo_stored[c % 2], 16)
                        back, bc = lagged(y, c)
                        if back in TURNED:
                            store_turned(j, back, bc)
            sp.wait_ge(w_lo_done, W_CREDIT + NTILES + 1)
            sp.dma_start(w_raw[:, 0], D.w_in[:, O_AB:O_AB + P].rearrange("(k p) c -> p k c", p=P)).then_inc(w_loaded[0], 16)
            sp.wait_ge(tail_done, 3 * NJ)
            with nc.allow_non_contiguous_dma(reason="the last three rows of a channel-major tile"):
                for r in range(TAIL):
                    sp.dma_start(D.new_conv[r].rearrange("(t p) -> p t", p=P), conv_tail[:, :, r]).then_inc(tail_stored, 16)
            sp.wait_ge(w_loaded[1], 16 * (NTILES // 2 + 1))
            sp.wait_ge(tail_stored, 16 * TAIL)
            for c in range(NCH):
                sp.wait_ge(sil_stored[c], 16 * 2 * NJ)
            for s in range(2):
                sp.wait_ge(hi_stored[s], 16 + 16 * 4 * NJ)
                sp.wait_ge(lo_stored[s], 16 + 16 * 4 * NJ)
                sp.wait_ge(z_stored[s], 16 + 16 * 4 * NJ)
                sp.wait_ge(tok_stored[s], 16 + 16 * 8 * NJ)

        @block.gpsimd
        def _(pool):
            pool.memset(ident[:], 0.0).then_inc(ident_set, 1)
            pool.memset(ones[:], 1.0).then_inc(ones_done, 1)
            pool.wait_ge(ident_set, 1)
            pool.affine_select(out=ident[:], in_=ident[:], compare_op=ALU.not_equal, fill=1.0, base=0,
                               pattern=[[-1, P]], channel_multiplier=1).then_inc(ident_done, 1)
            pool.memset(raw[:, 0:TAIL], 0.0).then_inc(raw_head, 1)
            pool.sem_inc(hT_lo_done, TMP_CREDIT)

            def h_low(n, rows, cols):
                for b in range(2):
                    pool.wait_ge(hT_hi_done, 2 * n + b + 1)
                    ks = slice(4 * b, 4 * b + 4)
                    t = tmp[:, b, 0:4 * rows].rearrange("p (k t) -> p k t", k=4)
                    pool.tensor_tensor(hT_lo[:, ks, cols], t, hT_hi[:, ks, cols].bitcast(F32), ALU.subtract).then_inc(hT_lo_done, 1)

            with pool.Fori(0, NT) as n:
                h_low(n, P, bass.ds(P * n, P))
            h_low(NT, NS, slice(SEQ, TOK))

            with pool.Fori(0, DEC_BATCH) as b:
                pool.wait_ge(pj_done, 16 * b + 1)
                pool.sem_inc(seen, 1)
                for old, new in ((D.cache_k, D.out_k), (D.cache_v, D.out_v)):
                    pool.dma_start(new[bass.ds(b, 1), 0:PAST - DEC_SEQ, :], old[bass.ds(b, 1), DEC_SEQ:PAST, :]).then_inc(shifted, 16)
            pool.wait_ge(shifted, 16 * 2 * DEC_BATCH)

        @block.tensor
        def _(pe):
            pe.sem_inc(xT_done, X_CREDIT)
            pe.wait_ge(ident_done, 1)

            def turn_x(n, s, rows):
                pe.wait_ge(xn_done, n + 1)
                for b in range(2):
                    pe.wait_ge(tmp_done, 2 * n + b + 1)
                    for k in range(4):
                        x_k = xr[0:rows, s, (4 * b + k) * P:(4 * b + k + 1) * P]
                        mm = pe.transpose(pj[b][:, k * rows:(k + 1) * rows], x_k, ident[0:rows, 0:rows])
                    mm.then_inc(xT_done, 1)

            with pe.Fori(0, NT // 2) as i:
                for s in range(2):
                    turn_x(2 * i + s, s, P)
            turn_x(NT, 0, NS)
            pe.wait_ge(tmp_done, TMP_CREDIT + 2 * NT + 2)
            pe.wait_ge(hT_lo_done, TMP_CREDIT + 2 * NT + 2)
            pe.wait_ge(ones_done, 1)
            for c in range(NCH):
                pe.sem_inc(pj_free[c], 1)
            pe.sem_inc(sam_free, 1)

            def product(out, s, cols, m=P):
                for k in range(KT):
                    pe.matmul(out, w_hi[s][:, k, 0:m], hT_hi[:, k, cols], start=(k == 0), stop=False)
                    pe.matmul(out, w_hi[s][:, k, 0:m], hT_lo[:, k, cols], start=False, stop=False)
                    mm = pe.matmul(out, w_lo[s][:, k, 0:m], hT_hi[:, k, cols], start=False, stop=(k == KT - 1))
                return mm

            def post(j, kind, c):
                y = KINDS.index(kind)
                if kind in ("q", "k"):
                    r = 4 * (2 * j + y) + c
                    pe.wait_ge(sq_done, r + 1)
                    pe.wait_ge(ssq_read, r + 1)
                    for b in range(4):
                        mm = pe.matmul(p_ssq[:, 4 * (c % 2) + b:4 * (c % 2) + b + 1], sq[:, c % 2, b * P:(b + 1) * P],
                                       ones[:, 0:1], start=True, stop=True)
                if kind in TURNED:
                    if kind in ("k", "v"):
                        pe.wait_ge(sil_done, SIL_CREDIT + 4 * (3 * j + y) + c + 1)
                    elif kind == "wk":
                        pe.wait_ge(w_f32_done, 4 * j + c + 1)
                    else:
                        pe.wait_ge(pj_free[c], NK * j + y + 2)
                    pe.wait_ge(tok_done, turned_before(j, kind, c) + 1)
                    for b in range(4):
                        mm = pe.transpose(tp[c % 2][:, b * P:(b + 1) * P], sil[:, c, b * P:(b + 1) * P], ident[:])
                mm.then_inc(post_done, 1)

            with pe.Fori(0, NJ) as j:
                for y, kind in enumerate(KINDS):
                    t = NK * j + y
                    pe.wait_ge(w_lo_done, W_CREDIT + t + 1)
                    for c in range(NCH):
                        pe.wait_ge(pj_free[c], t + 1)
                        product(pj[c][:, :], y % 2, slice(CHUNK * c, CHUNK * (c + 1))).then_inc(pj_done, 1)
                        if c == NCH - 1:
                            pe.wait_ge(sam_free, t + 1)
                            product(p_sam[:, 0:NS], y % 2, slice(SEQ, TOK)).then_inc(sam_mm, 1)
                        back, bc = lagged(y, c)
                        if back in POSTED:
                            post(j, back, bc)
            pe.wait_ge(w_lo_done, W_CREDIT + NTILES + 2)
            for c in range(NCH):
                pe.wait_ge(pj_free[c], NTILES + 1)
                product(pj[c][0:2 * DN_HEADS, :], 0, slice(CHUNK * c, CHUNK * (c + 1)), 2 * DN_HEADS).then_inc(pj_done, 1)
            pe.wait_ge(sam_free, NTILES + 1)
            product(p_sam[0:2 * DN_HEADS, 0:NS], 0, slice(SEQ, TOK), 2 * DN_HEADS).then_inc(sam_mm, 1)
            pe.wait_ge(ab_evac, NCH + 1)
            pe.wait_ge(tok_done, TOK_CREDIT + 16 * NJ)
            for n in range(NT):
                pe.transpose(tp[0][:, 8 * n:8 * n + 8], abT[:, n * P:(n + 1) * P], ident[0:8, 0:8])
            pe.transpose(tp[0][0:NS, 8 * NT:8 * NT + 8], ab_sam[:], ident[0:8, 0:8]).then_inc(ab_turned, 1)

        @block.scalar
        def _(act):
            act.sem_inc(sam_mm, W_CREDIT)

            def norm_a(n, s, i, rows):
                act.wait_ge(x_loaded[s], 16 * i + 16)
                act.activation(junk[0:rows, :], xr[0:rows, s, :], ACT.Square, accum_out=stat[0:rows, s, 0:1]).then_inc(sq_summed, 1)
                act.wait_ge(ms_done, n + 1)
                act.activation(stat[0:rows, s, 2:3], stat[0:rows, s, 1:2], ACT.Sqrt).then_inc(root_done, 1)

            def norm_b(n, rows, cols):
                for b in range(2):
                    act.wait_ge(tmp_done, TMP_CREDIT + 2 * n + b + 1)
                    t = tmp[:, b, 0:4 * rows].rearrange("p (k t) -> p k t", k=4)
                    act.activation(hT_hi[:, 4 * b:4 * b + 4, cols], t, ACT.Copy).then_inc(hT_hi_done, 1)

            norm_a(0, 0, 0, P)
            with act.Fori(0, NT // 2 - 1) as i:
                for s in range(2):
                    norm_a(2 * i + s + 1, (s + 1) % 2, i + s, P)
                    norm_b(2 * i + s, P, bass.ds(P * (2 * i + s), P))
            norm_a(NT - 1, 1, NT // 2 - 1, P)
            norm_b(NT - 2, P, slice(SEQ - 2 * P, SEQ - P))
            norm_a(NT, 0, NT // 2, NS)
            norm_b(NT - 1, P, slice(SEQ - P, SEQ))
            norm_b(NT, NS, slice(SEQ, TOK))

            def split(t, s, nth):
                act.wait_ge(w_loaded[s], 16 * nth + 16)
                act.wait_ge(sam_mm, t + 1)
                act.activation(w_hi[s][:], w_raw[:, s], ACT.Copy).then_inc(w_hi_done, 1)

            split(0, 0, 0)
            with act.Fori(0, NJ) as j:
                for y, kind in enumerate(KINDS):
                    t = NK * j + y
                    split(t + 1, (y + 1) % 2, NK // 2 * j + (y + 1) // 2)
                    for c in range(NCH):
                        act.wait_ge(pj_done, 4 * t + c + 1)
                        if kind in ("q", "k", "v"):
                            u = 4 * (3 * j + y) + c
                            act.wait_ge(conv_done, 4 * (3 * j + y) + min(c + 1, NCH - 1) + 1)
                            act.activation(raw[:, TAIL + CHUNK * c:TAIL + CHUNK * (c + 1)], pj[c][:], ACT.Copy).then_inc(pj_free[c], 1)
                            act.wait_ge(conv_done, CONV_CREDIT + u + 1)
                            act.wait_ge(post_done, posts_before(j, kind, c) + 1)
                            if kind != "q":
                                act.wait_ge(sil_stored[c], 16 * (2 * j + y))
                            act.activation(sil[:, c, :], acc[:, c % 2, :], ACT.Silu).then_inc(sil_done, 1)
                            if kind != "v":
                                act.wait_ge(sil_done, SIL_CREDIT + u + 1)
                                act.wait_ge(post_done, posts_before(j, kind, c) + 3)
                                act.activation(sq[:, c % 2, :], sil[:, c, :], ACT.Square).then_inc(sq_done, 1)
                        elif kind in ("za", "zb"):
                            act.wait_ge(z_stored[c % 2], 16 * (2 * (2 * j + (kind == "zb")) + c // 2) + 16)
                            act.activation(zr[:, c % 2, :], pj[c][:], ACT.Silu).then_inc(pj_free[c], 1)
                        elif kind == "wv":
                            act.wait_ge(post_done, posts_before(j, kind, c) + 1)
                            act.activation(sil[:, c, :], pj[c][:], ACT.Copy).then_inc(pj_free[c], 1)
                        else:
                            act.wait_ge(hi_stored[c % 2], 16 * (2 * (2 * j + (kind == "wk")) + c // 2) + 16)
                            act.wait_ge(pj_free[(c + 2) % NCH], t + 1 + (c >= 2))
                            if kind == "wk":
                                act.wait_ge(post_done, posts_before(j, kind, c) + 1)
                                act.activation(sil[:, c, :], pj[c][:], ACT.Copy).then_inc(w_f32_done, 1)
                            act.activation(hi[:, c % 2, :], pj[c][:], ACT.Copy).then_inc(hi_done, 1)
                    act.wait_ge(sam_mm, W_CREDIT + t + 1)
                    act.activation(sam[:, y, bass.ds(j, 1), :].rearrange("p a t -> p (a t)"), p_sam[:, 0:NS],
                                   ACT.Silu if kind in ("za", "zb") else ACT.Copy).then_inc(sam_free, 1)
            split(NTILES, 0, NTILES // 2 + 1)
            for c in range(NCH):
                act.wait_ge(pj_done, 4 * NTILES + c + 1)
                act.activation(abT[:, CHUNK * c:CHUNK * (c + 1)], pj[c][0:8, :], ACT.Copy).then_inc(ab_evac, 1)
            act.wait_ge(sam_mm, W_CREDIT + NTILES + 1)
            act.activation(ab_sam[:], p_sam[0:8, 0:NS], ACT.Copy).then_inc(ab_evac, 1)

        @block.vector
        def _(dve):
            dve.sem_inc(tmp_done, TMP_CREDIT)
            dve.sem_inc(w_lo_done, W_CREDIT)
            dve.sem_inc(conv_done, CONV_CREDIT)
            dve.sem_inc(sil_done, SIL_CREDIT)
            dve.sem_inc(post_done, POST_CREDIT)
            dve.sem_inc(tok_done, TOK_CREDIT)
            dve.sem_inc(ssq_read, SSQ_CREDIT)

            def norm_a(n, s, rows):
                dve.wait_ge(sq_summed, n + 1)
                dve.tensor_scalar(stat[0:rows, s, 1:2], stat[0:rows, s, 0:1], 1.0 / D_MODEL, EPS, ALU.mult, ALU.add).then_inc(ms_done, 1)
                dve.wait_ge(root_done, n + 1)
                dve.reciprocal(stat[0:rows, s, 3:4], stat[0:rows, s, 2:3]).then_inc(inv_done, 1)
                dve.wait_ge(inv_done, n + 1)
                dve.tensor_scalar(xr[0:rows, s, :], xr[0:rows, s, :], stat[0:rows, s, 3:4], None, ALU.mult).then_inc(xn_done, 1)

            def norm_b(n, rows):
                for b in range(2):
                    dve.wait_ge(xT_done, X_CREDIT + 2 * n + b + 1)
                    dve.wait_ge(hT_lo_done, 2 * n + b + 1)
                    view = lambda a: a.rearrange("p (k t) -> p k t", k=4)
                    dve.tensor_tensor(view(tmp[:, b, 0:4 * rows]), view(pj[b][:, 0:4 * rows]),
                                      g_in[:, 4 * b:4 * b + 4].unsqueeze(2).to_broadcast([P, 4, rows]), ALU.mult).then_inc(tmp_done, 1)

            dve.wait_ge(consts_in, 16 * (1 + CONV_W))
            norm_a(0, 0, P)
            with dve.Fori(0, NT // 2 - 1) as i:
                for s in range(2):
                    norm_a(2 * i + s + 1, (s + 1) % 2, P)
                    norm_b(2 * i + s, P)
            norm_a(NT - 1, 1, P)
            norm_b(NT - 2, P)
            norm_a(NT, 0, NS)
            norm_b(NT - 1, P)
            norm_b(NT, NS)

            def split(t, s):
                dve.wait_ge(w_hi_done, t + 1)
                dve.tensor_tensor(w_lo[s][:], w_raw[:, s], w_hi[s][:].bitcast(F32), ALU.subtract).then_inc(w_lo_done, 1)

            def conv(j, y, c):
                u = 4 * (3 * j + y) + c
                dve.wait_ge(sil_done, u + 1)
                w = lambda r: conv_wt[:, bass.ds(NJ * y + j, 1), r]
                x = lambda r: raw[:, CHUNK * c + r:CHUNK * c + r + CHUNK]
                a = acc[:, c % 2, :]
                dve.tensor_scalar(a, x(0), w(0), None, ALU.mult).then_inc(chain, 1)
                for r in range(1, CONV_W):
                    dve.wait_ge(chain, (CONV_W - 1) * u + r)
                    dve.scalar_tensor_tensor(out=a, in0=x(r), scalar=w(r), in1=a, op0=ALU.mult, op1=ALU.add).then_inc(
                        chain if r < CONV_W - 1 else conv_done, 1)

            split(0, 0)
            dve.wait_ge(raw_head, 1)
            with dve.Fori(0, NJ) as j:
                for y, kind in enumerate(KINDS):
                    t = NK * j + y
                    split(t + 1, (y + 1) % 2)
                    for c in range(NCH):
                        if kind in ("q", "k", "v"):
                            dve.wait_ge(pj_free[c], t + 2)
                            if c == NCH - 1:
                                dve.tensor_copy(conv_tail[:, bass.ds(NJ * y + j, 1), :].rearrange("p a r -> p (a r)"), raw[:, SEQ:SEQ + TAIL]).then_inc(tail_done, 1)
                            conv(j, y, c)
                        if kind in ("wq", "wk"):
                            q = int(kind == "wk")
                            dve.wait_ge(hi_done, 4 * (2 * j + q) + c + 1)
                            dve.wait_ge(lo_stored[c % 2], 16 * (2 * (2 * j + q) + c // 2) + 16)
                            dve.tensor_tensor(lo[:, c % 2, :], pj[c][:], hi[:, c % 2, :].bitcast(F32), ALU.subtract).then_inc(pj_free[c], 1)
                        back, bc = lagged(y, c)
                        if back in POSTED:
                            dve.wait_ge(post_done, POST_CREDIT + posts_before(j, back, bc) + 1)
                        if back in ("q", "k"):
                            dve.tensor_copy(ssq[:, 4 * bc:4 * bc + 4, KINDS.index(back), bass.ds(j, 1)].rearrange("p b a -> p (b a)"),
                                            p_ssq[:, 4 * (bc % 2):4 * (bc % 2) + 4]).then_inc(ssq_read, 1)
                        if back in TURNED:
                            dve.wait_ge(tok_stored[bc % 2], 16 * (2 * (4 * j + TURNED.index(back)) + bc // 2) + 16)
                            dve.tensor_copy(tok[:, bc % 2, :], tp[bc % 2][:]).then_inc(tok_done, 1)
            split(NTILES + 1, 0)
            dve.wait_ge(ab_turned, 1)
            dve.tensor_copy(flat(ab_tok[:, 0:NT, :]), tp[0][:, 0:8 * NT])
            dve.tensor_copy(ab_tok[0:NS, NT, :], tp[0][0:NS, 8 * NT:8 * NT + 8])


LN2, LN3 = 0.6931471805599453, 1.0986122886681098
NEG = -1e30
SCALE = HD ** -0.5
LEVELS = (2, 4, 8, 16, 32, 64)
GROUP = 4


def groups(qb):
    return -(-(qb + 1) // GROUP)


GROUPS_BEFORE = [sum(groups(b) for b in range(qb)) for qb in range(NT + 1)]
NG = GROUPS_BEFORE[NT]


def window_table(pool, dve, part, out, dist, a, b, iota_done, step, pattern, base, mult, step0, low_rows=None):
    if part == "pool":
        pool.iota(dist, pattern=pattern, base=base, channel_multiplier=mult).then_inc(iota_done, 1)
        return
    n = [step0]

    def then(ins):
        n[0] += 1
        ins.then_inc(step, 1)
        dve.wait_ge(step, n[0])

    ai = a.bitcast(I32)
    then(dve.tensor_scalar(ai, dist, 15, None, ALU.bitwise_and))
    then(dve.tensor_scalar(out, ai, 0, None, ALU.is_equal))
    then(dve.tensor_scalar(ai, dist, 3, None, ALU.bitwise_and))
    then(dve.tensor_scalar(a, ai, 0, None, ALU.is_equal))
    then(dve.tensor_scalar(b, dist, 512, None, ALU.is_le))
    then(dve.tensor_tensor(a, a, b, ALU.mult))
    then(dve.tensor_tensor(out, out, a, ALU.add))
    then(dve.tensor_scalar(b, dist, 128, None, ALU.is_le))
    then(dve.tensor_tensor(out, out, b, ALU.add))
    then(dve.tensor_scalar(b, dist, 0, None, ALU.is_ge))
    then(dve.tensor_tensor(out, out, b, ALU.mult))
    then(dve.tensor_scalar(a, out, 2, LN2 / SCALE, ALU.is_ge, ALU.mult))
    then(dve.tensor_scalar(b, out, 3, (LN3 - LN2) / SCALE, ALU.is_ge, ALU.mult))
    then(dve.tensor_tensor(a, a, b, ALU.add))
    then(dve.tensor_scalar(b, out, 1, NEG, ALU.is_lt, ALU.mult))
    then(dve.tensor_tensor(out, a, b, ALU.add))
    return n[0]


def gates(nc, env, D):
    with ExitStack() as ctx:
        sem = env.sem
        sb = lambda n, s, d=F32: ctx.enter_context(nc.sbuf_tensor(n, s, d))
        ps = [ctx.enter_context(nc.psum_tensor(f"gate_ps{i}", [P, CHUNK], F32)) for i in range(8)]
        dist = sb("dist", [P, SEQ], I32)
        wa, wb = sb("wa", [P, SEQ]), sb("wb", [P, SEQ])
        lg, dtb = sb("lg", [P, DN_HEADS]), sb("dtb", [P, DN_HEADS])
        H = DN_HEADS
        x, y, z = (sb(n, [P, NT + 1, H]) for n in ("gx", "gy", "gz"))
        g, beta = sb("gg", [P, NT + 1, H]), sb("gbeta", [P, NT + 1, H])
        gb = sb("gb", [NS, H, DEC_BATCH])
        half = sb("half", [P, NT * H])
        norms, loaded, dv, ac, pe_s, iota_done, built, wt, st = (sem(n) for n in ("norms_done", "gates_in", "gate_dve", "gate_act", "gate_pe", "iota_done", "tables", "wt", "st"))
        block = ctx.enter_context(nc.Block())
        E = env

        @block.sync
        def _(sp):
            sp.dma_start(lg[:], D.a_log.unsqueeze(0).to_broadcast([P, H])).then_inc(loaded, 16)
            sp.dma_start(dtb[:], D.dt_bias.unsqueeze(0).to_broadcast([P, H])).then_inc(loaded, 16)
            with nc.allow_non_contiguous_dma(reason="one column"):
                sp.dma_start(E.g_dn[:], D.dn_norm_g.unsqueeze(1)).then_inc(loaded, 16)

        @block.gpsimd
        def _(pool):
            window_table(pool, None, "pool", None, dist[:], None, None, iota_done, None, [[-1, SEQ]], SEQ - P, 1, 0)
            n = 0

            def then(ins):
                nonlocal n
                n += 1
                ins.then_inc(built, 1)
                pool.wait_ge(built, n)

            def select(v, op, fill, base, pattern, mult):
                then(pool.affine_select(out=v, in_=v, compare_op=op, fill=fill, base=base, pattern=pattern, channel_multiplier=mult))

            then(pool.memset(E.upto[:], 1.0))
            select(E.upto[:], ALU.is_ge, 0.0, 0, [[1, P]], -1)
            then(pool.memset(E.after[:], 1.0))
            select(E.after[:], ALU.is_gt, 0.0, 0, [[-1, P]], 1)
            then(pool.memset(E.pair[:], 0.0))
            odd = E.pair[:].rearrange("p (m u) -> p m u", u=2)[:, :, 1]
            select(odd, ALU.not_equal, -1.0, 0, [[-2, P // 2]], 1)
            then(pool.memset(E.below[:], 1.0))
            for l, s in enumerate(LEVELS):
                v = E.below[:, l, :].rearrange("p (m u) -> p m u", u=s)
                m = P // (2 * s)
                select(v, ALU.is_ge, 0.0, -s, [[-2 * s, m], [0, s]], 1)
                select(v, ALU.is_ge, 0.0, 2 * s - 1, [[2 * s, m], [0, s]], -1)
            T = DEC_SEQ
            for t, u in ((E.s_upto, E.upto), (E.s_after, E.after)):
                then(pool.tensor_copy(t[:], u[0:NS, 0:NS]))
                v = t[:].rearrange("p (b t) -> p b t", t=T)
                select(v, ALU.is_ge, 0.0, 0, [[-T, DEC_BATCH], [0, T]], 1)
                select(v, ALU.is_ge, 0.0, T - 1, [[T, DEC_BATCH], [0, T]], -1)
            then(pool.memset(E.s_own[:], 1.0))
            select(E.s_own[:], ALU.is_ge, 0.0, 0, [[-T, DEC_BATCH]], 1)
            select(E.s_own[:], ALU.is_ge, 0.0, T - 1, [[T, DEC_BATCH]], -1)
            pool.memset(half[:], -0.5).then_inc(built, 1)
            n += 1
            env.n_built = n
            pool.wait_ge(norms, 1)
            hv = half[:].rearrange("p (n h) -> p n h", h=H)
            pool.tensor_tensor(E.rinv[:], E.ssq[:, :, 1, :], hv, ALU.pow).then_inc(st, 1)
            pool.tensor_tensor(E.rq[:], E.ssq[:, :, 0, :], hv, ALU.pow).then_inc(st, 1)

        @block.vector
        def _(dve):
            n = 0

            def then(ins):
                nonlocal n
                n += 1
                ins.then_inc(dv, 1)
                dve.wait_ge(dv, n)
                return n

            bc = lambda a: a.unsqueeze(1).to_broadcast([P, NT, H])
            dve.wait_ge(loaded, 48)
            then(dve.memset(x[:], 0.0))
            then(dve.memset(y[:], 0.0))
            then(dve.tensor_tensor(x[:, 0:NT], E.ab_tok[:, 0:NT, 0:H], bc(dtb[:]), ALU.add))
            then(dve.tensor_tensor(x[0:NS, NT], E.ab_tok[0:NS, NT, 0:H], dtb[0:NS], ALU.add))
            then(dve.tensor_scalar(y[:, 0:NT], E.ab_tok[:, 0:NT, H:2 * H], -1.0, None, ALU.mult))
            then(dve.tensor_scalar(y[0:NS, NT], E.ab_tok[0:NS, NT, H:2 * H], -1.0, None, ALU.mult))
            then(dve.tensor_scalar(z[:], x[:], -1.0, None, ALU.mult))
            then(dve.tensor_tensor(z[:], z[:], x[:], ALU.min))
            env.n1 = n
            dve.wait_ge(ac, 3)
            then(dve.tensor_scalar(z[:], z[:], 1.0, None, ALU.add))
            env.n2 = n
            then(dve.tensor_scalar(y[:], y[:], 1.0, None, ALU.add))
            then(dve.reciprocal(beta[:], y[:]))
            then(dve.tensor_scalar(x[:], x[:], 0.0, None, ALU.max))
            dve.wait_ge(ac, 4)
            then(dve.tensor_tensor(x[:], x[:], z[:], ALU.add))
            then(dve.tensor_scalar(lg[:], lg[:], -1.0, None, ALU.mult))
            then(dve.tensor_tensor(g[:], x[:], lg[:].unsqueeze(1).to_broadcast([P, NT + 1, H]), ALU.mult))
            then(dve.tensor_copy(E.g_tok[:], g[:, 0:NT]))
            then(dve.tensor_copy(E.sg_tok[:], g[0:NS, NT]))
            dve.wait_ge(built, env.n_built)
            then(dve.tensor_tensor(gb[:], g[0:NS, NT].unsqueeze(2).to_broadcast([NS, H, DEC_BATCH]), E.s_own[:].unsqueeze(1).to_broadcast([NS, H, DEC_BATCH]), ALU.mult))
            env.n3 = n
            then(dve.tensor_scalar(E.ssq[:], E.ssq[:], EPS, None, ALU.add))
            then(dve.reciprocal(E.d2[:], E.ssq[:, :, 1, :]))
            then(dve.tensor_tensor(E.d2[:], E.d2[:], beta[:, 0:NT], ALU.mult))
            then(dve.tensor_copy(E.s_beta[:], beta[0:NS, NT]))
            dve.sem_inc(norms, 1)
            dve.wait_ge(iota_done, 1)
            window_table(None, dve, "dve", E.win[:], dist[:], wa[:], wb[:], None, wt, None, None, None, 0)
            dve.wait_ge(ac, 8)
            dve.tensor_scalar(E.negc[:], E.egc[:], -1.0, None, ALU.mult)
            dve.wait_ge(st, 2)
            then(dve.tensor_tensor(E.rinv[:], E.ssq[:, :, 1, :], E.rinv[:], ALU.mult))
            then(dve.tensor_scalar(E.rq[:], E.rq[:], DK ** -0.5, None, ALU.mult))
            then(dve.tensor_tensor(E.rq2[:], E.rq[:], E.rq[:], ALU.mult))
            then(dve.tensor_scalar(E.rq2[:], E.rq2[:], 1.0 / DK, None, ALU.mult))

        @block.tensor
        def _(pe):
            pe.wait_ge(dv, env.n3)
            gt = E.g_tok[:].rearrange("p n h -> p (n h)")
            N = NT * H
            pe.matmul(ps[0][:, 0:N], E.upto[:], gt, start=True, stop=True)
            pe.matmul(ps[1][:, 0:N], E.ones[:], gt, start=True, stop=True)
            pe.matmul(ps[2][:, 0:N], E.after[:], gt, start=True, stop=True)
            pe.matmul(ps[3][0:NS, 0:H], E.s_upto[:], E.sg_tok[:], start=True, stop=True)
            pe.matmul(ps[4][0:NS, 0:H], E.s_after[:], E.sg_tok[:], start=True, stop=True)
            pe.matmul(ps[5][:, 0:H * DEC_BATCH], E.ones[0:NS, :], gb[:].rearrange("p h b -> p (h b)"), start=True, stop=True).then_inc(pe_s, 1)

        @block.scalar
        def _(act):
            act.wait_ge(dv, env.n1)
            act.activation(z[:], z[:], ACT.Exp).then_inc(ac, 1)
            act.activation(y[:], y[:], ACT.Exp).then_inc(ac, 1)
            act.activation(lg[:], lg[:], ACT.Exp).then_inc(ac, 1)
            act.wait_ge(dv, env.n2)
            act.activation(z[:], z[:], ACT.Ln).then_inc(ac, 1)
            act.wait_ge(pe_s, 1)
            N = NT * H
            fl = lambda a: a[:].rearrange("p n h -> p (n h)")
            act.activation(fl(E.egc), ps[0][:, 0:N], ACT.Exp).then_inc(ac, 1)
            act.activation(fl(E.gl), ps[1][:, 0:N], ACT.Exp).then_inc(ac, 1)
            act.activation(fl(E.dl), ps[2][:, 0:N], ACT.Exp).then_inc(ac, 1)
            act.activation(E.s_egc[:], ps[3][0:NS, 0:H], ACT.Exp).then_inc(ac, 1)
            act.activation(E.s_dl[:], ps[4][0:NS, 0:H], ACT.Exp).then_inc(ac, 1)
            act.activation(E.s_gl[:].rearrange("p h b -> p (h b)"), ps[5][:, 0:H * DEC_BATCH], ACT.Exp).then_inc(ac, 1)


def gate_tensors(nc, env, ctx):
    sb = lambda n, s, d=F32: ctx.enter_context(nc.sbuf_tensor(n, s, d))
    H = DN_HEADS
    env.g_dn = sb("g_dn", [P, 1])
    env.upto, env.after, env.pair = (sb(n, [P, P]) for n in ("upto", "after", "pair"))
    env.below = sb("below", [P, len(LEVELS), P // 2])
    env.s_upto, env.s_after = sb("s_upto", [NS, NS]), sb("s_after", [NS, NS])
    env.s_own = sb("s_own", [NS, DEC_BATCH])
    env.g_tok, env.d2, env.rinv, env.rq, env.rq2, env.egc, env.negc, env.dl, env.gl = (
        sb(n, [P, NT, H]) for n in ("g_tok", "d2", "rinv", "rq", "rq2", "egc", "negc", "dl", "gl"))
    env.sg_tok, env.s_beta, env.s_egc, env.s_dl = (sb(n, [NS, H]) for n in ("sg_tok", "s_beta", "s_egc", "s_dl"))
    env.s_gl = sb("s_gl", [P, H, DEC_BATCH])
    env.win = sb("win", [P, SEQ])
    env.mix_s = sb("mix_s", [P, D_MODEL // P, NS])


def head_order():
    delta = [("delta", s, e) for e in range(2) for s in DELTA_STEPS]
    weights = [qb + 6 for qb in range(NT)]
    order, done, given = [("scores", 0)], 0, 0
    for qb in range(NT):
        done += weights[qb]
        upto = -(-len(delta) * done // sum(weights))
        mine, given = delta[given:upto], upto
        n = groups(qb)
        if qb + 1 < NT:
            order.append(("scores", qb + 1))
        order.append(("turn", qb, 0))
        if qb >= 2:
            order.append(("gate", qb - 2))
        order += mine[0:1]
        if n > 1:
            order.append(("turn", qb, 1))
        order += mine[1:2]
        for g in range(n):
            if g == n - 1:
                order += mine[2:]
            order.append(("mix", qb, g))
            if g + 2 < n:
                order.append(("turn", qb, g + 2))
        if qb:
            order.append(("out", qb - 1))
    return order + [("gate", NT - 2), ("out", NT - 1), ("gate", NT - 1)]


DELTA_STEPS = (["decay", "kq", "pairs", "pairs_t"] + [x + str(l) for l in range(len(LEVELS)) for x in ("cross", "double")]
               + ["state", "solve", "update", "turn_o"])
BODY = [(e,) + step for e in range(2) for step in head_order()]


def mixers(nc, env, D):
    with ExitStack() as ctx:
        sem = env.sem
        sb = lambda n, s, d=F32: ctx.enter_context(nc.sbuf_tensor(n, s, d))
        ps = lambda n: ctx.enter_context(nc.psum_tensor(n, [P, CHUNK], F32))
        E, H, ident = env, DN_HEADS, env.ident
        qs = [sb(f"qs{e}", [P, SEQ], F32R) for e in range(2)]
        kh = [sb(f"kh{e}", [P, SEQ], F32R) for e in range(2)]
        kl = [sb(f"kl{e}", [P, SEQ], F32R) for e in range(2)]
        vt = [sb(f"vt{e}", [P, NT, HD]) for e in range(2)]
        zb = [sb(f"zb{e}", [HD, SEQ]) for e in range(2)]
        sc = sb("sc", [P, 2, SEQ])
        pt = sb("pt", [P, 4, CHUNK])
        segmax, nmax, lsum, linv = sb("segmax", [P, 2, 4]), sb("nmax", [P, 2]), sb("lsum", [P, 4]), sb("linv", [P, 4])
        ob = sb("ob", [P, 2, HD])
        kq = [sb(f"kq{e}", [P, H, 2, P]) for e in range(2)]
        ktok = [sb(f"ktok{e}", [P, H, P]) for e in range(2)]
        vtok = [sb(f"vtok{e}", [P, H, P]) for e in range(2)]
        za = [sb(f"za{e}", [P, H, P]) for e in range(2)]
        names = "gm dec nt attn tt tl rr y1 vd o1 oo state sg px"
        gm, dec, nt, attn, tt, tl, rr, y1, vd, o1, oo, state, sg, px = (sb("d_" + n, [P, H, P]) for n in names.split())
        cross = sb("cross", [P, len(LEVELS), H, P])
        oss, ors = sb("oss", [P, H]), sb("ors", [P, H])
        half = sb("halves", [P, H])
        s_ps, pt_ps, o_ps, d_ps = ([ps(f"{n}{i}") for i in range(2)] for n in ("s_ps", "pt_ps", "o_ps", "d_ps"))

        S = {n: sem("m_" + n) for n in (
            "scores masked max exped turned turned_out mixed o_scaled o_turned o_gated linv "
            "seen gm_built decay_mm decay_exp decay_masked kq_mm nt_made attn_made px_made tt_made pairs_mm tl_made "
            "cross_mm cross_made double_mm tl_doubled tt_doubled "
            "ks_mm rr_made o1_made solve_mm y1_made vd_made sg_made "
            "av_mm su_mm oo_made state_made oss_made ors_a ors_b oo_scaled oT_mm gated_a v_scaled zeroed").split()}
        head_in = [sem(f"head_in{e}") for e in range(2)]
        head_stored = [sem(f"head_stored{e}") for e in range(2)]
        chunk_in = [sem(f"chunk_in{e}") for e in range(2)]
        chunk_stored = [sem(f"chunk_stored{e}") for e in range(2)]
        delta_stored = sem("delta_stored")
        HEAD_DMAS, CHUNK_DMAS = 8, 5
        O_CREDIT, S_CREDIT, PT_CREDIT = 2, 2, 4
        block = ctx.enter_context(nc.Block())
        L = len(LEVELS)

        @block.sync
        def _(sp):
            for e in range(2):
                sp.sem_inc(head_stored[e], 16)

            def load_head(h, e):
                r = bass.ds(HD * h, HD)
                for half_, part in ((0, 0), (1, 1)):
                    sp.dma_start(qs[e][HD * half_:HD * half_ + HD, :].bitcast(F32), D.wqk[0, part, r, :]).then_inc(head_in[e], 16)
                for half_ in range(2):
                    sp.dma_start(kh[e][HD * half_:HD * half_ + HD, :].bitcast(F32), D.wqk[1, 0, r, :]).then_inc(head_in[e], 16)
                    sp.dma_start(kl[e][HD * half_:HD * half_ + HD, :].bitcast(F32), D.wqk[1, 1, r, :]).then_inc(head_in[e], 16)
                sp.dma_start(vt[e][:], D.new_v[:, r].rearrange("(n p) d -> p n d", p=P)).then_inc(head_in[e], 16)
                sp.dma_start(zb[e][:], D.z_ch[1, r, :]).then_inc(head_in[e], 16)

            def load_chunk(c, e):
                t = bass.ds(P * c, P)
                for half_, y in ((0, 1), (1, 0)):
                    sp.dma_start(kq[e][:, :, half_, :], D.qk_ch[y, :, t].rearrange("(h p) t -> p h t", p=P)).then_inc(chunk_in[e], 16)
                sp.dma_start(flat(ktok[e][:]), D.k_tok[t, :]).then_inc(chunk_in[e], 16)
                sp.dma_start(flat(vtok[e][:]), D.v_tok[t, :]).then_inc(chunk_in[e], 16)
                sp.dma_start(za[e][:], D.z_ch[0, :, t].rearrange("(h p) t -> p h t", p=P)).then_inc(chunk_in[e], 16)

            load_head(0, 0)
            load_chunk(0, 0)
            load_chunk(1, 1)
            load_head(1, 1)
            with sp.Fori(0, SW_HEADS // 2) as i:
                for e in range(2):
                    h = 2 * i + e
                    for u in range(2):
                        c = 2 * h + u
                        sp.wait_ge(S["gated_a"], c + 2)
                        sp.sem_inc(S["seen"], 1)
                        sp.dma_start(D.mix[0:QK_W, bass.ds(P * c, P)].rearrange("(h p) t -> p h t", p=P), za[u][:]).then_inc(chunk_stored[u], 16)
                        sp.wait_ge(chunk_stored[u], 16 * h + 16)
                        load_chunk((c + 2) % NT, u)
                    sp.wait_ge(S["o_gated"], O_CREDIT + NT * (h + 1))
                    sp.sem_inc(S["seen"], 1)
                    sp.dma_start(D.mix[bass.ds(HD * h + QK_W, HD), :], zb[e][:]).then_inc(head_stored[e], 16)
                    sp.wait_ge(head_stored[e], 16 * i + 32)
                    load_head((h + 2) % SW_HEADS, e)
            sp.wait_ge(S["state_made"], NT + 1)
            sp.dma_start(D.new_delta.rearrange("h k v -> k h v"), state[:]).then_inc(delta_stored, 16)
            sp.wait_ge(delta_stored, 16)
            for e in range(2):
                sp.wait_ge(head_in[e], 16 * HEAD_DMAS * (SW_HEADS // 2 + 1))
                sp.wait_ge(chunk_in[e], 16 * CHUNK_DMAS * (NT // 2 + 1))

        def blocks(ap, l, odd):
            return ap.rearrange("p h (m two u) -> p h m two u", two=2, u=LEVELS[l])[:, :, :, odd, :]

        def compact(ap, l):
            return ap.rearrange("p (h m u) -> p h m u", h=H, u=LEVELS[l])

        def row(t, c):
            return t[:, bass.ds(c, 1), :].rearrange("p a h -> p (a h)").unsqueeze(2).to_broadcast([P, H, P])

        def col(t, c, h):
            return t[:, bass.ds(c, 1), h]

        def heads(t):
            return t[:].unsqueeze(1).to_broadcast([P, H, P])

        def by_head(t):
            return t[:].rearrange("p (h t) -> p h t", h=H)

        @block.gpsimd
        def _(pool):
            pool.memset(state[:], 0.0).then_inc(S["state_made"], 1)
            pool.memset(cross[:], 0.0).then_inc(S["zeroed"], 1)
            pool.memset(half[:], -0.5).then_inc(S["zeroed"], 1)
            for n in "gm_built decay_masked px_made tt_made v_scaled sg_made vd_made oo_scaled ors_b".split():
                pool.sem_inc(S[n], 1)
            pool.wait_ge(S["zeroed"], 2)

            def delta(c, u, step):
                if step == "decay":
                    pool.wait_ge(S["decay_mm"], c + 1)
                    pool.tensor_tensor(gm[:], heads(E.upto), row(E.g_tok, c), ALU.mult).then_inc(S["gm_built"], 1)
                    pool.wait_ge(S["decay_exp"], c + 2)
                    pool.tensor_tensor(dec[:], dec[:], heads(E.upto), ALU.mult).then_inc(S["decay_masked"], 1)
                elif step == "kq":
                    pool.wait_ge(chunk_in[u], 8 * CHUNK_DMAS * (c - u) + 16 * CHUNK_DMAS)
                    pool.tensor_tensor(vtok[u][:], vtok[u][:], row(E.rinv, c), ALU.mult).then_inc(S["v_scaled"], 1)
                elif step == "pairs":
                    pool.wait_ge(S["nt_made"], c + 2)
                    pool.tensor_tensor(px[:], nt[:], heads(E.pair), ALU.mult).then_inc(S["px_made"], 1)
                    pool.wait_ge(S["px_made"], c + 2)
                    pool.wait_ge(S["solve_mm"], c + 1)
                    pool.tensor_tensor(tt[:], px[:], heads(ident), ALU.add).then_inc(S["tt_made"], 1)
                elif step == "state":
                    pool.wait_ge(S["state_made"], c + 1)
                    pool.tensor_tensor(sg[:], state[:], row(E.gl, c), ALU.mult).then_inc(S["sg_made"], 1)
                elif step == "solve":
                    pool.wait_ge(S["y1_made"], c + 2)
                    pool.wait_ge(S["su_mm"], c + 1)
                    pool.tensor_tensor(vd[:], y1[:], row(E.dl, c), ALU.mult).then_inc(S["vd_made"], 1)
                elif step == "update":
                    r = lambda t: t[:, bass.ds(c, 1), :].rearrange("p a h -> p (a h)")
                    pool.wait_ge(S["oss_made"], c + 2)
                    pool.tensor_tensor(ors[:], oss[:], r(E.rq2), ALU.mult).then_inc(S["ors_a"], 1)
                    pool.wait_ge(S["ors_a"], 3 * c + 1)
                    pool.sem_inc(S["seen"], 1)
                    pool.tensor_scalar(ors[:], ors[:], EPS, None, ALU.add).then_inc(S["ors_a"], 1)
                    pool.wait_ge(S["ors_a"], 3 * c + 2)
                    pool.tensor_tensor(ors[:], ors[:], half[:], ALU.pow).then_inc(S["ors_a"], 1)
                    pool.wait_ge(S["ors_a"], 3 * c + 3)
                    pool.tensor_tensor(ors[:], ors[:], r(E.rq), ALU.mult).then_inc(S["ors_b"], 1)
                    pool.wait_ge(S["ors_b"], c + 2)
                    pool.tensor_tensor(oo[:], oo[:], ors[:].unsqueeze(2).to_broadcast([P, H, P]), ALU.mult).then_inc(S["oo_scaled"], 1)

            with pool.Fori(0, SW_HEADS // 2) as i:
                for e, step, *a in BODY:
                    if step == "delta":
                        name, u = a
                        delta(4 * i + 2 * e + u, u, name)

        @block.tensor
        def _(pe):
            pe.sem_inc(S["turned"], NG)
            pe.sem_inc(S["o_turned"], O_CREDIT)
            pe.sem_inc(S["mixed"], PT_CREDIT)
            for n in "decay_mm solve_mm su_mm av_mm oT_mm pairs_mm".split():
                pe.sem_inc(S[n], 1)

            def delta(c, u, step):
                if step == "decay":
                    pe.wait_ge(S["gm_built"], c + 2)
                    pe.wait_ge(S["gated_a"], c + 1)
                    pe.matmul(d_ps[0][:], E.after[:], flat(gm[:]), start=True, stop=True).then_inc(S["decay_mm"], 1)
                elif step == "kq":
                    pe.wait_ge(chunk_in[u], 8 * CHUNK_DMAS * (c - u) + 16 * CHUNK_DMAS)
                    for b in range(2):
                        if b == 0:
                            pe.wait_ge(S["state_made"], c + 1)
                        else:
                            pe.wait_ge(S["decay_exp"], c + 2)
                        for h in (2 * b, 2 * b + 1):
                            mm = pe.matmul(d_ps[1 - b][:, 256 * (h % 2):256 * (h % 2) + 256], kq[u][:, h, 0, :], flat(kq[u][:, h, :, :]), start=True, stop=True)
                        mm.then_inc(S["kq_mm"], 1)
                elif step == "pairs_t":
                    pe.wait_ge(S["tt_made"], c + 2)
                    pe.wait_ge(S["attn_made"], c + 2)
                    for h in range(H):
                        mm = pe.transpose(d_ps[0][:, P * h:P * h + P], tt[:, h, :], ident[:])
                    mm.then_inc(S["pairs_mm"], 1)
                elif step.startswith("cross"):
                    l = int(step[5:])
                    if l == 0:
                        pe.wait_ge(S["tl_made"], c + 2)
                    else:
                        pe.wait_ge(S["tl_doubled"], (L - 1) * c + l)
                    for h in range(H):
                        mm = pe.matmul(d_ps[1][:, 64 * h:64 * h + 64], nt[:, h, :], blocks(tl[:], l, 0)[:, h], start=True, stop=True)
                    mm.then_inc(S["cross_mm"], 1)
                elif step.startswith("double"):
                    l = int(step[6:])
                    pe.wait_ge(S["cross_made"], L * c + l + 1)
                    if l:
                        pe.wait_ge(S["tt_doubled"], L * c + l)
                    for h in range(H):
                        x = cross[:, l, :, :]
                        if l < L - 1:
                            pe.matmul(d_ps[0][:, 64 * h:64 * h + 64], tt[:, h, :], blocks(x, l, 0)[:, h], start=True, stop=True)
                        mm = pe.matmul(d_ps[0][:, 256 + 64 * h:256 + 64 * h + 64], x[:, h, :], blocks(tt[:], l, 1)[:, h], start=True, stop=True)
                    mm.then_inc(S["double_mm"], 1)
                elif step == "state":
                    pe.wait_ge(S["state_made"], c + 1)
                    for h in range(H):
                        mm = pe.matmul(d_ps[1][:, P * h:P * h + P], kq[u][:, h, 0, :], state[:, h, :], start=True, stop=True)
                    mm.then_inc(S["ks_mm"], 1)
                    pe.wait_ge(S["tt_doubled"], L * c + L)
                    for h in range(H):
                        mm = pe.matmul(d_ps[0][:, P * h:P * h + P], kq[u][:, h, 1, :], state[:, h, :], start=True, stop=True)
                    mm.then_inc(S["ks_mm"], 1)
                elif step == "solve":
                    pe.wait_ge(S["rr_made"], c + 2)
                    for h in range(H):
                        mm = pe.matmul(d_ps[1][:, P * h:P * h + P], tt[:, h, :], rr[:, h, :], start=True, stop=True)
                    mm.then_inc(S["solve_mm"], 1)
                elif step == "update":
                    pe.wait_ge(S["y1_made"], c + 2)
                    pe.wait_ge(S["o1_made"], c + 2)
                    for h in range(H):
                        mm = pe.matmul(d_ps[0][:, P * h:P * h + P], attn[:, h, :], y1[:, h, :], start=True, stop=True)
                    mm.then_inc(S["av_mm"], 1)
                    pe.wait_ge(S["vd_made"], c + 2)
                    for h in range(H):
                        mm = pe.matmul(d_ps[1][:, P * h:P * h + P], ktok[u][:, h, :], vd[:, h, :], start=True, stop=True)
                    mm.then_inc(S["su_mm"], 1)
                elif step == "turn_o":
                    pe.wait_ge(S["oo_scaled"], c + 2)
                    for h in range(H):
                        mm = pe.transpose(d_ps[0][:, P * h:P * h + P], oo[:, h, :], ident[:])
                    mm.then_inc(S["oT_mm"], 1)

            with pe.Fori(0, SW_HEADS // 2) as i:
                for e, step, *a in BODY:
                    hh = 2 * i + e
                    if step == "delta":
                        name, u = a
                        delta(4 * i + 2 * e + u, u, name)
                        continue
                    qb = a[0]
                    if step == "scores":
                        if qb == 0:
                            pe.wait_ge(head_in[e], 16 * HEAD_DMAS * (i + 1))
                        for g in range(groups(qb)):
                            n = GROUPS_BEFORE[qb] + g
                            w = P * min(GROUP, qb + 1 - GROUP * g)
                            pe.wait_ge(S["masked"], NG * hh + n + 1)
                            q, ks = qs[e][:, P * qb:P * qb + P], slice(CHUNK * g, CHUNK * g + w)
                            pe.matmul(s_ps[n % 2][:, 0:w], q, kh[e][:, ks], start=True, stop=False)
                            pe.matmul(s_ps[n % 2][:, 0:w], q, kl[e][:, ks], start=False, stop=True).then_inc(S["scores"], 1)
                    elif step == "turn":
                        n = GROUPS_BEFORE[qb] + a[1]
                        pe.wait_ge(S["exped"], NT * hh + qb + 1)
                        pe.wait_ge(S["turned_out"], NG * hh + n + 1)
                        for b in range(GROUP * a[1], min(GROUP * a[1] + GROUP, qb + 1)):
                            mm = pe.transpose(pt_ps[n % 2][:, P * (b % GROUP):P * (b % GROUP) + P], sc[:, qb % 2, P * b:P * b + P], ident[:])
                        mm.then_inc(S["turned"], 1)
                    elif step == "mix":
                        n = GROUPS_BEFORE[qb] + a[1]
                        pe.wait_ge(S["turned_out"], S_CREDIT + NG * hh + n + 1)
                        if a[1] == 0:
                            pe.wait_ge(S["o_gated"], NT * hh + qb + 1)
                        for b in range(GROUP * a[1], min(GROUP * a[1] + GROUP, qb + 1)):
                            mm = pe.matmul(o_ps[qb % 2][:, 0:HD], pt[:, n % 4, P * (b % GROUP):P * (b % GROUP) + P], vt[e][:, b, :], start=(b == 0), stop=(b == qb))
                        mm.then_inc(S["mixed"], 1)
                    elif step == "out":
                        pe.wait_ge(S["o_scaled"], NT * hh + qb + 1)
                        pe.sem_inc(S["seen"], 1)
                        pe.transpose(o_ps[qb % 2][0:HD, P:2 * P], ob[:, qb % 2, :], ident[:]).then_inc(S["o_turned"], 1)

        @block.scalar
        def _(act):
            act.sem_inc(S["turned_out"], S_CREDIT)
            for n in "decay_exp tl_made o1_made oss_made".split():
                act.sem_inc(S[n], 1)

            def delta(c, u, step):
                if step == "decay":
                    act.wait_ge(S["decay_mm"], c + 2)
                    act.wait_ge(S["attn_made"], c + 1)
                    act.activation(flat(dec[:]), d_ps[0][:], ACT.Exp).then_inc(S["decay_exp"], 1)
                elif step == "pairs_t":
                    act.wait_ge(S["pairs_mm"], c + 2)
                    act.activation(flat(tl[:]), d_ps[0][:], ACT.Copy).then_inc(S["tl_made"], 1)
                elif step == "state":
                    act.wait_ge(S["ks_mm"], 2 * c + 2)
                    act.wait_ge(S["ors_b"], c + 1)
                    for h in range(H):
                        ins = act.activation(o1[:, h, :], d_ps[0][:, P * h:P * h + P], ACT.Copy, scale=col(E.egc, c, h))
                    ins.then_inc(S["o1_made"], 1)
                elif step == "update":
                    act.wait_ge(S["oo_made"], c + 2)
                    for h in range(H):
                        ins = act.activation(o1[:, h, :], oo[:, h, :], ACT.Square, accum_out=oss[:, h:h + 1])
                    ins.then_inc(S["oss_made"], 1)

            with act.Fori(0, SW_HEADS // 2) as i:
                for e, step, *a in BODY:
                    hh = 2 * i + e
                    if step == "delta":
                        name, u = a
                        delta(4 * i + 2 * e + u, u, name)
                        continue
                    qb = a[0]
                    if step == "scores":
                        act.wait_ge(S["max"], NT * hh + qb + 1)
                        act.wait_ge(S["linv"], NT * hh + qb + 1)
                        x = sc[:, qb % 2, 0:P * (qb + 1)]
                        act.activation(x, x, ACT.Exp, bias=nmax[:, qb % 2:qb % 2 + 1], accum_out=lsum[:, qb % 4:qb % 4 + 1]).then_inc(S["exped"], 1)
                    elif step == "turn":
                        n = GROUPS_BEFORE[qb] + a[1]
                        w = P * min(GROUP, qb + 1 - GROUP * a[1])
                        act.wait_ge(S["turned"], NG * hh + NG + n + 1)
                        act.wait_ge(S["mixed"], NG * hh + n + 1)
                        act.activation(pt[:, n % 4, 0:w], pt_ps[n % 2][:, 0:w], ACT.Copy).then_inc(S["turned_out"], 1)

        @block.vector
        def _(dve):
            dve.sem_inc(S["masked"], S_CREDIT)
            dve.sem_inc(S["linv"], PT_CREDIT)
            dve.sem_inc(S["o_gated"], O_CREDIT)
            for n in "nt_made attn_made rr_made y1_made oo_made gated_a".split():
                dve.sem_inc(S[n], 1)
            dve.wait_ge(S["zeroed"], 1)

            def delta(c, u, step):
                if step == "kq":
                    dve.wait_ge(S["decay_masked"], c + 2)
                    for b in range(2):
                        dve.wait_ge(S["kq_mm"], 2 * c + b + 1)
                        t = d_ps[1 - b][:].rearrange("p (h x t) -> p h x t", h=2, x=2)
                        for h in (2 * b, 2 * b + 1):
                            ins = dve.scalar_tensor_tensor(out=nt[:, h, :], in0=t[:, h % 2, 0], scalar=col(E.d2, c, h), in1=dec[:, h, :], op0=ALU.mult, op1=ALU.mult)
                        if b == 1:
                            ins.then_inc(S["nt_made"], 1)
                        ins = dve.tensor_tensor(attn[:, 2 * b:2 * b + 2, :], t[:, :, 1], dec[:, 2 * b:2 * b + 2, :], ALU.mult)
                    ins.then_inc(S["attn_made"], 1)
                elif step.startswith("cross"):
                    l = int(step[5:])
                    dve.wait_ge(S["cross_mm"], L * c + l + 1)
                    m = E.below[:, l, :].rearrange("p (m u) -> p m u", u=LEVELS[l])
                    m = m.unsqueeze(1).to_broadcast([P, H, P // (2 * LEVELS[l]), LEVELS[l]])
                    dve.tensor_tensor(blocks(cross[:, l], l, 0), compact(d_ps[1][:, 0:256], l), m, ALU.mult).then_inc(S["cross_made"], 1)
                elif step.startswith("double"):
                    l = int(step[6:])
                    dve.wait_ge(S["double_mm"], L * c + l + 1)
                    if l < L - 1:
                        t = blocks(tl[:], l, 0)
                        dve.tensor_tensor(t, t, compact(d_ps[0][:, 0:256], l), ALU.subtract).then_inc(S["tl_doubled"], 1)
                    t = blocks(tt[:], l, 1)
                    dve.tensor_tensor(t, t, compact(d_ps[0][:, 256:512], l), ALU.subtract).then_inc(S["tt_doubled"], 1)
                elif step == "state":
                    dve.wait_ge(S["v_scaled"], c + 2)
                    dve.wait_ge(S["ks_mm"], 2 * c + 1)
                    for h in range(H):
                        ins = dve.scalar_tensor_tensor(out=rr[:, h, :], in0=d_ps[1][:, P * h:P * h + P], scalar=col(E.negc, c, h), in1=vtok[u][:, h, :], op0=ALU.mult, op1=ALU.add)
                    ins.then_inc(S["rr_made"], 1)
                elif step == "solve":
                    dve.wait_ge(S["solve_mm"], c + 2)
                    dve.wait_ge(S["vd_made"], c + 1)
                    dve.tensor_tensor(y1[:], by_head(d_ps[1]), row(E.d2, c), ALU.mult).then_inc(S["y1_made"], 1)
                elif step == "update":
                    dve.wait_ge(S["av_mm"], c + 2)
                    dve.wait_ge(S["o1_made"], c + 2)
                    dve.tensor_tensor(oo[:], by_head(d_ps[0]), o1[:], ALU.add).then_inc(S["oo_made"], 1)
                    dve.wait_ge(S["su_mm"], c + 2)
                    dve.wait_ge(S["sg_made"], c + 2)
                    dve.tensor_tensor(state[:], by_head(d_ps[1]), sg[:], ALU.add).then_inc(S["state_made"], 1)
                elif step == "turn_o":
                    dve.wait_ge(S["oT_mm"], c + 2)
                    dve.scalar_tensor_tensor(out=za[u][:], in0=by_head(d_ps[0]), scalar=E.g_dn[:, 0:1], in1=za[u][:], op0=ALU.mult, op1=ALU.mult).then_inc(S["gated_a"], 1)

            with dve.Fori(0, SW_HEADS // 2) as i:
                for e, step, *a in BODY:
                    hh = 2 * i + e
                    if step == "delta":
                        name, u = a
                        delta(4 * i + 2 * e + u, u, name)
                        continue
                    qb = a[0]
                    s, l = qb % 2, qb % 4
                    if step == "scores":
                        dve.wait_ge(S["turned"], NG * hh + (NG + GROUPS_BEFORE[qb - 1] if qb else GROUPS_BEFORE[NT - 1]))
                        for g in range(groups(qb)):
                            n = GROUPS_BEFORE[qb] + g
                            w = P * min(GROUP, qb + 1 - GROUP * g)
                            at = P * (NT - 1 - qb) + CHUNK * g
                            dve.wait_ge(S["scores"], NG * hh + n + 1)
                            dve.sem_inc(S["seen"], 1)
                            dve.tensor_tensor_reduce(sc[:, s, CHUNK * g:CHUNK * g + w], s_ps[n % 2][:, 0:w], E.win[:, at:at + w], SCALE, -3.0e38,
                                                     ALU.add, ALU.max, segmax[:, s, g:g + 1]).then_inc(S["masked"], 1)
                        dve.wait_ge(S["masked"], S_CREDIT + NG * hh + GROUPS_BEFORE[qb + 1])
                        dve.tensor_reduce(nmax[:, s:s + 1], segmax[:, s, 0:groups(qb)], AX.X, ALU.max, negate=True).then_inc(S["max"], 1)
                    elif step == "out":
                        dve.wait_ge(S["exped"], NT * hh + qb + 1)
                        dve.reciprocal(linv[:, l:l + 1], lsum[:, l:l + 1]).then_inc(S["linv"], 1)
                        dve.wait_ge(S["linv"], PT_CREDIT + NT * hh + qb + 1)
                        dve.wait_ge(S["mixed"], PT_CREDIT + NG * hh + GROUPS_BEFORE[qb + 1])
                        dve.wait_ge(S["o_turned"], NT * hh + qb + 1)
                        dve.tensor_scalar(ob[:, s, :], o_ps[s][:, 0:HD], linv[:, l:l + 1], None, ALU.mult).then_inc(S["o_scaled"], 1)
                    elif step == "gate":
                        if qb == 0:
                            dve.wait_ge(head_in[e], 16 * HEAD_DMAS * (i + 1))
                        dve.wait_ge(S["o_turned"], O_CREDIT + NT * hh + qb + 1)
                        z = zb[e][:, P * qb:P * qb + P]
                        dve.tensor_tensor(z, o_ps[s][0:HD, P:2 * P], z, ALU.mult).then_inc(S["o_gated"], 1)


H = DN_HEADS
T = DEC_SEQ
ROWS = SW_HEADS * T
NEAR = 512
FAR = (PAST - NEAR) // 16
FARS = T * FAR
KEYS = NEAR + FARS + T


def sample(nc, env, D):
    with ExitStack() as ctx:
        sem = env.sem
        sb = lambda n, s, d=F32: ctx.enter_context(nc.sbuf_tensor(n, s, d))
        bank = [ctx.enter_context(nc.psum_tensor(f"s_bank{i}", [P, CHUNK], F32)) for i in range(8)]
        E, ident, sam = env, env.ident, env.sam
        stc = sb("stc", [DEC_BATCH * TAIL, CONV_CH])
        ext = sb("ext", [P, 3 * NJ, DEC_BATCH, TAIL + T])
        cacc, ctmp = (sb(n, [P, 3 * NJ, DEC_BATCH, T]) for n in ("cacc", "ctmp"))
        raw_tok = sb("raw_tok", [NS, CONV_CH])
        kv_tok = sb("kv_tok", [NS, 2, SW_WIDTH])
        skq, svc = sb("skq", [P, 2, H, NS]), sb("svc", [P, H, NS])
        ssq2 = sb("ssq2", [P, 2, H, NS])
        ssum = sb("ssum", [NS, 2, H])
        sd2, srinv, srq, srq2, soss, sors, shalf = (sb(n, [NS, H]) for n in ("sd2", "srinv", "srq", "srq2", "soss", "sors", "shalf"))
        x2 = sb("x2", [NS, NS])
        sgm, sdec, snt, sattn, stt, stl, sx, sz = (sb(n, [NS, H, NS]) for n in ("sgm", "sdec", "snt", "sattn", "stt", "stl", "sx", "sz"))
        sktok, svtok, srr, sy1, so = (sb(n, [NS, H, P]) for n in ("sktok", "svtok", "srr", "sy1", "so"))
        sts = sb("sts", [P, 2, H, NS])
        svd = sb("svd", [NS, H, P])
        vdb = sb("vdb", [NS, H, DEC_BATCH, P])
        st = sb("st", [P, DEC_BATCH, H, P])
        kn, vn = ([sb(f"{n}{u}", [P, T, SW_WIDTH]) for u in range(2)] for n in ("kn", "vn"))
        kf, vf = ([sb(f"{n}{u}", [FAR, T, SW_WIDTH]) for u in range(2)] for n in ("kf", "vf"))
        vnew = [sb(f"vnew{u}", [T, SW_WIDTH]) for u in range(2)]
        kT = sb("kT", [P, 2, NEAR + FARS])
        DIAG = ROWS + 2 * T
        qw = [sb(f"qw{u}", [P, NJ * DIAG]) for u in range(2)]
        kw = [sb(f"kw{u}", [P, NJ, T]) for u in range(2)]
        tab, dist, ta, tb = sb("s_tab", [ROWS, KEYS]), sb("s_dist", [ROWS, KEYS], I32), sb("s_ta", [ROWS, KEYS]), sb("s_tb", [ROWS, KEYS])
        tix = sb("tix", [ROWS, 1], I32)
        pr = sb("pr", [ROWS, 2, KEYS])
        smax, snmax, slsum, slinv = sb("smax", [ROWS, 2, 2]), sb("snmax", [ROWS, 2]), sb("slsum", [ROWS, 2]), sb("slinv", [ROWS, 2])
        pT = sb("pT", [P, 9 * ROWS])

        G = {n: sem("s_" + n) for n in (
            "inputs stc_turned ext_made conv_done silu_done squared sums norms pows tables "
            "turned_rows rows_copied out_rows turned_kv kv_copied read_states states_copied decay decay_exp gm dec kqm pairs tt tl z_mm z m solved "
            "r_made y1 vd attn_mm o_made o_squared o_eps o_pow o_scaled o_turned delta_gated su su_read st_stored "
            "kT_mm kT_act kT_dve kT_used scored masked max exped lsum normed pT_mm pT_out mixed o_picked q_picked tab_dist tab_step step qw_zero seen".split())}
        cache_in = [sem(f"s_cache{u}") for u in range(2)]
        K_IN = 5
        block = ctx.enter_context(nc.Block())

        @block.sync
        def _(sp):
            sp.dma_start(stc[:], D.state_conv.rearrange("b r c -> (b r) c")).then_inc(G["inputs"], 16)
            sp.dma_start(st[:], D.state_delta.rearrange("b h k v -> k b h v")).then_inc(G["inputs"], 16)

            def load(b, u):
                one = bass.ds(b, 1)
                for cache, near, far in ((D.cache_k, kn[u], kf[u]), (D.cache_v, vn[u], vf[u])):
                    sp.dma_start(near[:], cache[one, PAST - NEAR:PAST, :].rearrange("a (p t) c -> (a p) t c", t=T)).then_inc(cache_in[u], 16)
                    rows = cache[one, 0:PAST - NEAR, :].rearrange("a (m r) c -> (a m) r c", r=16)[:, 0:T, :]
                    sp.dma_start(far[:], rows).then_inc(cache_in[u], 16)
                sp.dma_start(vnew[u][:], D.out_v[one, PAST - T:PAST, :].rearrange("a t c -> (a t) c")).then_inc(cache_in[u], 16)

            sp.wait_ge(G["kv_copied"], 2)
            for b in range(DEC_BATCH):
                for y, out in ((0, D.out_k), (1, D.out_v)):
                    sp.dma_start(out[b, PAST - T:PAST, :], kv_tok[T * b:T * b + T, y, :]).then_inc(G["out_rows"], 16)
            sp.wait_ge(G["out_rows"], 16 * 2 * DEC_BATCH)
            load(0, 0)
            load(1, 1)
            sp.wait_ge(G["rows_copied"], 3)
            for b in range(DEC_BATCH):
                sp.dma_start(D.new_conv_s[b], raw_tok[T * b + 1:T * b + T, :]).then_inc(G["out_rows"], 16)
            with sp.Fori(0, DEC_BATCH // 2 - 1) as i:
                for u in range(2):
                    b = 2 * i + u
                    sp.wait_ge(G["mixed"], b + 1)
                    sp.sem_inc(G["seen"], 1)
                    load(b + 2, u)
            sp.wait_ge(G["su_read"], 2 * H)
            sp.dma_start(D.new_delta_s.rearrange("b h k v -> k b h v"), st[:]).then_inc(G["st_stored"], 16)
            sp.wait_ge(G["st_stored"], 16)
            sp.wait_ge(G["out_rows"], 16 * 3 * DEC_BATCH)

        @block.gpsimd
        def _(pool):
            n = [0]

            def then(ins):
                n[0] += 1
                ins.then_inc(G["tables"], 1)
                pool.wait_ge(G["tables"], n[0])

            pool.iota(dist[:, 0:NEAR], pattern=[[-1, T], [-T, P]], base=NEAR, channel_multiplier=0)
            pool.iota(dist[:, NEAR:NEAR + FARS], pattern=[[-1, T], [-16, FAR]], base=PAST, channel_multiplier=0)
            pool.iota(dist[:, NEAR + FARS:KEYS], pattern=[[-1, T]], base=0, channel_multiplier=0)
            pool.iota(tix[:], pattern=[[0, 1]], base=0, channel_multiplier=1).then_inc(G["tab_dist"], 1)
            then(pool.memset(x2[:], 0.0))
            odd = x2[:].rearrange("p (m two u) -> p m two u", two=2, u=2)[:, :, 1, :]
            then(pool.memset(odd, 1.0))
            then(pool.affine_select(out=odd, in_=odd, compare_op=ALU.is_ge, fill=0.0, base=0, pattern=[[-T, DEC_BATCH], [0, 2]], channel_multiplier=1))
            then(pool.affine_select(out=odd, in_=odd, compare_op=ALU.is_ge, fill=0.0, base=1, pattern=[[T, DEC_BATCH], [0, 2]], channel_multiplier=-1))
            then(pool.memset(shalf[:], -0.5))
            bh = lambda t: t[:].unsqueeze(1).to_broadcast([NS, H, NS])
            pool.tensor_tensor(sgm[:], bh(E.s_upto), E.sg_tok[:].unsqueeze(2).to_broadcast([NS, H, NS]), ALU.mult).then_inc(G["gm"], 1)
            pool.wait_ge(G["norms"], 1)
            pool.tensor_tensor(srinv[:], ssum[:, 0, :], shalf[:], ALU.pow)
            pool.tensor_tensor(srq[:], ssum[:, 1, :], shalf[:], ALU.pow).then_inc(G["pows"], 1)
            pool.wait_ge(G["vd"], 1)
            vd4 = svd[:].unsqueeze(2).to_broadcast([NS, H, DEC_BATCH, P])
            own = E.s_own[:].unsqueeze(1).unsqueeze(3).to_broadcast([NS, H, DEC_BATCH, P])
            pool.tensor_tensor(vdb[:], vd4, own, ALU.mult).then_inc(G["vd"], 1)
            pool.wait_ge(G["o_eps"], 1)
            pool.tensor_tensor(sors[:], sors[:], shalf[:], ALU.pow).then_inc(G["o_pow"], 1)

        @block.tensor
        def _(pe):
            pe.wait_ge(G["inputs"], 32)
            for t in range(3 * NJ):
                mm = pe.transpose(bank[0][:, 24 * t:24 * t + 24], stc[:, P * t:P * t + P], ident[0:24, 0:24])
            mm.then_inc(G["stc_turned"], 1)
            for y, kind in enumerate(("wk", "wv")):
                for j in range(NJ):
                    mm = pe.transpose(bank[4 + y][0:NS, P * j:P * j + P], sam[:, KINDS.index(kind), j, :], ident[:])
                mm.then_inc(G["turned_kv"], 1)
            for y in range(3):
                for j in range(NJ):
                    mm = pe.transpose(bank[1 + y][0:NS, P * j:P * j + P], sam[:, y, j, :], ident[:])
                mm.then_inc(G["turned_rows"], 1)
            pe.wait_ge(G["gm"], 1)
            pe.matmul(bank[6][0:NS, 0:H * NS], E.s_after[:], flat(sgm[:]), start=True, stop=True).then_inc(G["decay"], 1)
            pe.wait_ge(G["squared"], 1)
            for x in range(2):
                for h in range(H):
                    mm = pe.matmul(bank[7][0:NS, H * x + h:H * x + h + 1], ssq2[:, x, h, :], E.ones[:, 0:1], start=True, stop=True)
            mm.then_inc(G["sums"], 1)
            pe.wait_ge(G["decay_exp"], 1)
            for h in range(H):
                for x in range(2):
                    mm = pe.matmul(bank[6][0:NS, (2 * h + x) * NS:(2 * h + x) * NS + NS], skq[:, 0, h, :], skq[:, x, h, :], start=True, stop=True)
            mm.then_inc(G["kqm"], 1)
            pe.wait_ge(G["rows_copied"], 3)
            for x, t in ((0, skq[:, 0]), (1, svc[:])):
                for h in range(H):
                    mm = pe.transpose(bank[1 + x][0:NS, P * h:P * h + P], t[:, h, :], ident[:])
            mm.then_inc(G["turned_rows"], 1)
            pe.wait_ge(G["kv_copied"], 2)
            for b in range(DEC_BATCH):
                for h in range(H):
                    out = bank[4][:, 0:2 * H * NS].rearrange("p (x h t) -> p x h t", x=2, h=H)[:, :, h, T * b:T * b + T]
                    mm = pe.matmul(out, st[:, b, h, :], skq[:, :, h, T * b:T * b + T], start=True, stop=True)
            mm.then_inc(G["read_states"], 1)
            pe.wait_ge(G["tt"], 1)
            for h in range(H):
                mm = pe.transpose(bank[0][0:NS, NS * h:NS * h + NS], stt[:, h, :], ident[0:NS, 0:NS])
            mm.then_inc(G["pairs"], 1)
            pe.wait_ge(G["tl"], 1)
            for h in range(H):
                mm = pe.matmul(bank[5][0:NS, NS * h:NS * h + NS], sx[:, h, :], stl[:, h, :], start=True, stop=True)
            mm.then_inc(G["z_mm"], 1)
            pe.wait_ge(G["z"], 1)
            for h in range(H):
                mm = pe.matmul(bank[0][0:NS, NS * h:NS * h + NS], sz[:, h, :], stt[:, h, :], start=True, stop=True)
            mm.then_inc(G["m"], 1)
            pe.wait_ge(G["states_copied"], 1)
            pe.wait_ge(G["rows_copied"], 4)
            for x in range(2):
                for h in range(H):
                    mm = pe.transpose(bank[(3, 1)[x]][0:NS, P * h:P * h + P], sts[:, x, h, :], ident[:])
            mm.then_inc(G["read_states"], 1)
            pe.wait_ge(G["tt"], 2)
            pe.wait_ge(G["r_made"], 1)
            for h in range(H):
                mm = pe.matmul(bank[3][0:NS, P * h:P * h + P], stt[:, h, :], srr[:, h, :], start=True, stop=True)
            mm.then_inc(G["solved"], 1)
            pe.wait_ge(G["y1"], 1)
            for h in range(H):
                mm = pe.matmul(bank[4][0:NS, P * h:P * h + P], sattn[:, h, :], sy1[:, h, :], start=True, stop=True)
            mm.then_inc(G["attn_mm"], 1)
            pe.wait_ge(G["vd"], 2)
            for h in range(H):
                for x in range(2):
                    n = 2 * h + x
                    if n >= 2:
                        pe.wait_ge(G["su_read"], n - 1)
                    pe.matmul(bank[6 + x][:], sktok[:, h, :], flat(vdb[:, h, 4 * x:4 * x + 4, :]), start=True, stop=True).then_inc(G["su"], 1)
            pe.wait_ge(G["o_scaled"], 1)
            for h in range(H):
                mm = pe.transpose(bank[5][:, NS * h:NS * h + NS], so[:, h, :], ident[0:NS, 0:NS])
            mm.then_inc(G["o_turned"], 1)

            pe.wait_ge(G["delta_gated"], 1)
            pe.wait_ge(G["su_read"], 2 * H)

            def turn(b, i, u, j):
                if j == 0:
                    pe.wait_ge(cache_in[u], 16 * K_IN * (i + 1))
                pe.wait_ge(G["kT_act"], NJ * b + j + 1)
                pe.sem_inc(G["seen"], 1)
                for t in range(T):
                    mm = pe.transpose(bank[j % 2][:, P * t:P * t + P], kn[u][:, t, P * j:P * j + P], ident[:])
                mm.then_inc(G["kT_mm"], 1)
                pe.wait_ge(G["kT_dve"], NJ * b + j + 1)
                pe.sem_inc(G["seen"], 1)
                for t in range(T):
                    mm = pe.transpose(bank[2 + j % 2][:, FAR * t:FAR * t + FAR], kf[u][:, t, P * j:P * j + P], ident[0:FAR, 0:FAR])
                mm.then_inc(G["kT_mm"], 1)

            def score(b, u, j):
                pe.wait_ge(G["kT_act"], 2 + NJ * b + j + 1)
                pe.wait_ge(G["kT_dve"], 2 + NJ * b + j + 1)
                if j == 0:
                    pe.wait_ge(G["masked"], 2 * b + 2)
                pe.sem_inc(G["seen"], 1)
                q = qw[u][:, ROWS * j:ROWS * j + ROWS]
                a = dict(start=(j == 0), stop=(j == NJ - 1))
                pe.matmul(bank[4][0:ROWS, :], q, kT[:, j % 2, 0:NEAR], **a)
                pe.matmul(bank[5][0:ROWS, 0:FARS], q, kT[:, j % 2, NEAR:], **a).then_inc(G["kT_used"], 1)
                if j == NJ - 1:
                    for k in range(NJ):
                        mm = pe.matmul(bank[5][0:ROWS, FARS:FARS + T], qw[u][:, ROWS * k:ROWS * k + ROWS], kw[u][:, k, :], start=(k == 0), stop=(k == NJ - 1))
                    mm.then_inc(G["scored"], 1)

            def scores(b, i, u):
                pe.wait_ge(G["q_picked"], b + 1)
                turn(b, i, u, 0)
                for j in range(NJ):
                    if j + 1 < NJ:
                        turn(b, i, u, j + 1)
                    score(b, u, j)

            def mix(b, u):
                pe.wait_ge(G["normed"], b + 1)
                pe.wait_ge(G["pT_out"], b + 1)
                pe.sem_inc(G["seen"], 1)
                for k in range(9):
                    w, at = (P, P * k) if k < T else (FAR, NEAR + FAR * (k - T)) if k < 2 * T else (T, NEAR + FARS)
                    mm = pe.transpose(bank[6][0:w, ROWS * k:ROWS * k + ROWS], pr[:, u, at:at + w], ident[0:ROWS, 0:ROWS])
                mm.then_inc(G["pT_mm"], 1)
                pe.wait_ge(G["pT_out"], 1 + b + 1)
                pe.wait_ge(G["o_picked"], b + 1)
                pe.sem_inc(G["seen"], 1)
                for j in range(NJ):
                    for k in range(9):
                        v, w = (vn[u][:, k], P) if k < T else (vf[u][:, k - T], FAR) if k < 2 * T else (vnew[u][:], T)
                        p = pT[0:w, ROWS * k + 2 * T * j:ROWS * k + 2 * T * j + 2 * T]
                        mm = pe.matmul(bank[7][:, 2 * T * j:2 * T * j + 2 * T], v[:, P * j:P * j + P], p, start=(k == 0), stop=(k == 8))
                mm.then_inc(G["mixed"], 1)

            for n, credit in (("kT_used", 2),):
                pe.sem_inc(G[n], credit)
            scores(0, 0, 0)
            with pe.Fori(0, DEC_BATCH // 2 - 1) as i:
                for e in range(2):
                    scores(2 * i + 1 + e, i + e, 1 - e)
                    mix(2 * i + e, e)
            scores(DEC_BATCH - 1, DEC_BATCH // 2 - 1, 1)
            mix(DEC_BATCH - 2, 0)
            mix(DEC_BATCH - 1, 1)

        @block.scalar
        def _(act):
            act.sem_inc(G["kT_act"], 2)
            act.sem_inc(G["pT_out"], 1)
            for y in range(2):
                act.wait_ge(G["turned_kv"], y + 1)
                act.activation(kv_tok[:, y, :], bank[4 + y][0:NS, :], ACT.Copy).then_inc(G["kv_copied"], 1)
            for y in range(3):
                act.wait_ge(G["turned_rows"], y + 1)
                act.activation(raw_tok[:, QK_W * y:QK_W * (y + 1)], bank[1 + y][0:NS, :], ACT.Copy).then_inc(G["rows_copied"], 1)
            act.wait_ge(G["decay"], 1)
            act.activation(flat(sdec[:]), bank[6][0:NS, 0:H * NS], ACT.Exp).then_inc(G["decay_exp"], 1)
            act.wait_ge(G["conv_done"], 1)
            c = lambda y: cacc[:, NJ * y:NJ * (y + 1)].rearrange("p a b t -> p a (b t)")
            act.activation(skq[:, 0], c(1), ACT.Silu)
            act.activation(skq[:, 1], c(0), ACT.Silu)
            act.activation(svc[:], c(2), ACT.Silu).then_inc(G["silu_done"], 1)
            act.wait_ge(G["turned_rows"], 4)
            act.activation(flat(sktok[:]), bank[1][0:NS, :], ACT.Copy).then_inc(G["rows_copied"], 1)
            act.activation(flat(svtok[:]), bank[2][0:NS, :], ACT.Copy).then_inc(G["rows_copied"], 1)
            act.wait_ge(G["read_states"], 1)
            act.activation(sts[:].rearrange("p x h t -> p (x h t)"), bank[4][:, 0:2 * H * NS], ACT.Copy).then_inc(G["states_copied"], 1)
            act.wait_ge(G["pairs"], 1)
            act.activation(flat(stl[:]), bank[0][0:NS, 0:H * NS], ACT.Copy).then_inc(G["tl"], 1)
            act.wait_ge(G["z_mm"], 1)
            act.activation(flat(sz[:]), bank[5][0:NS, 0:H * NS], ACT.Copy).then_inc(G["z"], 1)
            act.wait_ge(G["o_made"], 1)
            for h in range(H):
                ins = act.activation(srr[:, h, :], so[:, h, :], ACT.Square, accum_out=soss[:, h:h + 1])
            ins.then_inc(G["o_squared"], 1)

            def turned(b):
                for j in range(NJ):
                    act.wait_ge(G["kT_used"], NJ * b + j + 1)
                    act.wait_ge(G["kT_mm"], 2 * (NJ * b + j) + 1)
                    act.activation(kT[:, j % 2, 0:NEAR], bank[j % 2][:], ACT.Copy).then_inc(G["kT_act"], 1)

            def p_out(b):
                act.wait_ge(G["pT_mm"], b + 1)
                for w, a, z in ((P, 0, T), (FAR, T, 2 * T), (T, 2 * T, 9)):
                    ins = act.activation(pT[0:w, ROWS * a:ROWS * z], bank[6][0:w, ROWS * a:ROWS * z], ACT.Copy)
                ins.then_inc(G["pT_out"], 1)

            def exp(b, u):
                act.wait_ge(G["max"], b + 1)
                x = pr[:, u, :]
                act.activation(x, x, ACT.Exp, bias=snmax[:, u:u + 1], accum_out=slsum[:, u:u + 1]).then_inc(G["exped"], 1)

            turned(0)
            exp(0, 0)
            with act.Fori(0, DEC_BATCH // 2 - 1) as i:
                for e in range(2):
                    turned(2 * i + 1 + e)
                    p_out(2 * i + e)
                    exp(2 * i + 1 + e, 1 - e)
            turned(DEC_BATCH - 1)
            p_out(DEC_BATCH - 2)
            exp(DEC_BATCH - 1, 1)
            p_out(DEC_BATCH - 1)

        @block.vector
        def _(dve):
            dve.sem_inc(G["kT_dve"], 2)
            dve.sem_inc(G["masked"], 2)
            dve.sem_inc(G["o_picked"], 1)
            n = [0]

            def then(ins):
                n[0] += 1
                ins.then_inc(G["step"], 1)
                dve.wait_ge(G["step"], n[0])

            for u in range(2):
                dve.memset(qw[u][:], 0.0).then_inc(G["qw_zero"], 1)
            dve.tensor_copy(ext[:, :, :, TAIL:], sam[:, 0:3].rearrange("p y j (b t) -> p (y j) b t", t=T))
            dve.wait_ge(G["stc_turned"], 1)
            then(dve.tensor_copy(ext[:, :, :, 0:TAIL], bank[0][:, 0:24 * 3 * NJ].rearrange("p (a b r) -> p a b r", b=DEC_BATCH, r=TAIL)))
            w = lambda r: E.conv_wt[:, :, r].unsqueeze(2).unsqueeze(3).to_broadcast([P, 3 * NJ, DEC_BATCH, T])
            then(dve.tensor_tensor(cacc[:], ext[:, :, :, 0:T], w(0), ALU.mult))
            for r in range(1, CONV_W):
                then(dve.tensor_tensor(ctmp[:], ext[:, :, :, r:r + T], w(r), ALU.mult))
                then(dve.tensor_tensor(cacc[:], cacc[:], ctmp[:], ALU.add))
            dve.sem_inc(G["conv_done"], 1)
            dve.wait_ge(G["silu_done"], 1)
            dve.tensor_tensor(ssq2[:], skq[:], skq[:], ALU.mult).then_inc(G["squared"], 1)
            dve.wait_ge(G["sums"], 1)
            then(dve.tensor_scalar(ssum[:].rearrange("p x h -> p (x h)"), bank[7][0:NS, 0:2 * H], EPS, None, ALU.add))
            dve.sem_inc(G["norms"], 1)
            then(dve.reciprocal(sd2[:], ssum[:, 0, :]))
            then(dve.tensor_tensor(sd2[:], sd2[:], E.s_beta[:], ALU.mult))
            s32 = lambda t: t[:].unsqueeze(2).to_broadcast([NS, H, NS])
            s128 = lambda t: t[:].unsqueeze(2).to_broadcast([NS, H, P])
            m32 = lambda t: t.unsqueeze(1).to_broadcast([NS, H, NS])
            tok = lambda t: t[0:NS, :].rearrange("p (h d) -> p h d", h=H)
            dve.wait_ge(G["decay_exp"], 1)
            then(dve.tensor_tensor(sdec[:], sdec[:], m32(E.s_upto[:]), ALU.mult))
            dve.wait_ge(G["kqm"], 1)
            kq = bank[6][0:NS, 0:2 * H * NS].rearrange("p (h x t) -> p h x t", h=H, x=2)
            dve.tensor_tensor(sattn[:], kq[:, :, 1], sdec[:], ALU.mult)
            then(dve.tensor_tensor(snt[:], kq[:, :, 0], sdec[:], ALU.mult))
            then(dve.tensor_tensor(snt[:], snt[:], s32(sd2), ALU.mult))
            dve.wait_ge(G["tables"], 5)
            dve.tensor_tensor(sx[:], snt[:], m32(x2[:]), ALU.mult)
            then(dve.tensor_tensor(stt[:], snt[:], m32(E.pair[0:NS, 0:NS]), ALU.mult))
            dve.tensor_tensor(stt[:], stt[:], m32(ident[0:NS, 0:NS]), ALU.add).then_inc(G["tt"], 1)
            dve.wait_ge(G["pows"], 1)
            then(dve.tensor_tensor(srinv[:], srinv[:], ssum[:, 0, :], ALU.mult))
            then(dve.tensor_scalar(srq[:], srq[:], DK ** -0.5, None, ALU.mult))
            then(dve.tensor_tensor(srq2[:], srq[:], srq[:], ALU.mult))
            then(dve.tensor_scalar(srq2[:], srq2[:], 1.0 / DK, None, ALU.mult))
            dve.wait_ge(G["rows_copied"], 5)
            then(dve.tensor_tensor(svtok[:], svtok[:], s128(srinv), ALU.mult))
            dve.wait_ge(G["m"], 1)
            dve.tensor_tensor(stt[:], stt[:], bank[0][0:NS, 0:H * NS].rearrange("p (h t) -> p h t", h=H), ALU.subtract).then_inc(G["tt"], 1)
            dve.wait_ge(G["read_states"], 2)
            dve.tensor_tensor(so[:], tok(bank[1]), s128(E.s_egc), ALU.mult)
            then(dve.tensor_tensor(srr[:], tok(bank[3]), s128(E.s_egc), ALU.mult))
            dve.tensor_tensor(srr[:], svtok[:], srr[:], ALU.subtract).then_inc(G["r_made"], 1)
            dve.wait_ge(G["solved"], 1)
            dve.tensor_tensor(sy1[:], tok(bank[3]), s128(sd2), ALU.mult).then_inc(G["y1"], 1)
            dve.wait_ge(G["y1"], 1)
            dve.tensor_tensor(svd[:], sy1[:], s128(E.s_dl), ALU.mult).then_inc(G["vd"], 1)
            dve.wait_ge(G["attn_mm"], 1)
            dve.tensor_tensor(so[:], so[:], tok(bank[4]), ALU.add).then_inc(G["o_made"], 1)
            for h in range(H):
                for x in range(2):
                    dve.wait_ge(G["su"], 2 * h + x + 1)
                    for b in range(4):
                        s = st[:, 4 * x + b, h, :]
                        ins = dve.scalar_tensor_tensor(out=s, in0=s, scalar=E.s_gl[:, h, 4 * x + b:4 * x + b + 1], in1=bank[6 + x][:, P * b:P * b + P],
                                                       op0=ALU.mult, op1=ALU.add)
                    ins.then_inc(G["su_read"], 1)
            dve.wait_ge(G["o_squared"], 1)
            then(dve.tensor_tensor(sors[:], soss[:], srq2[:], ALU.mult))
            dve.tensor_scalar(sors[:], sors[:], EPS, None, ALU.add).then_inc(G["o_eps"], 1)
            dve.wait_ge(G["o_pow"], 1)
            then(dve.tensor_tensor(sors[:], sors[:], srq[:], ALU.mult))
            dve.tensor_tensor(so[:], so[:], s128(sors), ALU.mult).then_inc(G["o_scaled"], 1)
            dve.wait_ge(G["o_turned"], 1)
            dve.scalar_tensor_tensor(out=E.mix_s[:, 0:NJ, :], in0=bank[5][:, 0:H * NS].rearrange("p (h t) -> p h t", h=H), scalar=E.g_dn[:, 0:1],
                                     in1=sam[:, KINDS.index("za")], op0=ALU.mult, op1=ALU.mult).then_inc(G["delta_gated"], 1)
            dve.wait_ge(G["tab_dist"], 1)
            then(dve.tensor_scalar(tix[:], tix[:], T - 1, None, ALU.bitwise_and))
            then(dve.tensor_tensor(dist[:], dist[:], tix[:].to_broadcast([ROWS, KEYS]), ALU.add))
            window_table(None, dve, "dve", tab[:], dist[:], ta[:], tb[:], None, G["tab_step"], None, None, None, 0)
            dve.wait_ge(G["qw_zero"], 2)

            def pick_q(b, u):
                t = bass.ds(T * b, T)
                for e in range(2):
                    half = slice(HD * e, HD * e + HD)
                    dve.tensor_copy(qw[u][half, :].rearrange("p (j z) -> p j z", z=DIAG)[:, :, T * e:T * e + T], sam[half, KINDS.index("wq"), :, t])
                dve.tensor_copy(kw[u][:], sam[:, KINDS.index("wk"), :, t]).then_inc(G["q_picked"], 1)

            def turned(b):
                for j in range(NJ):
                    dve.wait_ge(G["kT_used"], NJ * b + j + 1)
                    dve.wait_ge(G["kT_mm"], 2 * (NJ * b + j) + 2)
                    dve.tensor_copy(kT[:, j % 2, NEAR:], bank[2 + j % 2][:, 0:FARS]).then_inc(G["kT_dve"], 1)

            def mask(b, u):
                dve.wait_ge(G["scored"], b + 1)
                dve.sem_inc(G["seen"], 1)
                for x, (a, z) in enumerate(((0, NEAR), (NEAR, KEYS))):
                    dve.tensor_tensor_reduce(pr[:, u, a:z], bank[4 + x][0:ROWS, 0:z - a], tab[:, a:z], SCALE, -3.0e38, ALU.add, ALU.max,
                                             smax[:, u, x:x + 1]).then_inc(G["masked"], 1)
                dve.wait_ge(G["masked"], 2 * b + 4)
                dve.tensor_reduce(snmax[:, u:u + 1], smax[:, u, :], AX.X, ALU.max, negate=True).then_inc(G["max"], 1)

            def normalise(b, u):
                dve.wait_ge(G["exped"], b + 1)
                dve.reciprocal(slinv[:, u:u + 1], slsum[:, u:u + 1]).then_inc(G["lsum"], 1)
                dve.wait_ge(G["lsum"], b + 1)
                dve.tensor_scalar(pr[:, u, :], pr[:, u, :], slinv[:, u:u + 1], None, ALU.mult).then_inc(G["normed"], 1)

            def pick_o(b):
                dve.wait_ge(G["mixed"], b + 1)
                t = bass.ds(T * b, T)
                for e in range(2):
                    half = slice(HD * e, HD * e + HD)
                    o = bank[7][half, 0:2 * T * NJ].rearrange("p (j e t) -> p j e t", e=2, t=T)[:, :, e, :]
                    ins = dve.tensor_tensor(E.mix_s[half, NJ:2 * NJ, t], o, sam[half, KINDS.index("zb"), :, t], ALU.mult)
                ins.then_inc(G["o_picked"], 1)

            pick_q(0, 0)
            turned(0)
            mask(0, 0)
            pick_q(1, 1)
            with dve.Fori(0, DEC_BATCH // 2 - 1) as i:
                for e in range(2):
                    b, u = 2 * i + 1 + e, 1 - e
                    turned(b)
                    normalise(b - 1, e)
                    mask(b, u)
                    pick_q(b + 1, e)
                    pick_o(b - 1)
            b = DEC_BATCH - 1
            turned(b)
            normalise(b - 1, 0)
            mask(b, 1)
            pick_o(b - 1)
            normalise(b, 1)
            pick_o(b)


def output(nc, env, D):
    with ExitStack() as ctx:
        sem = env.sem
        sb = lambda n, s, d=F32: ctx.enter_context(nc.sbuf_tensor(n, s, d))
        yp = [ctx.enter_context(nc.psum_tensor(f"y_ps{i}", [P, CHUNK], F32)) for i in range(4)]
        wraw = sb("wraw", [P, 2, D_MODEL])
        w_hi, w_lo = (sb(n, [P, KT, D_MODEL], F32R) for n in ("wo_hi", "wo_lo"))
        mx, mh, ml = sb("mx", [P, 2, KT, P]), sb("mh", [P, 2, KT, P], F32R), sb("ml", [P, 2, KT, P], F32R)
        xt, yt = sb("xt", [P, 2, D_MODEL]), sb("yt", [P, 2, D_MODEL])
        gf, junk, st = sb("gf", [P, D_MODEL]), sb("y_junk", [P, D_MODEL]), sb("y_st", [P, 2, 4])
        O = {n: sem("y_" + n) for n in "const w_hi w_lo hi lo mm added squared mean root inv done seen".split()}
        w_in, x_in, out = ([sem(f"y_{n}{u}") for u in range(2)] for n in ("w_in", "in", "out"))
        block = ctx.enter_context(nc.Block())
        N_IN = 2

        @block.sync
        def _(sp):
            sp.dma_start(gf[:], D.final_norm_g.unsqueeze(0).to_broadcast([P, D_MODEL])).then_inc(O["const"], 16)
            for k in range(KT):
                if k >= 2:
                    sp.wait_ge(O["w_lo"], k - 1)
                sp.dma_start(wraw[:, k % 2, :], D.w_out[P * k:P * k + P, :]).then_inc(w_in[k % 2], 16)

            def load(n, u):
                t = bass.ds(P * n, P)
                sp.dma_start(mx[:, u], D.mix[:, t].rearrange("(k p) t -> p k t", p=P)).then_inc(x_in[u], 16)
                sp.dma_start(xt[:, u, :], D.x[t, :]).then_inc(x_in[u], 16)

            load(0, 0)
            load(1, 1)
            with sp.Fori(0, NT // 2 - 1) as i:
                for u in range(2):
                    n = 2 * i + u
                    sp.wait_ge(O["done"], n + 1)
                    sp.sem_inc(O["seen"], 1)
                    sp.dma_start(D.y[bass.ds(P * n, P), :], yt[:, u, :]).then_inc(out[u], 16)
                    load(n + 2, u)
            for u in range(2):
                sp.wait_ge(O["done"], NT - 2 + u + 1)
                sp.dma_start(D.y[P * (NT - 2 + u):P * (NT - 1 + u), :], yt[:, u, :]).then_inc(out[u], 16)
                if u == 0:
                    sp.dma_start(xt[0:NS, 0, :], D.x_sample).then_inc(x_in[0], 16)
            sp.wait_ge(O["done"], NT + 1)
            sp.dma_start(D.y_s, yt[0:NS, 0, :]).then_inc(out[0], 16)
            sp.wait_ge(out[0], 16 * (NT // 2 + 1))
            sp.wait_ge(out[1], 16 * (NT // 2))

        @block.scalar
        def _(act):
            for k in range(KT):
                act.wait_ge(w_in[k % 2], 16 * (k // 2) + 16)
                act.activation(w_hi[:, k, :], wraw[:, k % 2, :], ACT.Copy).then_inc(O["w_hi"], 1)

            def split(n, u, i):
                act.wait_ge(x_in[u], 16 * N_IN * (i + 1))
                act.wait_ge(O["mm"], 2 * n + 2)
                act.activation(mh[:, u], mx[:, u], ACT.Copy).then_inc(O["hi"], 1)

            def root(n, u, rows):
                act.wait_ge(O["added"], 4 + 2 * n + 2)
                act.activation(junk[0:rows, :], yt[0:rows, u, :], ACT.Square, accum_out=st[0:rows, u, 0:1]).then_inc(O["squared"], 1)
                act.wait_ge(O["mean"], n + 1)
                act.activation(st[0:rows, u, 2:3], st[0:rows, u, 1:2], ACT.Sqrt).then_inc(O["root"], 1)

            split(0, 0, 0)
            split(1, 1, 0)
            with act.Fori(0, NT // 2 - 1) as i:
                for u in range(2):
                    root(2 * i + u, u, P)
                    split(2 * i + u + 2, u, i + 1)
            root(NT - 2, 0, P)
            act.wait_ge(O["mm"], 2 * NT + 2)
            act.activation(mh[:, 0, :, 0:NS], env.mix_s[:], ACT.Copy).then_inc(O["hi"], 1)
            root(NT - 1, 1, P)
            root(NT, 0, NS)

        @block.gpsimd
        def _(pool):
            def split(n, u):
                pool.wait_ge(O["hi"], n + 1)
                pool.tensor_tensor(ml[:, u], mx[:, u], mh[:, u].bitcast(F32), ALU.subtract).then_inc(O["lo"], 1)

            with pool.Fori(0, NT // 2) as i:
                for u in range(2):
                    split(2 * i + u, u)
            pool.wait_ge(O["hi"], NT + 1)
            pool.tensor_tensor(ml[:, 0, :, 0:NS], env.mix_s[:], mh[:, 0, :, 0:NS].bitcast(F32), ALU.subtract).then_inc(O["lo"], 1)

        @block.tensor
        def _(pe):
            pe.sem_inc(O["mm"], 4)
            pe.wait_ge(O["w_lo"], KT)

            def tile(n, u, rows):
                pe.wait_ge(O["lo"], n + 1)
                pe.wait_ge(O["added"], 2 * n + 2)
                for c in range(2):
                    cs = slice(CHUNK * c, CHUNK * (c + 1))
                    o = yp[2 * u + c][0:rows, :]
                    for k in range(KT):
                        pe.matmul(o, mh[:, u, k, 0:rows], w_hi[:, k, cs], start=(k == 0), stop=False)
                        pe.matmul(o, mh[:, u, k, 0:rows], w_lo[:, k, cs], start=False, stop=False)
                        mm = pe.matmul(o, ml[:, u, k, 0:rows], w_hi[:, k, cs], start=False, stop=(k == KT - 1))
                    mm.then_inc(O["mm"], 1)

            with pe.Fori(0, NT // 2) as i:
                for u in range(2):
                    tile(2 * i + u, u, P)
            tile(NT, 0, NS)

        @block.vector
        def _(dve):
            dve.sem_inc(O["added"], 4)
            for k in range(KT):
                dve.wait_ge(O["w_hi"], k + 1)
                dve.tensor_tensor(w_lo[:, k, :], wraw[:, k % 2, :], w_hi[:, k, :].bitcast(F32), ALU.subtract).then_inc(O["w_lo"], 1)
            dve.wait_ge(O["const"], 16)

            def tile(n, u, i, rows, out_wait):
                if out_wait:
                    dve.wait_ge(out[u], 16 * i)
                for c in range(2):
                    cs = slice(CHUNK * c, CHUNK * (c + 1))
                    dve.wait_ge(O["mm"], 4 + 2 * n + c + 1)
                    dve.tensor_tensor(yt[0:rows, u, cs], yp[2 * u + c][0:rows, :], xt[0:rows, u, cs], ALU.add).then_inc(O["added"], 1)
                dve.wait_ge(O["squared"], n + 1)
                dve.tensor_scalar(st[0:rows, u, 1:2], st[0:rows, u, 0:1], 1.0 / D_MODEL, EPS, ALU.mult, ALU.add).then_inc(O["mean"], 1)
                dve.wait_ge(O["root"], n + 1)
                dve.reciprocal(st[0:rows, u, 3:4], st[0:rows, u, 2:3]).then_inc(O["inv"], 1)
                dve.wait_ge(O["inv"], n + 1)
                y = yt[0:rows, u, :]
                dve.scalar_tensor_tensor(out=y, in0=y, scalar=st[0:rows, u, 3:4], in1=gf[0:rows, :], op0=ALU.mult, op1=ALU.mult).then_inc(O["done"], 1)

            tile(0, 0, 0, P, False)
            tile(1, 1, 0, P, False)
            with dve.Fori(1, NT // 2) as i:
                for u in range(2):
                    tile(2 * i + u, u, i, P, True)
            dve.wait_ge(x_in[0], 16 * (N_IN * NT // 2 + 1))
            tile(NT, 0, NT // 2, NS, True)


class Env:
    pass


class Dram:
    pass


def in_phase(nc, env, phase, D):
    mine = []

    def sem(name):
        mine.append(nc.alloc_semaphore(name=name))
        return mine[-1]

    env.sem = sem
    phase(nc, env, D)
    nc.all_engine_barrier()
    nc.clear_and_free_semaphores(mine)
    nc.all_engine_barrier()


def hybrid_step(nc, x_prompt, x_sample, state_conv, state_delta, cache_k_win, cache_v_win, norm_g, final_norm_g, w_in, conv_w,
                a_log, dt_bias, dn_norm_g, w_out, y_prompt, y_sample, new_conv_prompt, new_delta_prompt, new_k_prompt, new_v_prompt,
                new_conv_sample, new_delta_sample, new_k_sample, new_v_sample):
    env, D = Env(), Dram()
    D.x, D.y = x_prompt[0], y_prompt[0]
    D.x_sample, D.y_s = (t.rearrange("b t d -> (b t) d") for t in (x_sample, y_sample))
    D.state_conv, D.state_delta, D.new_conv_s, D.new_delta_s = state_conv[0], state_delta[0], new_conv_sample[0], new_delta_sample[0]
    D.cache_k, D.cache_v, D.out_k, D.out_v = (t[0].rearrange("b n h d -> b n (h d)") for t in (cache_k_win, cache_v_win, new_k_sample, new_v_sample))
    D.norm_g, D.final_norm_g, D.w_in, D.conv_w = norm_g[0], final_norm_g, w_in[0], conv_w[0]
    D.a_log, D.dt_bias, D.dn_norm_g, D.w_out = a_log[0], dt_bias[0], dn_norm_g[0], w_out[0]
    D.new_conv, D.new_delta = new_conv_prompt[0, 0], new_delta_prompt[0, 0]
    D.new_k, D.new_v = (t[0, 0].rearrange("n h d -> n (h d)") for t in (new_k_prompt, new_v_prompt))
    scratch = lambda n, s: nc.dram_tensor(n, s, F32, kind="Internal").ap()
    D.qk_ch, D.z_ch = scratch("qk_ch", [2, QK_W, SEQ]), scratch("z_ch", [2, QK_W, SEQ])
    D.k_tok, D.v_tok = scratch("k_tok", [SEQ, QK_W]), scratch("v_tok", [SEQ, QK_W])
    D.wqk, D.mix = scratch("wqk", [2, 2, SW_WIDTH, SEQ]), scratch("mix", [D_MODEL, SEQ])
    with ExitStack() as ctx:
        constants(nc, env, ctx)
        in_phase(nc, env, project, D)
        gate_tensors(nc, env, ctx)
        in_phase(nc, env, gates, D)
        in_phase(nc, env, mixers, D)
        in_phase(nc, env, sample, D)
        in_phase(nc, env, output, D)


_INS = ["x_prompt", "x_sample", "state_conv", "state_delta", "cache_k_win", "cache_v_win", "norm_g", "final_norm_g",
        "w_in", "conv_w", "a_log", "dt_bias", "dn_norm_g", "w_out"]
_OUTS = [(1, 2048, 1024), (8, 4, 1024), (1, 1, 3, 1536), (1, 1, 4, 128, 128), (1, 1, 2048, 8, 64), (1, 1, 2048, 8, 64),
         (1, 8, 3, 1536), (1, 8, 4, 128, 128), (1, 8, 2048, 8, 64), (1, 8, 2048, 8, 64)]


def kernel(**inputs):
    import numpy as _np
    import concourse.bacc as _bacc
    from concourse import mybir as _mybir
    from concourse.bass_utils import run_bass_kernel_spmd as _run

    nc = _bacc.Bacc("TRN2", target_bir_lowering=False, num_devices=1)
    arrays, args = {}, []
    for name in _INS:
        a = _np.ascontiguousarray(inputs[name])
        arrays[f"in_{name}_dram"] = a
        args.append(nc.dram_tensor(f"in_{name}_dram", a.shape, _mybir.dt.from_np(a.dtype), kind="ExternalInput").ap())
    for i, shape in enumerate(_OUTS):
        args.append(nc.dram_tensor(f"out_{i}_dram", shape, _mybir.dt.from_np(_np.dtype("float32")), kind="ExternalOutput").ap())
    hybrid_step(nc, *args)
    r = _run(nc, [arrays], core_ids=[0])
    return tuple(r.results[0][f"out_{i}_dram"] for i in range(len(_OUTS)))
```

```python
from contextlib import ExitStack

import concourse.bass as bass
from concourse import mybir

F32 = mybir.dt.float32
F32R = mybir.dt.float32r
BF16 = mybir.dt.bfloat16
I32 = mybir.dt.int32
ALU = mybir.AluOpType
ACT = mybir.ActivationFunctionType
AX = mybir.AxisListType

P = 128
D_MODEL = 1024
SEQ = 2048
DEC_BATCH = 8
DEC_SEQ = 4
NS = DEC_BATCH * DEC_SEQ
PAST = 2048
CONV_W = 4
TAIL = CONV_W - 1
DN_HEADS = 4
DK = 128
QK_W = DN_HEADS * DK
CONV_CH = 3 * QK_W
SW_HEADS = 8
HD = 64
SW_WIDTH = SW_HEADS * HD
EPS = 1e-6
KT = D_MODEL // P
CHUNK = 512
NCH = SEQ // CHUNK
NT = SEQ // P
KINDS = ("q", "k", "v", "za", "wq", "wk", "wv", "zb")
NK = len(KINDS)
O_AB = CONV_CH + QK_W
O_WIN = O_AB + 2 * DN_HEADS
COLS = (0, QK_W, 2 * QK_W, CONV_CH, O_WIN, O_WIN + SW_WIDTH, O_WIN + 2 * SW_WIDTH, O_WIN + 3 * SW_WIDTH)
NJ = QK_W // P
NTILES = NK * NJ
POSTED = ("q", "k", "v", "wk", "wv")
TURNED = ("k", "v", "wk", "wv")


def flat(t):
    return t.rearrange("p a b -> p (a b)")


def constants(nc, env, ctx):
    sb = lambda n, s, d=F32: ctx.enter_context(nc.sbuf_tensor(n, s, d))
    env.ident = sb("ident", [P, P])
    env.ones = sb("ones", [P, P])
    env.sam = sb("sam", [P, NK, NJ, NS])
    env.ab_tok = sb("ab_tok", [P, NT + 1, 8])
    env.ssq = sb("ssq", [P, NT, 2, NJ])
    env.conv_tail = sb("conv_tail", [P, 3 * NJ, TAIL])
    env.conv_wt = sb("conv_wt", [P, 3 * NJ, CONV_W])
    env.g_in = sb("g_in", [P, KT])


def project(nc, env, D):
    with ExitStack() as ctx:
        sb = lambda n, s, d=F32: ctx.enter_context(nc.sbuf_tensor(n, s, d))
        ps = lambda n: ctx.enter_context(nc.psum_tensor(n, [P, CHUNK], F32))
        sem = env.sem
        ident, ones, sam, ab_tok, ssq, g_in = env.ident, env.ones, env.sam, env.ab_tok, env.ssq, env.g_in
        conv_tail, conv_wt = env.conv_tail, env.conv_wt

        XS = 4
        hT_hi = sb("hT_hi", [P, KT, SEQ], F32R)
        hT_lo = sb("hT_lo", [P, KT, SEQ], F32R)
        w_raw = sb("w_raw", [P, 2, KT, P])
        w_hi = [sb(f"w_hi{s}", [P, KT, P], F32R) for s in range(2)]
        w_lo = [sb(f"w_lo{s}", [P, KT, P], F32R) for s in range(2)]
        raw = sb("raw", [P, TAIL + SEQ])
        acc = sb("acc", [P, 2, CHUNK])
        sil = sb("sil", [P, NCH, CHUNK])
        sq = sb("sq", [P, 2, CHUNK])
        hi = sb("hi", [P, 2, CHUNK], F32R)
        lo = sb("lo", [P, 2, CHUNK], F32R)
        xr = sb("xr", [P, 2, D_MODEL])
        tmp = acc
        tok, zr = (xr[:, s, :].rearrange("p (a b) -> p a b", a=2) for s in range(2))
        junk = flat(sil[:, 0:2, :])
        stat = sb("stat", [P, XS, 4])
        x_slot = [xr[:, 0, :], raw[:, TAIL:TAIL + D_MODEL], xr[:, 1, :], raw[:, TAIL + D_MODEL:TAIL + 2 * D_MODEL]]
        h_sam = sb("h_sam", [P, KT, NS])
        sam_row = sb("sam_row", [NS, P])
        abT = flat(sil)[0:2 * DN_HEADS, :]

        pj = [ps(f"pj{c}") for c in range(NCH)]
        tp = [ps(f"tp{c}") for c in range(2)]
        p_sam = ps("p_sam")
        p_ssq = ps("p_ssq")

        ident_set, ident_done, ones_done, consts_in = (sem(n) for n in ("ident_set", "ident_done", "ones_done", "consts_in"))
        w_loaded, x_loaded = [sem(f"w_loaded{s}") for s in range(2)], [sem(f"x_loaded{s}") for s in range(XS)]
        sq_summed, ms_done, root_done, inv_done, xn_done = (sem(n) for n in ("sq_summed", "ms_done", "root_done", "inv_done", "xn_done"))
        xT_done, tmp_done, hT_hi_done, hT_lo_done = (sem(n) for n in ("xT_done", "tmp_done", "hT_hi_done", "hT_lo_done"))
        w_hi_done, w_lo_done, pj_done, sam_mm, sam_row_done, sam_turned, sam_free = (
            sem(n) for n in ("w_hi_done", "w_lo_done", "pj_done", "sam_mm", "sam_row_done", "sam_turned", "sam_free"))
        pj_free = [sem(f"pj_free{c}") for c in range(NCH)]
        chain, conv_done, sil_done, sq_done = (sem(n) for n in ("chain", "conv_done", "sil_done", "sq_done"))
        post_done, tok_done, ssq_read, hi_done, w_f32_done = (sem(n) for n in ("post_done", "tok_done", "ssq_read", "hi_done", "w_f32_done"))
        sil_stored = [sem(f"sil_stored{c}") for c in range(NCH)]
        tok_stored, hi_stored, lo_stored, z_stored = ([sem(f"{n}{s}") for s in range(2)] for n in ("tok_stored", "hi_stored", "lo_stored", "z_stored"))
        seen = sem("seen")
        shifted, tail_done, tail_stored = sem("shifted"), sem("tail_done"), sem("tail_stored")
        raw_head, ab_evac, ab_turned = sem("raw_head"), sem("ab_evac"), sem("ab_turned")
        block = ctx.enter_context(nc.Block())

        X_CREDIT = 2 * XS
        TMP_CREDIT = 2
        W_CREDIT = 2
        CONV_CREDIT = 4
        SIL_CREDIT = 2
        POST_CREDIT = 4
        TOK_CREDIT = 2
        SSQ_CREDIT = 1

        def lagged(y, c):
            return (KINDS[y], c - 2) if c >= 2 else (KINDS[y - 1] if y else None, c + 2)

        def posts_before(j, kind, c):
            return 4 * (len(POSTED) * j + POSTED.index(kind)) + c

        def turned_before(j, kind, c):
            return 4 * (len(TURNED) * j + TURNED.index(kind)) + c

        @block.sync
        def _(sp):
            with sp.Fori(0, NT // XS) as i:
                for s in range(XS):
                    n = XS * i + s
                    sp.wait_ge(xT_done, 2 * n + 2)
                    sp.dma_start(x_slot[s], D.x[bass.ds(P * n, P), :]).then_inc(x_loaded[s], 16)
            sp.wait_ge(xT_done, 2 * NT + 2)
            sp.dma_start(x_slot[0][0:NS, :], D.x_sample).then_inc(x_loaded[0], 16)

            def load_w(j, y):
                src = D.w_in[:, bass.ds(P * j + COLS[y], P)].rearrange("(k p) c -> p k c", p=P)
                sp.dma_start(w_raw[:, y % 2], src).then_inc(w_loaded[y % 2], 16)

            for s in range(2):
                for stored in (hi_stored, lo_stored, z_stored, tok_stored):
                    sp.sem_inc(stored[s], 16)
                load_w(0, s)

            def store_turned(j, kind, c):
                sp.wait_ge(tok_done, TOK_CREDIT + turned_before(j, kind, c) + 1)
                sp.sem_inc(seen, 1)
                dst = {"k": D.k_tok, "v": D.v_tok, "wk": D.new_k, "wv": D.new_v}[kind]
                dst = dst[CHUNK * c:CHUNK * (c + 1), bass.ds(P * j, P)].rearrange("(b p) d -> p b d", p=P)
                sp.dma_start(dst, tok[:, c % 2, :].rearrange("p (b d) -> p b d", b=4)).then_inc(tok_stored[c % 2], 16)

            with sp.Fori(0, NJ) as j:
                for y, kind in enumerate(KINDS):
                    sp.wait_ge(sam_mm, NK * j + y + 1)
                    load_w(j + (y + 2) // NK, (y + 2) % NK)
                    rows = bass.ds(P * j, P)
                    for c in range(NCH):
                        cs = slice(CHUNK * c, CHUNK * (c + 1))
                        if kind in ("q", "k"):
                            sp.wait_ge(sil_done, SIL_CREDIT + 4 * (3 * j + y) + c + 1)
                            sp.dma_start(D.qk_ch[y, rows, cs], sil[:, c, :]).then_inc(sil_stored[c], 16)
                        if kind in ("za", "zb"):
                            sp.wait_ge(pj_free[c], NK * j + y + 2)
                            sp.dma_start(D.z_ch[int(kind == "zb"), rows, cs], zr[:, c % 2, :]).then_inc(z_stored[c % 2], 16)
                        if kind in ("wq", "wk"):
                            q = int(kind == "wk")
                            sp.wait_ge(hi_done, 4 * (2 * j + q) + c + 1)
                            sp.dma_start(D.wqk[q, 0, rows, cs], hi[:, c % 2, :].bitcast(F32)).then_inc(hi_stored[c % 2], 16)
                            sp.wait_ge(pj_free[c], NK * j + y + 2)
                            sp.dma_start(D.wqk[q, 1, rows, cs], lo[:, c % 2, :].bitcast(F32)).then_inc(lo_stored[c % 2], 16)
                        back, bc = lagged(y, c)
                        if back in TURNED:
                            store_turned(j, back, bc)
            sp.wait_ge(w_lo_done, W_CREDIT + NTILES + 1)
            sp.dma_start(w_raw[:, 0], D.w_in[:, O_AB:O_AB + P].rearrange("(k p) c -> p k c", p=P)).then_inc(w_loaded[0], 16)
            sp.wait_ge(tail_done, 3 * NJ)
            with nc.allow_non_contiguous_dma(reason="the last three rows of a channel-major tile"):
                for r in range(TAIL):
                    sp.dma_start(D.new_conv[r].rearrange("(t p) -> p t", p=P), conv_tail[:, :, r]).then_inc(tail_stored, 16)
            sp.wait_ge(w_loaded[1], 16 * (NTILES // 2 + 1))
            sp.wait_ge(tail_stored, 16 * TAIL)
            for c in range(NCH):
                sp.wait_ge(sil_stored[c], 16 * 2 * NJ)
            for s in range(2):
                sp.wait_ge(hi_stored[s], 16 + 16 * 4 * NJ)
                sp.wait_ge(lo_stored[s], 16 + 16 * 4 * NJ)
                sp.wait_ge(z_stored[s], 16 + 16 * 4 * NJ)
                sp.wait_ge(tok_stored[s], 16 + 16 * 8 * NJ)

        @block.gpsimd
        def _(pool):
            pool.memset(ident[:], 0.0).then_inc(ident_set, 1)
            pool.memset(ones[:], 1.0).then_inc(ones_done, 1)
            pool.wait_ge(ident_set, 1)
            pool.affine_select(out=ident[:], in_=ident[:], compare_op=ALU.not_equal, fill=1.0, base=0,
                               pattern=[[-1, P]], channel_multiplier=1).then_inc(ident_done, 1)
            pool.sem_inc(hT_lo_done, TMP_CREDIT)

            def h_low(n, rows, cols):
                for b in range(2):
                    pool.wait_ge(hT_hi_done, 2 * n + b + 1)
                    ks = slice(4 * b, 4 * b + 4)
                    t = tmp[:, b, 0:4 * rows].rearrange("p (k t) -> p k t", k=4)
                    pool.tensor_tensor(hT_lo[:, ks, cols], t, hT_hi[:, ks, cols].bitcast(F32), ALU.subtract).then_inc(hT_lo_done, 1)

            with pool.Fori(0, NT) as n:
                h_low(n, P, bass.ds(P * n, P))
            pool.memset(raw[:, 0:TAIL], 0.0).then_inc(raw_head, 1)

            with pool.Fori(0, DEC_BATCH) as b:
                pool.wait_ge(pj_done, 16 * b + 1)
                pool.sem_inc(seen, 1)
                for old, new in ((D.cache_k, D.out_k), (D.cache_v, D.out_v)):
                    pool.dma_start(new[bass.ds(b, 1), 0:PAST - DEC_SEQ, :], old[bass.ds(b, 1), DEC_SEQ:PAST, :]).then_inc(shifted, 16)
            pool.wait_ge(shifted, 16 * 2 * DEC_BATCH)

        @block.tensor
        def _(pe):
            pe.sem_inc(xT_done, X_CREDIT)
            pe.wait_ge(ident_done, 1)

            def turn_x(n, s, rows):
                pe.wait_ge(xn_done, n + 1)
                for b in range(2):
                    pe.wait_ge(tmp_done, 2 * n + b + 1)
                    for k in range(4):
                        x_k = x_slot[s][0:rows, (4 * b + k) * P:(4 * b + k + 1) * P]
                        mm = pe.transpose(pj[b][:, k * rows:(k + 1) * rows], x_k, ident[0:rows, 0:rows])
                    mm.then_inc(xT_done, 1)

            with pe.Fori(0, NT // XS) as i:
                for s in range(XS):
                    turn_x(XS * i + s, s, P)
            turn_x(NT, 0, NS)
            pe.wait_ge(tmp_done, TMP_CREDIT + 2 * NT + 2)
            pe.wait_ge(hT_lo_done, TMP_CREDIT + 2 * NT)
            pe.wait_ge(ones_done, 1)
            for c in range(NCH):
                pe.sem_inc(pj_free[c], 1)
            pe.sem_inc(sam_free, 1)

            def product(out, s, cols, m=P):
                for k in range(KT):
                    pe.matmul(out, w_hi[s][:, k, 0:m], hT_hi[:, k, cols], start=(k == 0), stop=False)
                    pe.matmul(out, w_hi[s][:, k, 0:m], hT_lo[:, k, cols], start=False, stop=False)
                    mm = pe.matmul(out, w_lo[s][:, k, 0:m], hT_hi[:, k, cols], start=False, stop=(k == KT - 1))
                return mm

            def sam_product(s, m=P):
                for k in range(KT):
                    mm = pe.matmul(p_sam[0:NS, 0:m], h_sam[:, k, :], w_raw[:, s, k, 0:m], start=(k == 0), stop=(k == KT - 1))
                mm.then_inc(sam_mm, 1)

            def post(j, kind, c):
                y = KINDS.index(kind)
                if kind in ("q", "k"):
                    r = 4 * (2 * j + y) + c
                    pe.wait_ge(sq_done, r + 1)
                    pe.wait_ge(ssq_read, r + 1)
                    for b in range(4):
                        mm = pe.matmul(p_ssq[:, 4 * (c % 2) + b:4 * (c % 2) + b + 1], sq[:, c % 2, b * P:(b + 1) * P],
                                       ones[:, 0:1], start=True, stop=True)
                if kind in TURNED:
                    if kind in ("k", "v"):
                        pe.wait_ge(sil_done, SIL_CREDIT + 4 * (3 * j + y) + c + 1)
                    elif kind == "wk":
                        pe.wait_ge(w_f32_done, 4 * j + c + 1)
                    else:
                        pe.wait_ge(pj_free[c], NK * j + y + 2)
                    pe.wait_ge(tok_done, turned_before(j, kind, c) + 1)
                    for b in range(4):
                        mm = pe.transpose(tp[c % 2][:, b * P:(b + 1) * P], sil[:, c, b * P:(b + 1) * P], ident[:])
                mm.then_inc(post_done, 1)

            with pe.Fori(0, NJ) as j:
                for y, kind in enumerate(KINDS):
                    t = NK * j + y
                    pe.wait_ge(w_lo_done, W_CREDIT + t + 1)
                    for c in range(NCH):
                        pe.wait_ge(pj_free[c], t + 1)
                        product(pj[c][:, :], y % 2, slice(CHUNK * c, CHUNK * (c + 1))).then_inc(pj_done, 1)
                        if c == 0:
                            pe.wait_ge(sam_free, t + 1)
                            sam_product(y % 2)
                        if c == 2:
                            pe.wait_ge(sam_row_done, t + 1)
                            pe.sem_inc(seen, 1)
                            pe.transpose(p_sam[:, P:P + NS], sam_row[:], ident[0:NS, 0:NS]).then_inc(sam_turned, 1)
                        back, bc = lagged(y, c)
                        if back in POSTED:
                            post(j, back, bc)
            pe.wait_ge(w_lo_done, W_CREDIT + NTILES + 2)
            for c in range(NCH):
                pe.wait_ge(pj_free[c], NTILES + 1)
                product(pj[c][0:2 * DN_HEADS, :], 0, slice(CHUNK * c, CHUNK * (c + 1)), 2 * DN_HEADS).then_inc(pj_done, 1)
            pe.wait_ge(sam_free, NTILES + 1)
            sam_product(0, 2 * DN_HEADS)
            pe.wait_ge(ab_evac, NCH)
            pe.wait_ge(tok_done, TOK_CREDIT + 16 * NJ)
            for n in range(NT):
                mm = pe.transpose(tp[0][:, 8 * n:8 * n + 8], abT[:, n * P:(n + 1) * P], ident[0:8, 0:8])
            mm.then_inc(ab_turned, 1)

        @block.scalar
        def _(act):
            with nc.allow_non_contiguous_dma(reason="a few weights, once"):
                act.dma_start(g_in[:], D.norm_g.rearrange("(k p) -> p k", p=P)).then_inc(consts_in, 16)
                for r in range(CONV_W):
                    act.dma_start(conv_wt[:, :, r], D.conv_w[r].rearrange("(t p) -> p t", p=P)).then_inc(consts_in, 16)
            def norm_a(n, s, i, rows):
                act.wait_ge(x_loaded[s], 16 * i + 16)
                act.activation(junk[0:rows, :], x_slot[s][0:rows, :], ACT.Square, accum_out=stat[0:rows, s, 0:1]).then_inc(sq_summed, 1)

            def norm_r(n, s, rows):
                act.wait_ge(ms_done, n + 1)
                act.activation(stat[0:rows, s, 2:3], stat[0:rows, s, 1:2], ACT.Sqrt).then_inc(root_done, 1)

            def norm_b(n, rows, cols):
                for b in range(2):
                    act.wait_ge(tmp_done, TMP_CREDIT + 2 * n + b + 1)
                    t = tmp[:, b, 0:4 * rows].rearrange("p (k t) -> p k t", k=4)
                    act.activation(hT_hi[:, 4 * b:4 * b + 4, cols], t, ACT.Copy).then_inc(hT_hi_done, 1)

            for n in range(2):
                norm_a(n, n, 0, P)
                norm_r(n, n, P)
            with act.Fori(0, NT // XS - 1) as i:
                for s in range(XS):
                    n, s2 = XS * i + s, (s + 2) % XS
                    norm_a(n + 2, s2, i + (s + 2) // XS, P)
                    norm_b(n, P, bass.ds(P * n, P))
                    norm_r(n + 2, s2, P)
            for n in range(NT - XS, NT):
                s2, rows = (n + 2) % XS, P if n + 2 < NT else NS
                if n + 2 <= NT:
                    norm_a(n + 2, s2, (n + 2) // XS, rows)
                norm_b(n, P, slice(P * n, P * (n + 1)))
                if n + 2 <= NT:
                    norm_r(n + 2, s2, rows)

            def split(t, s, nth):
                act.wait_ge(w_loaded[s], 16 * nth + 16)
                act.activation(w_hi[s][:], w_raw[:, s], ACT.Copy).then_inc(w_hi_done, 1)

            split(0, 0, 0)
            with act.Fori(0, NJ) as j:
                for y, kind in enumerate(KINDS):
                    t = NK * j + y
                    split(t + 1, (y + 1) % 2, NK // 2 * j + (y + 1) // 2)
                    for c in range(NCH):
                        if c == 1:
                            act.wait_ge(sam_mm, t + 1)
                            act.activation(sam_row[:], p_sam[0:NS, 0:P], ACT.Copy).then_inc(sam_row_done, 1)
                        if c == 3:
                            act.wait_ge(sam_turned, t + 1)
                            act.activation(sam[:, y, bass.ds(j, 1), :].rearrange("p a t -> p (a t)"), p_sam[:, P:P + NS],
                                           ACT.Silu if kind in ("za", "zb") else ACT.Copy).then_inc(sam_free, 1)
                        act.wait_ge(pj_done, 4 * t + c + 1)
                        if kind in ("q", "k", "v"):
                            u = 4 * (3 * j + y) + c
                            act.wait_ge(conv_done, 4 * (3 * j + y) + min(c + 1, NCH - 1) + 1)
                            act.activation(raw[:, TAIL + CHUNK * c:TAIL + CHUNK * (c + 1)], pj[c][:], ACT.Copy).then_inc(pj_free[c], 1)
                            act.wait_ge(conv_done, CONV_CREDIT + u + 1)
                            act.wait_ge(post_done, posts_before(j, kind, c) + 1)
                            if kind != "q":
                                act.wait_ge(sil_stored[c], 16 * (2 * j + y))
                            act.activation(sil[:, c, :], acc[:, c % 2, :], ACT.Silu).then_inc(sil_done, 1)
                            if kind != "v":
                                act.wait_ge(sil_done, SIL_CREDIT + u + 1)
                                act.wait_ge(post_done, posts_before(j, kind, c) + 3)
                                act.activation(sq[:, c % 2, :], sil[:, c, :], ACT.Square).then_inc(sq_done, 1)
                        elif kind in ("za", "zb"):
                            act.wait_ge(z_stored[c % 2], 16 * (2 * (2 * j + (kind == "zb")) + c // 2) + 16)
                            act.activation(zr[:, c % 2, :], pj[c][:], ACT.Silu).then_inc(pj_free[c], 1)
                        elif kind == "wv":
                            act.wait_ge(post_done, posts_before(j, kind, c) + 1)
                            act.activation(sil[:, c, :], pj[c][:], ACT.Copy).then_inc(pj_free[c], 1)
                        else:
                            act.wait_ge(hi_stored[c % 2], 16 * (2 * (2 * j + (kind == "wk")) + c // 2) + 16)
                            act.wait_ge(pj_free[(c + 2) % NCH], t + 1 + (c >= 2))
                            if kind == "wk":
                                act.wait_ge(post_done, posts_before(j, kind, c) + 1)
                                act.activation(sil[:, c, :], pj[c][:], ACT.Copy).then_inc(w_f32_done, 1)
                            act.activation(hi[:, c % 2, :], pj[c][:], ACT.Copy).then_inc(hi_done, 1)
            split(NTILES, 0, NTILES // 2 + 1)
            for c in range(NCH):
                act.wait_ge(pj_done, 4 * NTILES + c + 1)
                act.activation(abT[:, CHUNK * c:CHUNK * (c + 1)], pj[c][0:8, :], ACT.Copy).then_inc(ab_evac, 1)
            act.wait_ge(sam_mm, NTILES + 1)
            act.activation(ab_tok[0:NS, NT, :], p_sam[0:NS, 0:2 * DN_HEADS], ACT.Copy).then_inc(ab_evac, 1)

        @block.vector
        def _(dve):
            dve.sem_inc(tmp_done, TMP_CREDIT)
            dve.sem_inc(w_lo_done, W_CREDIT)
            dve.sem_inc(conv_done, CONV_CREDIT)
            dve.sem_inc(sil_done, SIL_CREDIT)
            dve.sem_inc(post_done, POST_CREDIT)
            dve.sem_inc(tok_done, TOK_CREDIT)
            dve.sem_inc(ssq_read, SSQ_CREDIT)

            def norm_a(n, s, rows):
                dve.wait_ge(sq_summed, n + 1)
                dve.tensor_scalar(stat[0:rows, s, 1:2], stat[0:rows, s, 0:1], 1.0 / D_MODEL, EPS, ALU.mult, ALU.add).then_inc(ms_done, 1)

            def norm_s(n, s, rows):
                dve.wait_ge(root_done, n + 1)
                dve.reciprocal(stat[0:rows, s, 3:4], stat[0:rows, s, 2:3]).then_inc(inv_done, 1)
                dve.wait_ge(inv_done, n + 1)
                dve.tensor_scalar(x_slot[s][0:rows, :], x_slot[s][0:rows, :], stat[0:rows, s, 3:4], None, ALU.mult).then_inc(xn_done, 1)

            def norm_b(n, rows, out=None):
                for b in range(2):
                    dve.wait_ge(xT_done, X_CREDIT + 2 * n + b + 1)
                    if out is None:
                        dve.wait_ge(hT_lo_done, 2 * n + b + 1)
                    view = lambda a: a.rearrange("p (k t) -> p k t", k=4)
                    t = view(tmp[:, b, 0:4 * rows]) if out is None else out[:, 4 * b:4 * b + 4, :]
                    dve.tensor_tensor(t, view(pj[b][:, 0:4 * rows]),
                                      g_in[:, 4 * b:4 * b + 4].unsqueeze(2).to_broadcast([P, 4, rows]), ALU.mult).then_inc(tmp_done, 1)

            norm_a(0, 0, P)
            norm_s(0, 0, P)
            norm_a(1, 1, P)
            dve.wait_ge(consts_in, 16 * (1 + CONV_W))
            with dve.Fori(0, NT // XS - 1) as i:
                for s in range(XS):
                    n = XS * i + s
                    norm_s(n + 1, (s + 1) % XS, P)
                    norm_b(n, P)
                    norm_a(n + 2, (s + 2) % XS, P)
            for n in range(NT - XS, NT):
                norm_s(n + 1, (n + 1) % XS, P if n + 1 < NT else NS)
                norm_b(n, P)
                if n + 2 <= NT:
                    norm_a(n + 2, (n + 2) % XS, P if n + 2 < NT else NS)
            norm_b(NT, NS, h_sam)

            def split(t, s):
                dve.wait_ge(w_hi_done, t + 1)
                dve.tensor_tensor(w_lo[s][:], w_raw[:, s], w_hi[s][:].bitcast(F32), ALU.subtract).then_inc(w_lo_done, 1)

            def conv(j, y, c):
                u = 4 * (3 * j + y) + c
                dve.wait_ge(sil_done, u + 1)
                w = lambda r: conv_wt[:, bass.ds(NJ * y + j, 1), r]
                x = lambda r: raw[:, CHUNK * c + r:CHUNK * c + r + CHUNK]
                a = acc[:, c % 2, :]
                dve.tensor_scalar(a, x(0), w(0), None, ALU.mult).then_inc(chain, 1)
                for r in range(1, CONV_W):
                    dve.wait_ge(chain, (CONV_W - 1) * u + r)
                    dve.scalar_tensor_tensor(out=a, in0=x(r), scalar=w(r), in1=a, op0=ALU.mult, op1=ALU.add).then_inc(
                        chain if r < CONV_W - 1 else conv_done, 1)

            split(0, 0)
            dve.wait_ge(raw_head, 1)
            with dve.Fori(0, NJ) as j:
                for y, kind in enumerate(KINDS):
                    t = NK * j + y
                    split(t + 1, (y + 1) % 2)
                    for c in range(NCH):
                        if kind in ("q", "k", "v"):
                            dve.wait_ge(pj_free[c], t + 2)
                            if c == NCH - 1:
                                dve.tensor_copy(conv_tail[:, bass.ds(NJ * y + j, 1), :].rearrange("p a r -> p (a r)"), raw[:, SEQ:SEQ + TAIL]).then_inc(tail_done, 1)
                            conv(j, y, c)
                        if kind in ("wq", "wk"):
                            q = int(kind == "wk")
                            dve.wait_ge(hi_done, 4 * (2 * j + q) + c + 1)
                            dve.wait_ge(lo_stored[c % 2], 16 * (2 * (2 * j + q) + c // 2) + 16)
                            dve.tensor_tensor(lo[:, c % 2, :], pj[c][:], hi[:, c % 2, :].bitcast(F32), ALU.subtract).then_inc(pj_free[c], 1)
                        back, bc = lagged(y, c)
                        if back in POSTED:
                            dve.wait_ge(post_done, POST_CREDIT + posts_before(j, back, bc) + 1)
                        if back in ("q", "k"):
                            dve.tensor_copy(ssq[:, 4 * bc:4 * bc + 4, KINDS.index(back), bass.ds(j, 1)].rearrange("p b a -> p (b a)"),
                                            p_ssq[:, 4 * (bc % 2):4 * (bc % 2) + 4]).then_inc(ssq_read, 1)
                        if back in TURNED:
                            dve.wait_ge(tok_stored[bc % 2], 16 * (2 * (4 * j + TURNED.index(back)) + bc // 2) + 16)
                            dve.tensor_copy(tok[:, bc % 2, :], tp[bc % 2][:]).then_inc(tok_done, 1)
            split(NTILES + 1, 0)
            dve.wait_ge(ab_turned, 1)
            dve.tensor_copy(flat(ab_tok[:, 0:NT, :]), tp[0][:, 0:8 * NT])


LN2, LN3 = 0.6931471805599453, 1.0986122886681098
NEG = -1e30
SCALE = HD ** -0.5
LEVELS = (2, 4, 8, 16, 32, 64)
NEAR_W = 512 + 16 + P
GROUP = 4


def groups(qb):
    return -(-(qb + 1) // GROUP)


GROUPS_BEFORE = [sum(groups(b) for b in range(qb)) for qb in range(NT + 1)]
NG = GROUPS_BEFORE[NT]


def window_table(dve, out, dist, a, b, step):
    n = [0]

    def then(ins):
        n[0] += 1
        ins.then_inc(step, 1)
        dve.wait_ge(step, n[0])

    ai = a.bitcast(I32)
    then(dve.tensor_scalar(ai, dist, 15, None, ALU.bitwise_and))
    then(dve.tensor_scalar(out, ai, 0, None, ALU.is_equal))
    then(dve.tensor_scalar(ai, dist, 3, None, ALU.bitwise_and))
    then(dve.tensor_scalar(a, ai, 0, None, ALU.is_equal))
    then(dve.tensor_scalar(b, dist, 512, None, ALU.is_le))
    then(dve.tensor_tensor(a, a, b, ALU.mult))
    then(dve.tensor_tensor(out, out, a, ALU.add))
    then(dve.tensor_scalar(b, dist, 128, None, ALU.is_le))
    then(dve.tensor_tensor(out, out, b, ALU.add))
    then(dve.tensor_scalar(b, dist, 0, None, ALU.is_ge))
    then(dve.tensor_tensor(out, out, b, ALU.mult))
    then(dve.tensor_scalar(a, out, 2, LN2 / SCALE, ALU.is_ge, ALU.mult))
    then(dve.tensor_scalar(b, out, 3, (LN3 - LN2) / SCALE, ALU.is_ge, ALU.mult))
    then(dve.tensor_tensor(a, a, b, ALU.add))
    then(dve.tensor_scalar(b, out, 1, NEG, ALU.is_lt, ALU.mult))
    then(dve.tensor_tensor(out, a, b, ALU.add))
    return n[0]


def gates(nc, env, D):
    with ExitStack() as ctx:
        sem = env.sem
        sb = lambda n, s, d=F32: ctx.enter_context(nc.sbuf_tensor(n, s, d))
        ps = [ctx.enter_context(nc.psum_tensor(f"gate_ps{i}", [P, CHUNK], F32)) for i in range(8)]
        dist = sb("dist", [P, NEAR_W], I32)
        wa, wb = sb("wa", [P, NEAR_W]), sb("wb", [P, NEAR_W])
        lg, dtb = sb("lg", [P, DN_HEADS]), sb("dtb", [P, DN_HEADS])
        H = DN_HEADS
        x, y, z = (sb(n, [P, NT + 1, H]) for n in ("gx", "gy", "gz"))
        g, beta = sb("gg", [P, NT + 1, H]), sb("gbeta", [P, NT + 1, H])
        gb = sb("gb", [NS, H, DEC_BATCH])
        loaded, dv, ac, pe_s, iota_done, built, wt, st = (sem(n) for n in ("gates_in", "gate_dve", "gate_act", "gate_pe", "iota_done", "tables", "wt", "st"))
        block = ctx.enter_context(nc.Block())
        E = env

        @block.sync
        def _(sp):
            sp.dma_start(lg[:], D.a_log.unsqueeze(0).to_broadcast([P, H])).then_inc(loaded, 16)
            sp.dma_start(dtb[:], D.dt_bias.unsqueeze(0).to_broadcast([P, H])).then_inc(loaded, 16)
            with nc.allow_non_contiguous_dma(reason="one column"):
                sp.dma_start(E.g_dn[:], D.dn_norm_g.unsqueeze(1)).then_inc(loaded, 16)
            for e in range(2):
                load_head_from(sp, D, env, e, e)
                load_chunk_from(sp, D, env, e, e)
            sp.dma_start(E.stc[:], D.state_conv.rearrange("b r c -> (b r) c")).then_inc(E.state_in, 16)
            sp.dma_start(E.st[:], D.state_delta.rearrange("b h k v -> k b h v")).then_inc(E.state_in, 16)

        @block.gpsimd
        def _(pool):
            pool.iota(dist[:], pattern=[[-1, NEAR_W]], base=NEAR_W - P, channel_multiplier=1).then_inc(iota_done, 1)
            n = 0

            def then(ins):
                nonlocal n
                n += 1
                ins.then_inc(built, 1)
                pool.wait_ge(built, n)

            def select(v, op, fill, base, pattern, mult):
                then(pool.affine_select(out=v, in_=v, compare_op=op, fill=fill, base=base, pattern=pattern, channel_multiplier=mult))

            then(pool.memset(E.upto[:], 1.0))
            select(E.upto[:], ALU.is_ge, 0.0, 0, [[1, P]], -1)
            then(pool.memset(E.after[:], 1.0))
            select(E.after[:], ALU.is_gt, 0.0, 0, [[-1, P]], 1)
            T = DEC_SEQ
            for t, u in ((E.s_upto, E.upto), (E.s_after, E.after)):
                then(pool.tensor_copy(t[:], u[0:NS, 0:NS]))
                v = t[:].rearrange("p (b t) -> p b t", t=T)
                select(v, ALU.is_ge, 0.0, 0, [[-T, DEC_BATCH], [0, T]], 1)
                select(v, ALU.is_ge, 0.0, T - 1, [[T, DEC_BATCH], [0, T]], -1)
            then(pool.memset(E.s_own[:], 1.0))
            select(E.s_own[:], ALU.is_ge, 0.0, 0, [[-T, DEC_BATCH]], 1)
            select(E.s_own[:], ALU.is_ge, 0.0, T - 1, [[T, DEC_BATCH]], -1)
            env.n_built = n
            then(pool.memset(E.pair[:], 0.0))
            odd = E.pair[:].rearrange("p (m u) -> p m u", u=2)[:, :, 1]
            select(odd, ALU.not_equal, -1.0, 0, [[-2, P // 2]], 1)
            then(pool.memset(E.below[:], 1.0))
            for l, s in enumerate(LEVELS):
                v = E.below[:, l, :].rearrange("p (m u) -> p m u", u=s)
                m = P // (2 * s)
                select(v, ALU.is_ge, 0.0, -s, [[-2 * s, m], [0, s]], 1)
                select(v, ALU.is_ge, 0.0, 2 * s - 1, [[2 * s, m], [0, s]], -1)

        @block.vector
        def _(dve):
            n = 0

            def then(ins):
                nonlocal n
                n += 1
                ins.then_inc(dv, 1)
                dve.wait_ge(dv, n)
                return n

            bc = lambda a: a.unsqueeze(1).to_broadcast([P, NT, H])
            dve.wait_ge(loaded, 48)
            then(dve.memset(x[:], 0.0))
            then(dve.memset(y[:], 0.0))
            then(dve.tensor_tensor(x[:, 0:NT], E.ab_tok[:, 0:NT, 0:H], bc(dtb[:]), ALU.add))
            then(dve.tensor_tensor(x[0:NS, NT], E.ab_tok[0:NS, NT, 0:H], dtb[0:NS], ALU.add))
            then(dve.tensor_scalar(y[:, 0:NT], E.ab_tok[:, 0:NT, H:2 * H], -1.0, None, ALU.mult))
            then(dve.tensor_scalar(y[0:NS, NT], E.ab_tok[0:NS, NT, H:2 * H], -1.0, None, ALU.mult))
            then(dve.tensor_scalar(z[:], x[:], -1.0, None, ALU.mult))
            then(dve.tensor_tensor(z[:], z[:], x[:], ALU.min))
            env.n1 = n
            dve.wait_ge(ac, 3)
            then(dve.tensor_scalar(z[:], z[:], 1.0, None, ALU.add))
            env.n2 = n
            then(dve.tensor_scalar(y[:], y[:], 1.0, None, ALU.add))
            then(dve.reciprocal(beta[:], y[:]))
            then(dve.tensor_scalar(x[:], x[:], 0.0, None, ALU.max))
            dve.wait_ge(ac, 4)
            then(dve.tensor_tensor(x[:], x[:], z[:], ALU.add))
            then(dve.tensor_scalar(lg[:], lg[:], -1.0, None, ALU.mult))
            then(dve.tensor_tensor(g[:], x[:], lg[:].unsqueeze(1).to_broadcast([P, NT + 1, H]), ALU.mult))
            then(dve.tensor_copy(E.g_tok[:], g[:, 0:NT]))
            then(dve.tensor_copy(E.sg_tok[:], g[0:NS, NT]))
            dve.wait_ge(built, env.n_built)
            then(dve.tensor_tensor(gb[:], g[0:NS, NT].unsqueeze(2).to_broadcast([NS, H, DEC_BATCH]), E.s_own[:].unsqueeze(1).to_broadcast([NS, H, DEC_BATCH]), ALU.mult))
            env.n3 = n
            then(dve.tensor_scalar(E.ssq[:], E.ssq[:], EPS, None, ALU.add))
            then(dve.reciprocal(E.d2[:], E.ssq[:, :, 1, :]))
            then(dve.tensor_tensor(E.d2[:], E.d2[:], beta[:, 0:NT], ALU.mult))
            then(dve.tensor_copy(E.s_beta[:], beta[0:NS, NT]))
            env.n4 = n
            dve.wait_ge(iota_done, 1)
            near = E.win[:, SEQ - NEAR_W:]
            window_table(dve, near, dist[:], wa[:], wb[:], wt)
            far = E.win[:, 0:SEQ - NEAR_W].rearrange("p (m r) -> p m r", r=16)
            dve.tensor_copy(far, near[:, 0:16].unsqueeze(1).to_broadcast([P, (SEQ - NEAR_W) // 16, 16]))
            dve.wait_ge(ac, 8)
            dve.tensor_scalar(E.negc[:], E.egc[:], -1.0, None, ALU.mult)
            dve.wait_ge(st, 2)
            then(dve.reciprocal(E.rq[:], E.rq[:]))
            then(dve.tensor_scalar(E.rq[:], E.rq[:], DK ** -0.5, None, ALU.mult))
            then(dve.tensor_tensor(E.rq2[:], E.rq[:], E.rq[:], ALU.mult))
            then(dve.tensor_scalar(E.rq2[:], E.rq2[:], 1.0 / DK, None, ALU.mult))

        @block.tensor
        def _(pe):
            pe.wait_ge(dv, env.n3)
            gt = E.g_tok[:].rearrange("p n h -> p (n h)")
            N = NT * H
            pe.matmul(ps[0][:, 0:N], E.upto[:], gt, start=True, stop=True)
            pe.matmul(ps[1][:, 0:N], E.ones[:], gt, start=True, stop=True)
            pe.matmul(ps[2][:, 0:N], E.after[:], gt, start=True, stop=True)
            pe.matmul(ps[3][0:NS, 0:H], E.s_upto[:], E.sg_tok[:], start=True, stop=True)
            pe.matmul(ps[4][0:NS, 0:H], E.s_after[:], E.sg_tok[:], start=True, stop=True)
            pe.matmul(ps[5][:, 0:H * DEC_BATCH], E.ones[0:NS, :], gb[:].rearrange("p h b -> p (h b)"), start=True, stop=True).then_inc(pe_s, 1)

        @block.scalar
        def _(act):
            act.wait_ge(dv, env.n1)
            act.activation(z[:], z[:], ACT.Exp).then_inc(ac, 1)
            act.activation(y[:], y[:], ACT.Exp).then_inc(ac, 1)
            act.activation(lg[:], lg[:], ACT.Exp).then_inc(ac, 1)
            act.wait_ge(dv, env.n2)
            act.activation(z[:], z[:], ACT.Ln).then_inc(ac, 1)
            act.wait_ge(pe_s, 1)
            N = NT * H
            fl = lambda a: a[:].rearrange("p n h -> p (n h)")
            act.activation(fl(E.egc), ps[0][:, 0:N], ACT.Exp).then_inc(ac, 1)
            act.activation(fl(E.gl), ps[1][:, 0:N], ACT.Exp).then_inc(ac, 1)
            act.activation(fl(E.dl), ps[2][:, 0:N], ACT.Exp).then_inc(ac, 1)
            act.activation(E.s_egc[:], ps[3][0:NS, 0:H], ACT.Exp).then_inc(ac, 1)
            act.activation(E.s_dl[:], ps[4][0:NS, 0:H], ACT.Exp).then_inc(ac, 1)
            act.activation(E.s_gl[:].rearrange("p h b -> p (h b)"), ps[5][:, 0:H * DEC_BATCH], ACT.Exp).then_inc(ac, 1)
            act.wait_ge(dv, env.n4)
            act.activation(E.rinv[:], E.ssq[:, :, 1, :], ACT.Sqrt).then_inc(st, 1)
            act.activation(E.rq[:], E.ssq[:, :, 0, :], ACT.Sqrt).then_inc(st, 1)


def gate_tensors(nc, env, ctx):
    sb = lambda n, s, d=F32: ctx.enter_context(nc.sbuf_tensor(n, s, d))
    H = DN_HEADS
    env.g_dn = sb("g_dn", [P, 1])
    env.upto, env.after, env.pair = (sb(n, [P, P]) for n in ("upto", "after", "pair"))
    env.below = sb("below", [P, len(LEVELS), P // 2])
    env.s_upto, env.s_after = sb("s_upto", [NS, NS]), sb("s_after", [NS, NS])
    env.s_own = sb("s_own", [NS, DEC_BATCH])
    env.g_tok, env.d2, env.rinv, env.rq, env.rq2, env.egc, env.negc, env.dl, env.gl = (
        sb(n, [P, NT, H]) for n in ("g_tok", "d2", "rinv", "rq", "rq2", "egc", "negc", "dl", "gl"))
    env.sg_tok, env.s_beta, env.s_egc, env.s_dl = (sb(n, [NS, H]) for n in ("sg_tok", "s_beta", "s_egc", "s_dl"))
    env.s_gl = sb("s_gl", [P, H, DEC_BATCH])
    env.win = sb("win", [P, SEQ])
    env.stc = sb("stc", [DEC_BATCH * TAIL, CONV_CH])
    env.st = sb("st", [P, DEC_BATCH, H, P])
    env.state_in = nc.alloc_semaphore(name="state_in")
    env.mix_s = sb("mix_s", [P, D_MODEL // P, NS])


LAG = 1


def head_order():
    order = [("score", 0, 0), ("max", 0), ("score", 1, 0), ("max", 1), ("exp", 0, 0)]
    seq = [(qb, g) for qb in range(NT) for g in range(groups(qb))]

    def share(step, q, g, last):
        n = groups(q) if q < NT else 0
        order.extend((step, q, x) for x in (range(g, n) if last else range(g, min(g + 1, n))))

    for k in range(len(seq) + LAG):
        if k < len(seq):
            qb, g = seq[k]
            last = g == groups(qb) - 1
            order.append(("turn", qb, g))
            share("exp", qb + 1, g, last)
            share("score", qb + 2, g, last)
            if last and qb + 2 < NT:
                order.append(("max", qb + 2))
        if k >= LAG:
            qb, g = seq[k - LAG]
            order.append(("mix", qb, g))
            if g == 0 and qb:
                order.append(("norm", qb - 1))
            if g == min(1, groups(qb) - 1) and qb:
                order.append(("flip", qb - 1))
    order += [("norm", NT - 1), ("flip", NT - 1)]
    ungated, ordered = [], []
    for step in order:
        ordered.append(step)
        if step[0] in ("turn", "flip"):
            ordered += [("gate", qb) for qb in ungated]
            ungated = [step[1]] if step[0] == "flip" else []
    order = ordered + [("gate", qb) for qb in ungated]
    cost = [{"score": 8, "turn": 8, "mix": 16}.get(step, 0) * min(GROUP, a[0] + 1 - GROUP * a[-1]) // 4 for step, *a in order]
    delta = [("delta", s, e) for e in range(2) for s in DELTA_STEPS]
    woven, spent, given = [], 0, 0
    for step, c in zip(order, cost):
        woven.append(step)
        spent += c
        upto = len(delta) * spent // sum(cost)
        woven += delta[given:upto]
        given = upto
    return woven


DELTA_STEPS = (["decay", "kq", "pairs", "rest", "pairs_t"] + [x + str(l) for l in range(len(LEVELS)) for x in ("cross", "double")]
               + ["state", "solve", "update", "rest", "rest", "rest", "turn_o"])
BODY = [(e,) + step for e in range(2) for step in head_order()]
TURNS = [step for step in head_order() if step[0] in ("turn", "flip")]


def turned_bank(step):
    k = TURNS.index(step)
    before = TURNS[k - 2]
    number = GROUPS_BEFORE[before[1]] + before[2] if before[0] == "turn" else before[1]
    return k % 2, before[0], number, k < 2


def mixer_operands(nc, env, ctx):
    sb = lambda n, s, d=F32: ctx.enter_context(nc.sbuf_tensor(n, s, d))
    H = DN_HEADS
    qs = [sb(f"qs{e}", [P, SEQ], F32R) for e in range(2)]
    kh = [sb(f"kh{e}", [P, SEQ], F32R) for e in range(2)]
    kl = [sb(f"kl{e}", [P, SEQ], F32R) for e in range(2)]
    vt = [sb(f"vt{e}", [P, NT, HD]) for e in range(2)]
    zb = [sb(f"zb{e}", [HD, SEQ]) for e in range(2)]
    kq = [sb(f"kq{e}", [P, H, 2, P]) for e in range(2)]
    ktok = [sb(f"ktok{e}", [P, H, P]) for e in range(2)]
    vtok = [sb(f"vtok{e}", [P, H, P]) for e in range(2)]
    za = [sb(f"za{e}", [P, H, P]) for e in range(2)]
    env.operands = qs, kh, kl, vt, zb, kq, ktok, vtok, za
    env.head_in, env.chunk_in = ([nc.alloc_semaphore(name=f"{n}{e}") for e in range(2)] for n in ("head_in", "chunk_in"))


HEAD_DMAS, CHUNK_DMAS = 8, 5


def load_head_from(sp, D, env, h, e):
    qs, kh, kl, vt, zb = env.operands[0:5]
    head_in = env.head_in
    r = bass.ds(HD * h, HD)
    for half_, part in ((0, 0), (1, 1)):
        sp.dma_start(qs[e][HD * half_:HD * half_ + HD, :].bitcast(F32), D.wqk[0, part, r, :]).then_inc(head_in[e], 16)
    for half_ in range(2):
        sp.dma_start(kh[e][HD * half_:HD * half_ + HD, :].bitcast(F32), D.wqk[1, 0, r, :]).then_inc(head_in[e], 16)
        sp.dma_start(kl[e][HD * half_:HD * half_ + HD, :].bitcast(F32), D.wqk[1, 1, r, :]).then_inc(head_in[e], 16)
    sp.dma_start(vt[e][:], D.new_v[:, r].rearrange("(n p) d -> p n d", p=P)).then_inc(head_in[e], 16)
    sp.dma_start(zb[e][:], D.z_ch[1, r, :]).then_inc(head_in[e], 16)


def load_chunk_from(sp, D, env, c, e):
    kq, ktok, vtok, za = env.operands[5:]
    chunk_in = env.chunk_in
    t = bass.ds(P * c, P)
    for half_, y in ((0, 1), (1, 0)):
        sp.dma_start(kq[e][:, :, half_, :], D.qk_ch[y, :, t].rearrange("(h p) t -> p h t", p=P)).then_inc(chunk_in[e], 16)
    sp.dma_start(flat(ktok[e][:]), D.k_tok[t, :]).then_inc(chunk_in[e], 16)
    sp.dma_start(flat(vtok[e][:]), D.v_tok[t, :]).then_inc(chunk_in[e], 16)
    sp.dma_start(za[e][:], D.z_ch[0, :, t].rearrange("(h p) t -> p h t", p=P)).then_inc(chunk_in[e], 16)


def mixers(nc, env, D):
    with ExitStack() as ctx:
        sem = env.sem
        sb = lambda n, s, d=F32: ctx.enter_context(nc.sbuf_tensor(n, s, d))
        ps = lambda n: ctx.enter_context(nc.psum_tensor(n, [P, CHUNK], F32))
        E, H, ident = env, DN_HEADS, env.ident
        qs, kh, kl, vt, zb, kq, ktok, vtok, za = env.operands
        head_in, chunk_in = env.head_in, env.chunk_in
        sc = sb("sc", [P, 2, SEQ])
        pt = sb("pt", [P, 4, CHUNK])
        segmax, nmax, lsum, lall, linv = sb("segmax", [P, 2, 4]), sb("nmax", [P, 2]), sb("lsum", [P, 4, 4]), sb("lall", [P, 4]), sb("linv", [P, 4])
        ob = sb("ob", [P, 2, HD])
        names = "gm dec nt attn tt tl rr y1 vd o1 oo state sg px"
        gm, dec, nt, attn, tt, tl, rr, y1, vd, o1, oo, state, sg, px = (sb("d_" + n, [P, H, P]) for n in names.split())
        cross = sb("cross", [P, len(LEVELS), H, P])
        oss, ors = sb("oss", [P, H]), sb("ors", [P, H])
        half = sb("halves", [P, H])
        s_ps, pt_ps, o_ps, d_ps = ([ps(f"{n}{i}") for i in range(2)] for n in ("s_ps", "pt_ps", "o_ps", "d_ps"))

        S = {n: sem("m_" + n) for n in (
            "scores masked max exped turned turned_out mixed o_scaled o_turned o_gated linv summed "
            "seen gm_built decay_mm decay_exp decay_masked kq_mm nt_made attn_made px_made tt_made pairs_mm tl_made "
            "cross_mm cross_made double_mm tl_doubled tt_doubled "
            "ks_mm rr_made o1_made solve_mm y1_made vd_made sg_made "
            "av_mm su_mm oo_made state_made oss_made ors_a ors_b oo_scaled oT_mm gated_a v_scaled zeroed").split()}
        head_stored = [sem(f"head_stored{e}") for e in range(2)]
        chunk_stored = [sem(f"chunk_stored{e}") for e in range(2)]
        delta_stored = sem("delta_stored")
        O_CREDIT, S_CREDIT, PT_CREDIT = 2, 2, 4
        block = ctx.enter_context(nc.Block())
        L = len(LEVELS)

        @block.sync
        def _(sp):
            load_head = lambda h, e: load_head_from(sp, D, env, h, e)
            load_chunk = lambda c, e: load_chunk_from(sp, D, env, c, e)

            def store(i, e, load):
                h = 2 * i + e
                for u in range(2):
                    c = 2 * h + u
                    sp.wait_ge(S["gated_a"], c + 2)
                    sp.sem_inc(S["seen"], 1)
                    sp.dma_start(D.mix[0:QK_W, bass.ds(P * c, P)].rearrange("(h p) t -> p h t", p=P), za[u][:]).then_inc(chunk_stored[u], 16)
                    if load or e == 0:
                        sp.wait_ge(chunk_stored[u], 16 * h + 16)
                        load_chunk(c + 2, u)
                sp.wait_ge(S["o_gated"], NT + NT * (h + 1))
                sp.sem_inc(S["seen"], 1)
                sp.dma_start(D.mix[bass.ds(HD * h + QK_W, HD), :], zb[e][:]).then_inc(head_stored[e], 16)
                if load:
                    sp.wait_ge(head_stored[e], 16 * i + 16)
                    load_head(h + 2, e)

            with sp.Fori(0, SW_HEADS // 2 - 1) as i:
                for e in range(2):
                    store(i, e, True)
            for e in range(2):
                store(SW_HEADS // 2 - 1, e, False)
            sp.wait_ge(S["state_made"], NT + 1)
            sp.dma_start(D.new_delta.rearrange("h k v -> k h v"), state[:]).then_inc(delta_stored, 16)
            sp.wait_ge(delta_stored, 16)
            for e in range(2):
                sp.wait_ge(head_stored[e], 16 * SW_HEADS // 2)
                sp.wait_ge(chunk_stored[e], 16 * NT // 2)

        def blocks(ap, l, odd):
            return ap.rearrange("p h (m two u) -> p h m two u", two=2, u=LEVELS[l])[:, :, :, odd, :]

        def compact(ap, l):
            return ap.rearrange("p (h m u) -> p h m u", h=H, u=LEVELS[l])

        def row(t, c):
            return t[:, bass.ds(c, 1), :].rearrange("p a h -> p (a h)").unsqueeze(2).to_broadcast([P, H, P])

        def col(t, c, h):
            return t[:, bass.ds(c, 1), h]

        def heads(t):
            return t[:].unsqueeze(1).to_broadcast([P, H, P])

        def by_head(t):
            return t[:].rearrange("p (h t) -> p h t", h=H)

        @block.gpsimd
        def _(pool):
            pool.memset(state[:], 0.0).then_inc(S["state_made"], 1)
            pool.memset(cross[:], 0.0).then_inc(S["zeroed"], 1)
            pool.memset(half[:], -0.5).then_inc(S["zeroed"], 1)
            for n in "gm_built decay_masked px_made tt_made v_scaled sg_made vd_made oo_scaled ors_b".split():
                pool.sem_inc(S[n], 1)
            pool.wait_ge(S["zeroed"], 2)

            def delta(c, u, step):
                if step == "decay":
                    pool.wait_ge(S["decay_mm"], c + 1)
                    pool.tensor_tensor(gm[:], heads(E.upto), row(E.g_tok, c), ALU.mult).then_inc(S["gm_built"], 1)
                    pool.wait_ge(S["decay_exp"], c + 2)
                    pool.tensor_tensor(dec[:], dec[:], heads(E.upto), ALU.mult).then_inc(S["decay_masked"], 1)
                elif step == "kq":
                    pool.wait_ge(chunk_in[u], 8 * CHUNK_DMAS * (c - u) + 16 * CHUNK_DMAS)
                    pool.tensor_tensor(vtok[u][:], vtok[u][:], row(E.rinv, c), ALU.mult).then_inc(S["v_scaled"], 1)
                elif step == "pairs":
                    pool.wait_ge(S["nt_made"], c + 2)
                    pool.tensor_tensor(px[:], nt[:], heads(E.pair), ALU.mult).then_inc(S["px_made"], 1)
                    pool.wait_ge(S["px_made"], c + 2)
                    pool.wait_ge(S["solve_mm"], c + 1)
                    pool.tensor_tensor(tt[:], px[:], heads(ident), ALU.add).then_inc(S["tt_made"], 1)
                elif step == "state":
                    pool.wait_ge(S["state_made"], c + 1)
                    pool.tensor_tensor(sg[:], state[:], row(E.gl, c), ALU.mult).then_inc(S["sg_made"], 1)
                elif step == "solve":
                    pool.wait_ge(S["y1_made"], c + 2)
                    pool.wait_ge(S["su_mm"], c + 1)
                    pool.tensor_tensor(vd[:], y1[:], row(E.dl, c), ALU.mult).then_inc(S["vd_made"], 1)
                elif step == "update":
                    r = lambda t: t[:, bass.ds(c, 1), :].rearrange("p a h -> p (a h)")
                    pool.wait_ge(S["oss_made"], c + 2)
                    pool.tensor_tensor(ors[:], oss[:], r(E.rq2), ALU.mult).then_inc(S["ors_a"], 1)
                    pool.wait_ge(S["ors_a"], 3 * c + 1)
                    pool.sem_inc(S["seen"], 1)
                    pool.tensor_scalar(ors[:], ors[:], EPS, None, ALU.add).then_inc(S["ors_a"], 1)
                    pool.wait_ge(S["ors_a"], 3 * c + 2)
                    pool.tensor_tensor(ors[:], ors[:], half[:], ALU.pow).then_inc(S["ors_a"], 1)
                    pool.wait_ge(S["ors_a"], 3 * c + 3)
                    pool.tensor_tensor(ors[:], ors[:], r(E.rq), ALU.mult).then_inc(S["ors_b"], 1)
                    pool.wait_ge(S["ors_b"], c + 2)
                    pool.tensor_tensor(oo[:], oo[:], ors[:].unsqueeze(2).to_broadcast([P, H, P]), ALU.mult).then_inc(S["oo_scaled"], 1)

            with pool.Fori(0, SW_HEADS // 2) as i:
                for e, step, *a in BODY:
                    if step == "delta":
                        name, u = a
                        delta(4 * i + 2 * e + u, u, name)

        @block.tensor
        def _(pe):
            pe.sem_inc(S["turned"], NG)
            pe.sem_inc(S["o_turned"], O_CREDIT)
            pe.sem_inc(S["mixed"], PT_CREDIT)
            for n in "decay_mm solve_mm su_mm av_mm oT_mm pairs_mm".split():
                pe.sem_inc(S[n], 1)

            def delta(c, u, step):
                if step == "decay":
                    pe.wait_ge(S["gm_built"], c + 2)
                    pe.wait_ge(S["gated_a"], c + 1)
                    pe.matmul(d_ps[0][:], E.after[:], flat(gm[:]), start=True, stop=True).then_inc(S["decay_mm"], 1)
                elif step == "kq":
                    pe.wait_ge(chunk_in[u], 8 * CHUNK_DMAS * (c - u) + 16 * CHUNK_DMAS)
                    for b in range(2):
                        if b == 0:
                            pe.wait_ge(S["state_made"], c + 1)
                        else:
                            pe.wait_ge(S["decay_exp"], c + 2)
                        for h in (2 * b, 2 * b + 1):
                            mm = pe.matmul(d_ps[1 - b][:, 256 * (h % 2):256 * (h % 2) + 256], kq[u][:, h, 0, :], flat(kq[u][:, h, :, :]), start=True, stop=True)
                        mm.then_inc(S["kq_mm"], 1)
                elif step == "pairs_t":
                    pe.wait_ge(S["tt_made"], c + 2)
                    pe.wait_ge(S["attn_made"], c + 2)
                    for h in range(H):
                        mm = pe.transpose(d_ps[0][:, P * h:P * h + P], tt[:, h, :], ident[:])
                    mm.then_inc(S["pairs_mm"], 1)
                elif step.startswith("cross"):
                    l = int(step[5:])
                    if l == 0:
                        pe.wait_ge(S["tl_made"], c + 2)
                    else:
                        pe.wait_ge(S["tl_doubled"], (L - 1) * c + l)
                    for h in range(H):
                        mm = pe.matmul(d_ps[1][:, 64 * h:64 * h + 64], nt[:, h, :], blocks(tl[:], l, 0)[:, h], start=True, stop=True)
                    mm.then_inc(S["cross_mm"], 1)
                elif step.startswith("double"):
                    l = int(step[6:])
                    pe.wait_ge(S["cross_made"], L * c + l + 1)
                    if l:
                        pe.wait_ge(S["tt_doubled"], L * c + l)
                    for h in range(H):
                        x = cross[:, l, :, :]
                        if l < L - 1:
                            pe.matmul(d_ps[0][:, 64 * h:64 * h + 64], tt[:, h, :], blocks(x, l, 0)[:, h], start=True, stop=True)
                        mm = pe.matmul(d_ps[0][:, 256 + 64 * h:256 + 64 * h + 64], x[:, h, :], blocks(tt[:], l, 1)[:, h], start=True, stop=True)
                    mm.then_inc(S["double_mm"], 1)
                elif step == "state":
                    pe.wait_ge(S["state_made"], c + 1)
                    for h in range(H):
                        mm = pe.matmul(d_ps[1][:, P * h:P * h + P], kq[u][:, h, 0, :], state[:, h, :], start=True, stop=True)
                    mm.then_inc(S["ks_mm"], 1)
                    pe.wait_ge(S["tt_doubled"], L * c + L)
                    for h in range(H):
                        mm = pe.matmul(d_ps[0][:, P * h:P * h + P], kq[u][:, h, 1, :], state[:, h, :], start=True, stop=True)
                    mm.then_inc(S["ks_mm"], 1)
                elif step == "solve":
                    pe.wait_ge(S["rr_made"], c + 2)
                    for h in range(H):
                        mm = pe.matmul(d_ps[1][:, P * h:P * h + P], tt[:, h, :], rr[:, h, :], start=True, stop=True)
                    mm.then_inc(S["solve_mm"], 1)
                elif step == "update":
                    pe.wait_ge(S["y1_made"], c + 2)
                    pe.wait_ge(S["o1_made"], c + 2)
                    for h in range(H):
                        mm = pe.matmul(d_ps[0][:, P * h:P * h + P], attn[:, h, :], y1[:, h, :], start=True, stop=True)
                    mm.then_inc(S["av_mm"], 1)
                    pe.wait_ge(S["vd_made"], c + 2)
                    for h in range(H):
                        mm = pe.matmul(d_ps[1][:, P * h:P * h + P], ktok[u][:, h, :], vd[:, h, :], start=True, stop=True)
                    mm.then_inc(S["su_mm"], 1)
                elif step == "turn_o":
                    pe.wait_ge(S["oo_scaled"], c + 2)
                    for h in range(H):
                        mm = pe.transpose(d_ps[0][:, P * h:P * h + P], oo[:, h, :], ident[:])
                    mm.then_inc(S["oT_mm"], 1)

            with pe.Fori(0, SW_HEADS // 2) as i:
                for e, step, *a in BODY:
                    hh = 2 * i + e
                    if step == "delta":
                        name, u = a
                        delta(4 * i + 2 * e + u, u, name)
                        continue
                    qb = a[0]
                    if step == "score":
                        g = a[1]
                        if qb == 0:
                            pe.wait_ge(head_in[e], 16 * HEAD_DMAS * (i + 1))
                        n = GROUPS_BEFORE[qb] + g
                        w = P * min(GROUP, qb + 1 - GROUP * g)
                        pe.wait_ge(S["masked"], NG * hh + n + 1)
                        q, ks = qs[e][:, P * qb:P * qb + P], slice(CHUNK * g, CHUNK * g + w)
                        pe.matmul(s_ps[n % 2][:, 0:w], q, kh[e][:, ks], start=True, stop=False)
                        pe.matmul(s_ps[n % 2][:, 0:w], q, kl[e][:, ks], start=False, stop=True).then_inc(S["scores"], 1)
                    elif step in ("turn", "flip"):
                        s, kind, number, earlier = turned_bank((step, qb, *a[1:]))
                        if kind == "turn":
                            pe.wait_ge(S["turned_out"], NG * hh + (NG * (1 - earlier) + number + 1))
                        else:
                            pe.wait_ge(S["o_gated"], NT * hh + (NT * (1 - earlier) + number + 1))
                        if step == "flip":
                            pe.wait_ge(S["o_scaled"], O_CREDIT + NT * hh + qb + 1)
                            pe.sem_inc(S["seen"], 1)
                            pe.transpose(pt_ps[s][0:HD, 0:P], ob[:, qb % 2, :], ident[:]).then_inc(S["o_turned"], 1)
                            continue
                        n = GROUPS_BEFORE[qb] + a[1]
                        pe.wait_ge(S["exped"], NG * hh + n + 1)
                        for b in range(GROUP * a[1], min(GROUP * a[1] + GROUP, qb + 1)):
                            mm = pe.transpose(pt_ps[s][:, P * (b % GROUP):P * (b % GROUP) + P], sc[:, qb % 2, P * b:P * b + P], ident[:])
                        mm.then_inc(S["turned"], 1)
                    elif step == "mix":
                        n = GROUPS_BEFORE[qb] + a[1]
                        pe.wait_ge(S["turned_out"], NG * hh + (NG + n + 1))
                        if a[1] == 0:
                            pe.wait_ge(S["o_scaled"], NT * hh + qb + 1)
                        for b in range(GROUP * a[1], min(GROUP * a[1] + GROUP, qb + 1)):
                            mm = pe.matmul(o_ps[qb % 2][:, 0:HD], pt[:, n % 4, P * (b % GROUP):P * (b % GROUP) + P], vt[e][:, b, :], start=(b == 0), stop=(b == qb))
                        mm.then_inc(S["mixed"], 1)

        @block.scalar
        def _(act):
            act.sem_inc(S["turned_out"], NG)
            for n in "decay_exp tl_made o1_made oss_made".split():
                act.sem_inc(S[n], 1)

            def delta(c, u, step):
                if step == "decay":
                    act.wait_ge(S["decay_mm"], c + 2)
                    act.wait_ge(S["attn_made"], c + 1)
                    act.activation(flat(dec[:]), d_ps[0][:], ACT.Exp).then_inc(S["decay_exp"], 1)
                elif step == "pairs_t":
                    act.wait_ge(S["pairs_mm"], c + 2)
                    act.activation(flat(tl[:]), d_ps[0][:], ACT.Copy).then_inc(S["tl_made"], 1)
                elif step == "state":
                    act.wait_ge(S["ks_mm"], 2 * c + 2)
                    act.wait_ge(S["ors_b"], c + 1)
                    for h in range(H):
                        ins = act.activation(o1[:, h, :], d_ps[0][:, P * h:P * h + P], ACT.Copy, scale=col(E.egc, c, h))
                    ins.then_inc(S["o1_made"], 1)
                elif step == "update":
                    act.wait_ge(S["oo_made"], c + 2)
                    for h in range(H):
                        ins = act.activation(o1[:, h, :], oo[:, h, :], ACT.Square, accum_out=oss[:, h:h + 1])
                    ins.then_inc(S["oss_made"], 1)

            with act.Fori(0, SW_HEADS // 2) as i:
                for e, step, *a in BODY:
                    hh = 2 * i + e
                    if step == "delta":
                        name, u = a
                        delta(4 * i + 2 * e + u, u, name)
                        continue
                    qb = a[0]
                    if step == "exp":
                        g = a[1]
                        if g == 0:
                            act.wait_ge(S["max"], NT * hh + qb + 1)
                            act.wait_ge(S["linv"], NT * hh + qb + 1)
                        x = sc[:, qb % 2, CHUNK * g:P * min(GROUP * g + GROUP, qb + 1)]
                        act.activation(x, x, ACT.Exp, bias=nmax[:, qb % 2:qb % 2 + 1], accum_out=lsum[:, qb % 4, g:g + 1]).then_inc(S["exped"], 1)
                    elif step == "turn":
                        n = GROUPS_BEFORE[qb] + a[1]
                        w = P * min(GROUP, qb + 1 - GROUP * a[1])
                        act.wait_ge(S["turned"], NG * hh + NG + n + 1)
                        act.wait_ge(S["mixed"], NG * hh + n + 1)
                        act.activation(pt[:, n % 4, 0:w], pt_ps[turned_bank((step, qb, *a[1:]))[0]][:, 0:w], ACT.Copy).then_inc(S["turned_out"], 1)

        @block.vector
        def _(dve):
            dve.sem_inc(S["masked"], S_CREDIT)
            dve.sem_inc(S["linv"], PT_CREDIT)
            dve.sem_inc(S["o_gated"], NT)
            dve.sem_inc(S["o_scaled"], O_CREDIT)
            for n in "nt_made attn_made rr_made y1_made oo_made gated_a".split():
                dve.sem_inc(S[n], 1)
            dve.wait_ge(S["zeroed"], 1)

            def delta(c, u, step):
                if step == "kq":
                    dve.wait_ge(S["decay_masked"], c + 2)
                    for b in range(2):
                        dve.wait_ge(S["kq_mm"], 2 * c + b + 1)
                        t = d_ps[1 - b][:].rearrange("p (h x t) -> p h x t", h=2, x=2)
                        for h in (2 * b, 2 * b + 1):
                            ins = dve.scalar_tensor_tensor(out=nt[:, h, :], in0=t[:, h % 2, 0], scalar=col(E.d2, c, h), in1=dec[:, h, :], op0=ALU.mult, op1=ALU.mult)
                        if b == 1:
                            ins.then_inc(S["nt_made"], 1)
                        ins = dve.tensor_tensor(attn[:, 2 * b:2 * b + 2, :], t[:, :, 1], dec[:, 2 * b:2 * b + 2, :], ALU.mult)
                    ins.then_inc(S["attn_made"], 1)
                elif step.startswith("cross"):
                    l = int(step[5:])
                    dve.wait_ge(S["cross_mm"], L * c + l + 1)
                    m = E.below[:, l, :].rearrange("p (m u) -> p m u", u=LEVELS[l])
                    m = m.unsqueeze(1).to_broadcast([P, H, P // (2 * LEVELS[l]), LEVELS[l]])
                    dve.tensor_tensor(blocks(cross[:, l], l, 0), compact(d_ps[1][:, 0:256], l), m, ALU.mult).then_inc(S["cross_made"], 1)
                elif step.startswith("double"):
                    l = int(step[6:])
                    dve.wait_ge(S["double_mm"], L * c + l + 1)
                    if l < L - 1:
                        t = blocks(tl[:], l, 0)
                        dve.tensor_tensor(t, t, compact(d_ps[0][:, 0:256], l), ALU.subtract).then_inc(S["tl_doubled"], 1)
                    t = blocks(tt[:], l, 1)
                    dve.tensor_tensor(t, t, compact(d_ps[0][:, 256:512], l), ALU.subtract).then_inc(S["tt_doubled"], 1)
                elif step == "state":
                    dve.wait_ge(S["v_scaled"], c + 2)
                    dve.wait_ge(S["ks_mm"], 2 * c + 1)
                    for h in range(H):
                        ins = dve.scalar_tensor_tensor(out=rr[:, h, :], in0=d_ps[1][:, P * h:P * h + P], scalar=col(E.negc, c, h), in1=vtok[u][:, h, :], op0=ALU.mult, op1=ALU.add)
                    ins.then_inc(S["rr_made"], 1)
                elif step == "solve":
                    dve.wait_ge(S["solve_mm"], c + 2)
                    dve.wait_ge(S["vd_made"], c + 1)
                    dve.tensor_tensor(y1[:], by_head(d_ps[1]), row(E.d2, c), ALU.mult).then_inc(S["y1_made"], 1)
                elif step == "update":
                    dve.wait_ge(S["av_mm"], c + 2)
                    dve.wait_ge(S["o1_made"], c + 2)
                    dve.tensor_tensor(oo[:], by_head(d_ps[0]), o1[:], ALU.add).then_inc(S["oo_made"], 1)
                    dve.wait_ge(S["su_mm"], c + 2)
                    dve.wait_ge(S["sg_made"], c + 2)
                    dve.tensor_tensor(state[:], by_head(d_ps[1]), sg[:], ALU.add).then_inc(S["state_made"], 1)
                elif step == "turn_o":
                    dve.wait_ge(S["oT_mm"], c + 2)
                    dve.scalar_tensor_tensor(out=za[u][:], in0=by_head(d_ps[0]), scalar=E.g_dn[:, 0:1], in1=za[u][:], op0=ALU.mult, op1=ALU.mult).then_inc(S["gated_a"], 1)

            with dve.Fori(0, SW_HEADS // 2) as i:
                for e, step, *a in BODY:
                    hh = 2 * i + e
                    if step == "delta":
                        name, u = a
                        delta(4 * i + 2 * e + u, u, name)
                        continue
                    qb = a[0]
                    s, l = qb % 2, qb % 4
                    if step == "score":
                        g = a[1]
                        before = NG + GROUPS_BEFORE[qb - 2] + min(g, groups(qb - 2) - 1) + 1 if qb >= 2 else GROUPS_BEFORE[NT - 1 + qb]
                        n = GROUPS_BEFORE[qb] + g
                        w = P * min(GROUP, qb + 1 - GROUP * g)
                        at = P * (NT - 1 - qb) + CHUNK * g
                        dve.wait_ge(S["turned"], NG * hh + before)
                        dve.wait_ge(S["scores"], NG * hh + n + 1)
                        dve.sem_inc(S["seen"], 1)
                        dve.tensor_tensor_reduce(sc[:, s, CHUNK * g:CHUNK * g + w], s_ps[n % 2][:, 0:w], E.win[:, at:at + w], SCALE, -3.0e38,
                                                 ALU.add, ALU.max, segmax[:, s, g:g + 1]).then_inc(S["masked"], 1)
                    elif step == "max":
                        dve.wait_ge(S["masked"], S_CREDIT + NG * hh + GROUPS_BEFORE[qb + 1])
                        dve.tensor_reduce(nmax[:, s:s + 1], segmax[:, s, 0:groups(qb)], AX.X, ALU.max, negate=True).then_inc(S["max"], 1)
                    elif step == "norm":
                        dve.wait_ge(S["exped"], NG * hh + GROUPS_BEFORE[qb + 1])
                        dve.tensor_reduce(lall[:, l:l + 1], lsum[:, l, 0:groups(qb)], AX.X, ALU.add).then_inc(S["summed"], 1)
                        dve.wait_ge(S["summed"], NT * hh + qb + 1)
                        dve.reciprocal(linv[:, l:l + 1], lall[:, l:l + 1]).then_inc(S["linv"], 1)
                        dve.wait_ge(S["linv"], PT_CREDIT + NT * hh + qb + 1)
                        dve.wait_ge(S["mixed"], PT_CREDIT + NG * hh + GROUPS_BEFORE[qb + 1])
                        dve.wait_ge(S["o_turned"], NT * hh + qb + 1)
                        dve.tensor_scalar(ob[:, s, :], o_ps[s][:, 0:HD], linv[:, l:l + 1], None, ALU.mult).then_inc(S["o_scaled"], 1)
                    elif step == "gate":
                        if qb == 0:
                            dve.wait_ge(head_in[e], 16 * HEAD_DMAS * (i + 1))
                        dve.wait_ge(S["o_turned"], O_CREDIT + NT * hh + qb + 1)
                        z = zb[e][:, P * qb:P * qb + P]
                        dve.tensor_tensor(z, pt_ps[turned_bank(("flip", qb))[0]][0:HD, 0:P], z, ALU.mult).then_inc(S["o_gated"], 1)


H = DN_HEADS
T = DEC_SEQ
ROWS = SW_HEADS * T
NEAR = 512
FAR = (PAST - NEAR) // 16
FARS = T * FAR
KEYS = NEAR + FARS + T


def tail_tensors(nc, env, ctx):
    sb = lambda n, s, d=F32: ctx.enter_context(nc.sbuf_tensor(n, s, d))
    env.wo_hi, env.wo_lo = (sb(n, [P, KT, D_MODEL], F32R) for n in ("wo_hi", "wo_lo"))
    env.tab = sb("s_tab", [ROWS, KEYS])
    env.kn, env.kf = sb("kn", [P, T, SW_WIDTH]), sb("kf", [FAR, T, SW_WIDTH])
    env.mx = sb("mx", [P, 2, KT, P])
    env.k_in, env.m_in = nc.alloc_semaphore(name="a_k_in"), [nc.alloc_semaphore(name=f"y_m_in{u}") for u in range(2)]


def load_rows(sp, cache, b, near, far, into):
    one = bass.ds(b, 1)
    sp.dma_start(near[:], cache[one, PAST - NEAR:PAST, :].rearrange("a (p t) c -> (a p) t c", t=T)).then_inc(into, 16)
    reach = cache[one, 0:PAST - NEAR, :].rearrange("a (m r) c -> (a m) r c", r=16)[:, 0:T, :]
    sp.dma_start(far[:], reach).then_inc(into, 16)


def load_mix(sp, D, env, n, u):
    sp.dma_start(env.mx[:, u], D.mix[:, bass.ds(P * n, P)].rearrange("(k p) t -> p k t", p=P)).then_inc(env.m_in[u], 16)


def sample(nc, env, D):
    with ExitStack() as ctx:
        sem = env.sem
        sb = lambda n, s, d=F32: ctx.enter_context(nc.sbuf_tensor(n, s, d))
        bank = [ctx.enter_context(nc.psum_tensor(f"s_bank{i}", [P, CHUNK], F32)) for i in range(8)]
        E, ident, sam = env, env.ident, env.sam
        ext = sb("ext", [P, 3 * NJ, DEC_BATCH, TAIL + T])
        cacc, ctmp = (sb(n, [P, 3 * NJ, DEC_BATCH, T]) for n in ("cacc", "ctmp"))
        raw_tok = sb("raw_tok", [NS, CONV_CH])
        kv_tok = sb("kv_tok", [NS, 2, SW_WIDTH])
        skq, svc = sb("skq", [P, 2, H, NS]), sb("svc", [P, H, NS])
        ssq2 = sb("ssq2", [P, 2, H, NS])
        ssum = sb("ssum", [NS, 2, H])
        sd2, srinv, srq, srq2, soss, sors, shalf = (sb(n, [NS, H]) for n in ("sd2", "srinv", "srq", "srq2", "soss", "sors", "shalf"))
        x2 = sb("x2", [NS, NS])
        sgm, sdec, snt, sattn, stt, stl, sx, sz = (sb(n, [NS, H, NS]) for n in ("sgm", "sdec", "snt", "sattn", "stt", "stl", "sx", "sz"))
        sktok, svtok, srr, sy1, so = (sb(n, [NS, H, P]) for n in ("sktok", "svtok", "srr", "sy1", "so"))
        sts = sb("sts", [P, 2, H, NS])
        svd = sb("svd", [NS, H, P])
        vdb = sb("vdb", [NS, H, DEC_BATCH, P])
        stc, st = E.stc, E.st
        tab4 = sb("s_tab4", [T, KEYS])
        wraw = sb("wraw", [P, 2, D_MODEL])
        G = {n: sem("s_" + n) for n in (
            "stc_turned ext_made conv_done silu_done squared sums norms pows tables "
            "turned_rows rows_copied out_rows turned_kv kv_copied read_states states_copied decay decay_exp gm dec kqm pairs tt tl z_mm z m solved "
            "r_made y1 vd attn_mm o_made o_squared o_eps o_pow o_scaled o_turned delta_gated su su_read st_stored "
            "tab4 tab_copied step w_hi".split())}
        w_in, w_lo = ([sem(f"s_{n}{u}") for u in range(2)] for n in ("w_in", "w_lo"))
        block = ctx.enter_context(nc.Block())

        @block.sync
        def _(sp):
            def load_w(k):
                if k >= 2:
                    sp.wait_ge(w_lo[k % 2], k // 2)
                sp.dma_start(wraw[:, k % 2, :], D.w_out[P * k:P * k + P, :]).then_inc(w_in[k % 2], 16)

            load_w(0)
            load_w(1)
            sp.wait_ge(G["kv_copied"], 2)
            for b in range(DEC_BATCH):
                for y, out in ((0, D.out_k), (1, D.out_v)):
                    sp.dma_start(out[b, PAST - T:PAST, :], kv_tok[T * b:T * b + T, y, :]).then_inc(G["out_rows"], 16)
            load_w(2)
            load_w(3)
            sp.wait_ge(G["rows_copied"], 3)
            for b in range(DEC_BATCH):
                sp.dma_start(D.new_conv_s[b], raw_tok[T * b + 1:T * b + T, :]).then_inc(G["out_rows"], 16)
            sp.wait_ge(G["tab4"], 1)
            for h in range(SW_HEADS):
                sp.dma_start(E.tab[T * h:T * h + T, :], tab4[:]).then_inc(G["tab_copied"], 16)
            for k in range(4, KT):
                load_w(k)
            load_rows(sp, D.cache_k, 0, env.kn, env.kf, env.k_in)
            load_mix(sp, D, env, 0, 0)
            load_mix(sp, D, env, 1, 1)
            sp.wait_ge(G["su_read"], 2 * H)
            sp.dma_start(D.new_delta_s.rearrange("b h k v -> k b h v"), st[:]).then_inc(G["st_stored"], 16)
            sp.wait_ge(G["st_stored"], 16)
            sp.wait_ge(G["out_rows"], 16 * 3 * DEC_BATCH)
            sp.wait_ge(G["tab_copied"], 16 * SW_HEADS)

        @block.gpsimd
        def _(pool):
            n = [0]

            def then(ins):
                n[0] += 1
                ins.then_inc(G["tables"], 1)
                pool.wait_ge(G["tables"], n[0])

            then(pool.memset(x2[:], 0.0))
            odd = x2[:].rearrange("p (m two u) -> p m two u", two=2, u=2)[:, :, 1, :]
            then(pool.memset(odd, 1.0))
            then(pool.affine_select(out=odd, in_=odd, compare_op=ALU.is_ge, fill=0.0, base=0, pattern=[[-T, DEC_BATCH], [0, 2]], channel_multiplier=1))
            then(pool.affine_select(out=odd, in_=odd, compare_op=ALU.is_ge, fill=0.0, base=1, pattern=[[T, DEC_BATCH], [0, 2]], channel_multiplier=-1))
            then(pool.memset(shalf[:], -0.5))
            bh = lambda t: t[:].unsqueeze(1).to_broadcast([NS, H, NS])
            pool.tensor_tensor(sgm[:], bh(E.s_upto), E.sg_tok[:].unsqueeze(2).to_broadcast([NS, H, NS]), ALU.mult).then_inc(G["gm"], 1)
            def split_w(k):
                pool.wait_ge(G["w_hi"], k + 1)
                pool.tensor_tensor(E.wo_lo[:, k, :], wraw[:, k % 2, :], E.wo_hi[:, k, :].bitcast(F32), ALU.subtract).then_inc(w_lo[k % 2], 1)

            split_w(0)
            split_w(1)
            pool.wait_ge(G["norms"], 1)
            pool.tensor_tensor(srinv[:], ssum[:, 0, :], shalf[:], ALU.pow)
            pool.tensor_tensor(srq[:], ssum[:, 1, :], shalf[:], ALU.pow).then_inc(G["pows"], 1)
            for k in range(2, KT - 2):
                split_w(k)
            pool.wait_ge(G["vd"], 1)
            vd4 = svd[:].unsqueeze(2).to_broadcast([NS, H, DEC_BATCH, P])
            own = E.s_own[:].unsqueeze(1).unsqueeze(3).to_broadcast([NS, H, DEC_BATCH, P])
            pool.tensor_tensor(vdb[:], vd4, own, ALU.mult).then_inc(G["vd"], 1)
            pool.wait_ge(G["o_eps"], 1)
            pool.tensor_tensor(sors[:], sors[:], shalf[:], ALU.pow).then_inc(G["o_pow"], 1)

        @block.tensor
        def _(pe):
            pe.wait_ge(E.state_in, 32)
            for t in range(3 * NJ):
                mm = pe.transpose(bank[0][:, 24 * t:24 * t + 24], stc[:, P * t:P * t + P], ident[0:24, 0:24])
            mm.then_inc(G["stc_turned"], 1)
            for y, kind in enumerate(("wk", "wv")):
                for j in range(NJ):
                    mm = pe.transpose(bank[4 + y][0:NS, P * j:P * j + P], sam[:, KINDS.index(kind), j, :], ident[:])
                mm.then_inc(G["turned_kv"], 1)
            for y in range(3):
                for j in range(NJ):
                    mm = pe.transpose(bank[1 + y][0:NS, P * j:P * j + P], sam[:, y, j, :], ident[:])
                mm.then_inc(G["turned_rows"], 1)
            pe.wait_ge(G["gm"], 1)
            pe.matmul(bank[6][0:NS, 0:H * NS], E.s_after[:], flat(sgm[:]), start=True, stop=True).then_inc(G["decay"], 1)
            pe.wait_ge(G["squared"], 1)
            for x in range(2):
                for h in range(H):
                    mm = pe.matmul(bank[7][0:NS, H * x + h:H * x + h + 1], ssq2[:, x, h, :], E.ones[:, 0:1], start=True, stop=True)
            mm.then_inc(G["sums"], 1)
            pe.wait_ge(G["decay_exp"], 1)
            for h in range(H):
                for x in range(2):
                    mm = pe.matmul(bank[6][0:NS, (2 * h + x) * NS:(2 * h + x) * NS + NS], skq[:, 0, h, :], skq[:, x, h, :], start=True, stop=True)
            mm.then_inc(G["kqm"], 1)
            pe.wait_ge(G["rows_copied"], 3)
            for x, t in ((0, skq[:, 0]), (1, svc[:])):
                for h in range(H):
                    mm = pe.transpose(bank[1 + x][0:NS, P * h:P * h + P], t[:, h, :], ident[:])
            mm.then_inc(G["turned_rows"], 1)
            pe.wait_ge(G["kv_copied"], 2)
            for b in range(DEC_BATCH):
                for h in range(H):
                    out = bank[4][:, 0:2 * H * NS].rearrange("p (x h t) -> p x h t", x=2, h=H)[:, :, h, T * b:T * b + T]
                    mm = pe.matmul(out, st[:, b, h, :], skq[:, :, h, T * b:T * b + T], start=True, stop=True)
            mm.then_inc(G["read_states"], 1)
            pe.wait_ge(G["tt"], 1)
            for h in range(H):
                mm = pe.transpose(bank[0][0:NS, NS * h:NS * h + NS], stt[:, h, :], ident[0:NS, 0:NS])
            mm.then_inc(G["pairs"], 1)
            pe.wait_ge(G["tl"], 1)
            for h in range(H):
                mm = pe.matmul(bank[5][0:NS, NS * h:NS * h + NS], sx[:, h, :], stl[:, h, :], start=True, stop=True)
            mm.then_inc(G["z_mm"], 1)
            pe.wait_ge(G["z"], 1)
            for h in range(H):
                mm = pe.matmul(bank[0][0:NS, NS * h:NS * h + NS], sz[:, h, :], stt[:, h, :], start=True, stop=True)
            mm.then_inc(G["m"], 1)
            pe.wait_ge(G["states_copied"], 1)
            pe.wait_ge(G["rows_copied"], 4)
            for x in range(2):
                for h in range(H):
                    mm = pe.transpose(bank[(3, 1)[x]][0:NS, P * h:P * h + P], sts[:, x, h, :], ident[:])
            mm.then_inc(G["read_states"], 1)
            pe.wait_ge(G["tt"], 2)
            pe.wait_ge(G["r_made"], 1)
            for h in range(H):
                mm = pe.matmul(bank[3][0:NS, P * h:P * h + P], stt[:, h, :], srr[:, h, :], start=True, stop=True)
            mm.then_inc(G["solved"], 1)
            pe.wait_ge(G["y1"], 1)
            for h in range(H):
                mm = pe.matmul(bank[4][0:NS, P * h:P * h + P], sattn[:, h, :], sy1[:, h, :], start=True, stop=True)
            mm.then_inc(G["attn_mm"], 1)
            pe.wait_ge(G["vd"], 2)
            for h in range(H):
                for x in range(2):
                    n = 2 * h + x
                    if n >= 2:
                        pe.wait_ge(G["su_read"], n - 1)
                    pe.matmul(bank[6 + x][:], sktok[:, h, :], flat(vdb[:, h, 4 * x:4 * x + 4, :]), start=True, stop=True).then_inc(G["su"], 1)
            pe.wait_ge(G["o_scaled"], 1)
            for h in range(H):
                mm = pe.transpose(bank[5][:, NS * h:NS * h + NS], so[:, h, :], ident[0:NS, 0:NS])
            mm.then_inc(G["o_turned"], 1)

        @block.scalar
        def _(act):
            def split_w(k):
                act.wait_ge(w_in[k % 2], 16 * (k // 2) + 16)
                act.activation(E.wo_hi[:, k, :], wraw[:, k % 2, :], ACT.Copy).then_inc(G["w_hi"], 1)

            for y in range(2):
                act.wait_ge(G["turned_kv"], y + 1)
                act.activation(kv_tok[:, y, :], bank[4 + y][0:NS, :], ACT.Copy).then_inc(G["kv_copied"], 1)
            for y in range(3):
                act.wait_ge(G["turned_rows"], y + 1)
                act.activation(raw_tok[:, QK_W * y:QK_W * (y + 1)], bank[1 + y][0:NS, :], ACT.Copy).then_inc(G["rows_copied"], 1)
            split_w(0)
            act.wait_ge(G["decay"], 1)
            act.activation(flat(sdec[:]), bank[6][0:NS, 0:H * NS], ACT.Exp).then_inc(G["decay_exp"], 1)
            act.wait_ge(G["conv_done"], 1)
            c = lambda y: cacc[:, NJ * y:NJ * (y + 1)].rearrange("p a b t -> p a (b t)")
            act.activation(skq[:, 0], c(1), ACT.Silu)
            act.activation(skq[:, 1], c(0), ACT.Silu)
            act.activation(svc[:], c(2), ACT.Silu).then_inc(G["silu_done"], 1)
            act.wait_ge(G["turned_rows"], 4)
            act.activation(flat(sktok[:]), bank[1][0:NS, :], ACT.Copy).then_inc(G["rows_copied"], 1)
            act.activation(flat(svtok[:]), bank[2][0:NS, :], ACT.Copy).then_inc(G["rows_copied"], 1)
            for k in range(1, 4):
                split_w(k)
            act.wait_ge(G["read_states"], 1)
            act.activation(sts[:].rearrange("p x h t -> p (x h t)"), bank[4][:, 0:2 * H * NS], ACT.Copy).then_inc(G["states_copied"], 1)
            act.wait_ge(G["pairs"], 1)
            act.activation(flat(stl[:]), bank[0][0:NS, 0:H * NS], ACT.Copy).then_inc(G["tl"], 1)
            act.wait_ge(G["z_mm"], 1)
            act.activation(flat(sz[:]), bank[5][0:NS, 0:H * NS], ACT.Copy).then_inc(G["z"], 1)
            split_w(4)
            split_w(5)
            act.wait_ge(G["o_made"], 1)
            for h in range(H):
                ins = act.activation(srr[:, h, :], so[:, h, :], ACT.Square, accum_out=soss[:, h:h + 1])
            ins.then_inc(G["o_squared"], 1)
            split_w(6)
            split_w(7)

        @block.vector
        def _(dve):
            n = [0]

            def then(ins):
                n[0] += 1
                ins.then_inc(G["step"], 1)
                dve.wait_ge(G["step"], n[0])

            dve.tensor_copy(ext[:, :, :, TAIL:], sam[:, 0:3].rearrange("p y j (b t) -> p (y j) b t", t=T))
            dve.wait_ge(G["stc_turned"], 1)
            then(dve.tensor_copy(ext[:, :, :, 0:TAIL], bank[0][:, 0:24 * 3 * NJ].rearrange("p (a b r) -> p a b r", b=DEC_BATCH, r=TAIL)))
            w = lambda r: E.conv_wt[:, :, r].unsqueeze(2).unsqueeze(3).to_broadcast([P, 3 * NJ, DEC_BATCH, T])
            then(dve.tensor_tensor(cacc[:], ext[:, :, :, 0:T], w(0), ALU.mult))
            for r in range(1, CONV_W):
                then(dve.tensor_tensor(ctmp[:], ext[:, :, :, r:r + T], w(r), ALU.mult))
                then(dve.tensor_tensor(cacc[:], cacc[:], ctmp[:], ALU.add))
            dve.sem_inc(G["conv_done"], 1)
            at = SEQ - P - NEAR
            dve.tensor_copy(tab4[:, 0:NEAR].rearrange("p (j m) -> p j m", j=T), E.win[0:T, at:at + NEAR].rearrange("p (m j) -> p j m", j=T))
            dve.tensor_copy(tab4[:, NEAR:NEAR + FARS].rearrange("p (r m) -> p r m", r=T), E.win[0:T, 0:T].unsqueeze(2).to_broadcast([T, T, FAR]))
            dve.tensor_copy(tab4[:, NEAR + FARS:], E.win[0:T, SEQ - P:SEQ - P + T]).then_inc(G["tab4"], 1)
            dve.wait_ge(G["silu_done"], 1)
            dve.tensor_tensor(ssq2[:], skq[:], skq[:], ALU.mult).then_inc(G["squared"], 1)
            dve.wait_ge(G["sums"], 1)
            then(dve.tensor_scalar(ssum[:].rearrange("p x h -> p (x h)"), bank[7][0:NS, 0:2 * H], EPS, None, ALU.add))
            dve.sem_inc(G["norms"], 1)
            then(dve.reciprocal(sd2[:], ssum[:, 0, :]))
            then(dve.tensor_tensor(sd2[:], sd2[:], E.s_beta[:], ALU.mult))
            s32 = lambda t: t[:].unsqueeze(2).to_broadcast([NS, H, NS])
            s128 = lambda t: t[:].unsqueeze(2).to_broadcast([NS, H, P])
            m32 = lambda t: t.unsqueeze(1).to_broadcast([NS, H, NS])
            tok = lambda t: t[0:NS, :].rearrange("p (h d) -> p h d", h=H)
            dve.wait_ge(G["decay_exp"], 1)
            then(dve.tensor_tensor(sdec[:], sdec[:], m32(E.s_upto[:]), ALU.mult))
            dve.wait_ge(G["kqm"], 1)
            kq = bank[6][0:NS, 0:2 * H * NS].rearrange("p (h x t) -> p h x t", h=H, x=2)
            dve.tensor_tensor(sattn[:], kq[:, :, 1], sdec[:], ALU.mult)
            then(dve.tensor_tensor(snt[:], kq[:, :, 0], sdec[:], ALU.mult))
            then(dve.tensor_tensor(snt[:], snt[:], s32(sd2), ALU.mult))
            dve.wait_ge(G["tables"], 5)
            dve.tensor_tensor(sx[:], snt[:], m32(x2[:]), ALU.mult)
            then(dve.tensor_tensor(stt[:], snt[:], m32(E.pair[0:NS, 0:NS]), ALU.mult))
            dve.tensor_tensor(stt[:], stt[:], m32(ident[0:NS, 0:NS]), ALU.add).then_inc(G["tt"], 1)
            dve.wait_ge(G["pows"], 1)
            then(dve.tensor_tensor(srinv[:], srinv[:], ssum[:, 0, :], ALU.mult))
            then(dve.tensor_scalar(srq[:], srq[:], DK ** -0.5, None, ALU.mult))
            then(dve.tensor_tensor(srq2[:], srq[:], srq[:], ALU.mult))
            then(dve.tensor_scalar(srq2[:], srq2[:], 1.0 / DK, None, ALU.mult))
            dve.wait_ge(G["rows_copied"], 5)
            then(dve.tensor_tensor(svtok[:], svtok[:], s128(srinv), ALU.mult))
            dve.wait_ge(G["m"], 1)
            dve.tensor_tensor(stt[:], stt[:], bank[0][0:NS, 0:H * NS].rearrange("p (h t) -> p h t", h=H), ALU.subtract).then_inc(G["tt"], 1)
            dve.wait_ge(G["read_states"], 2)
            dve.tensor_tensor(so[:], tok(bank[1]), s128(E.s_egc), ALU.mult)
            then(dve.tensor_tensor(srr[:], tok(bank[3]), s128(E.s_egc), ALU.mult))
            dve.tensor_tensor(srr[:], svtok[:], srr[:], ALU.subtract).then_inc(G["r_made"], 1)
            dve.wait_ge(G["solved"], 1)
            dve.tensor_tensor(sy1[:], tok(bank[3]), s128(sd2), ALU.mult).then_inc(G["y1"], 1)
            dve.wait_ge(G["y1"], 1)
            dve.tensor_tensor(svd[:], sy1[:], s128(E.s_dl), ALU.mult).then_inc(G["vd"], 1)
            dve.wait_ge(G["attn_mm"], 1)
            dve.tensor_tensor(so[:], so[:], tok(bank[4]), ALU.add).then_inc(G["o_made"], 1)
            for h in range(H):
                for x in range(2):
                    dve.wait_ge(G["su"], 2 * h + x + 1)
                    for b in range(4):
                        s = st[:, 4 * x + b, h, :]
                        ins = dve.scalar_tensor_tensor(out=s, in0=s, scalar=E.s_gl[:, h, 4 * x + b:4 * x + b + 1], in1=bank[6 + x][:, P * b:P * b + P],
                                                       op0=ALU.mult, op1=ALU.add)
                    ins.then_inc(G["su_read"], 1)
            dve.wait_ge(G["o_squared"], 1)
            then(dve.tensor_tensor(sors[:], soss[:], srq2[:], ALU.mult))
            dve.tensor_scalar(sors[:], sors[:], EPS, None, ALU.add).then_inc(G["o_eps"], 1)
            dve.wait_ge(G["o_pow"], 1)
            then(dve.tensor_tensor(sors[:], sors[:], srq[:], ALU.mult))
            dve.tensor_tensor(so[:], so[:], s128(sors), ALU.mult).then_inc(G["o_scaled"], 1)
            dve.wait_ge(G["o_turned"], 1)
            dve.scalar_tensor_tensor(out=E.mix_s[:, 0:NJ, :], in0=bank[5][:, 0:H * NS].rearrange("p (h t) -> p h t", h=H), scalar=E.g_dn[:, 0:1],
                                     in1=sam[:, KINDS.index("za")], op0=ALU.mult, op1=ALU.mult).then_inc(G["delta_gated"], 1)
            for k in range(KT - 2, KT):
                dve.wait_ge(G["w_hi"], k + 1)
                dve.tensor_tensor(E.wo_lo[:, k, :], wraw[:, k % 2, :], E.wo_hi[:, k, :].bitcast(F32), ALU.subtract).then_inc(w_lo[k % 2], 1)


def output(nc, env, D):
    with ExitStack() as ctx:
        sem = env.sem
        sb = lambda n, s, d=F32: ctx.enter_context(nc.sbuf_tensor(n, s, d))
        bank = [ctx.enter_context(nc.psum_tensor(f"y_bank{i}", [P, CHUNK], F32)) for i in range(8)]
        near_ps, far_ps, s_ps, p_ps, y_ps = bank[0:2], bank[2:4], bank[4:6], bank[6], bank[7]
        E, ident, sam, tab = env, env.ident, env.sam, env.tab
        w_hi, w_lo = env.wo_hi, env.wo_lo
        kn, kf, vn, vf = env.kn, env.kf, sb("vn", [P, T, SW_WIDTH]), sb("vf", [FAR, T, SW_WIDTH])
        vnew = sb("vnew", [T, SW_WIDTH])
        kT = sb("kT", [P, 2, NEAR + FARS])
        DIAG = ROWS + 2 * T
        qw, kw = sb("qw", [P, NJ * DIAG]), sb("kw", [P, NJ, T])
        pr, pT = sb("pr", [ROWS, KEYS]), sb("pT", [P, 9 * ROWS])
        smax, snmax, slsum, slinv = sb("smax", [ROWS, 2]), sb("snmax", [ROWS, 1]), sb("slsum", [ROWS, 1]), sb("slinv", [ROWS, 1])
        o_sb = sb("o_sb", [ROWS, SW_WIDTH])
        O_AT = 9 * ROWS
        mx, mh, ml = env.mx, sb("mh", [P, 2, KT, P], F32R), sb("ml", [P, 2, KT, P], F32R)
        xt, yt = sb("xt", [P, 2, D_MODEL]), sb("yt", [P, 2, D_MODEL])
        gf, st, half_ = sb("gf", [P, D_MODEL]), sb("y_st", [P, 2, 3]), sb("y_half", [P, 1])
        G = {n: sem("a_" + n) for n in (
            "near_mm far_mm kT_act kT_dve kT_used scored masked max exped lsum normed pT_mm pT_out mixed o_out o_turned o_picked q_picked qw_zero seen".split())}
        O = {n: sem("y_" + n) for n in "const half hi lo mm added squared mean inv done".split()}
        k_in, v_in, m_in = env.k_in, sem("a_v_in"), env.m_in
        x_in, out = ([sem(f"y_{n}{u}") for u in range(2)] for n in ("x_in", "out"))
        block = ctx.enter_context(nc.Block())

        @block.sync
        def _(sp):
            def load_v(b):
                load_rows(sp, D.cache_v, b, vn, vf, v_in)
                sp.dma_start(vnew[:], D.out_v[bass.ds(b, 1), PAST - T:PAST, :].rearrange("a t c -> (a t) c")).then_inc(v_in, 16)

            def load_x(n, u):
                sp.dma_start(xt[:, u, :], D.x[bass.ds(P * n, P), :]).then_inc(x_in[u], 16)

            load_x(0, 0)
            load_x(1, 1)
            load_v(0)
            sp.dma_start(gf[:], D.final_norm_g.unsqueeze(0).to_broadcast([P, D_MODEL])).then_inc(O["const"], 16)

            def store(b, load):
                if load:
                    sp.wait_ge(O["lo"], 2 * b + 1)
                    sp.sem_inc(G["seen"], 1)
                    load_mix(sp, D, env, 2 * b + 2, 0)
                    sp.wait_ge(G["far_mm"], NJ * b + NJ)
                    sp.sem_inc(G["seen"], 1)
                    load_rows(sp, D.cache_k, b + 1, kn, kf, k_in)
                for u in range(2):
                    sp.wait_ge(O["done"], 2 * b + u + 1)
                    sp.sem_inc(G["seen"], 1)
                    sp.dma_start(D.y[bass.ds(P * (2 * b + u), P), :], yt[:, u, :]).then_inc(out[u], 16)
                    if load:
                        load_x(2 * b + u + 2, u)
                        if u == 0:
                            sp.wait_ge(O["lo"], 2 * b + 2)
                            sp.sem_inc(G["seen"], 1)
                            load_mix(sp, D, env, 2 * b + 3, 1)
                if load:
                    sp.wait_ge(G["mixed"], b + 1)
                    sp.sem_inc(G["seen"], 1)
                    load_v(b + 1)

            with sp.Fori(0, DEC_BATCH - 1) as b:
                store(b, True)
            store(DEC_BATCH - 1, False)
            sp.dma_start(xt[0:NS, 0, :], D.x_sample).then_inc(x_in[0], 16)
            sp.wait_ge(O["done"], NT + 1)
            sp.dma_start(D.y_s, yt[0:NS, 0, :]).then_inc(out[0], 16)
            sp.wait_ge(out[0], 16 * (NT // 2 + 1))
            sp.wait_ge(out[1], 16 * (NT // 2))

        @block.gpsimd
        def _(pool):
            pool.memset(half_[:], -0.5).then_inc(O["half"], 1)
            pool.memset(qw[:], 0.0).then_inc(G["qw_zero"], 1)
            pool.wait_ge(O["half"], 1)

            def low(n, u):
                pool.wait_ge(O["hi"], n + 1)
                pool.tensor_tensor(ml[:, u], mx[:, u], mh[:, u].bitcast(F32), ALU.subtract).then_inc(O["lo"], 1)

            def root(n, u, rows):
                pool.wait_ge(O["mean"], n + 1)
                pool.tensor_tensor(st[0:rows, u, 2:3], st[0:rows, u, 1:2], half_[0:rows, :], ALU.pow).then_inc(O["inv"], 1)

            low(0, 0)
            low(1, 1)
            with pool.Fori(0, DEC_BATCH - 1) as b:
                low(2 * b + 2, 0)
                root(2 * b, 0, P)
                root(2 * b + 1, 1, P)
                low(2 * b + 3, 1)
            root(NT - 2, 0, P)
            root(NT - 1, 1, P)
            pool.wait_ge(O["hi"], NT + 1)
            pool.tensor_tensor(ml[:, 0, :, 0:NS], E.mix_s[:], mh[:, 0, :, 0:NS].bitcast(F32), ALU.subtract).then_inc(O["lo"], 1)
            root(NT, 0, NS)

        @block.tensor
        def _(pe):
            pe.sem_inc(G["kT_used"], 2)
            pe.sem_inc(O["mm"], 4)

            def half_tile(n, u, c, rows, k0=0, k1=KT):
                if k0 == 0:
                    pe.wait_ge(O["lo"], n + 1)
                    pe.wait_ge(O["added"], 2 * n + c + 1)
                cs = slice(CHUNK * c, CHUNK * (c + 1))
                for k in range(k0, k1):
                    pe.matmul(y_ps[0:rows, :], mh[:, u, k, 0:rows], w_hi[:, k, cs], start=(k == 0), stop=False)
                    pe.matmul(y_ps[0:rows, :], mh[:, u, k, 0:rows], w_lo[:, k, cs], start=False, stop=False)
                    mm = pe.matmul(y_ps[0:rows, :], ml[:, u, k, 0:rows], w_hi[:, k, cs], start=False, stop=(k == KT - 1))
                if k1 == KT:
                    mm.then_inc(O["mm"], 1)

            def turn(b, j):
                if j == 0:
                    pe.wait_ge(k_in, 32 * b + 32)
                pe.wait_ge(G["kT_act"], NJ * b + j + 1)
                pe.sem_inc(G["seen"], 1)
                for t in range(T):
                    mm = pe.transpose(near_ps[j % 2][:, P * t:P * t + P], kn[:, t, P * j:P * j + P], ident[:])
                mm.then_inc(G["near_mm"], 1)
                pe.wait_ge(G["kT_dve"], NJ * b + j + 1)
                pe.sem_inc(G["seen"], 1)
                for t in range(T):
                    mm = pe.transpose(far_ps[j % 2][:, FAR * t:FAR * t + FAR], kf[:, t, P * j:P * j + P], ident[0:FAR, 0:FAR])
                mm.then_inc(G["far_mm"], 1)

            def score(b, j):
                pe.wait_ge(G["kT_act"], 2 + NJ * b + j + 1)
                pe.wait_ge(G["kT_dve"], 2 + NJ * b + j + 1)
                if j == 0:
                    pe.wait_ge(G["q_picked"], b + 1)
                    pe.wait_ge(G["masked"], 2 * b + 2)
                pe.sem_inc(G["seen"], 1)
                q = lambda k: qw[:, ROWS * k:ROWS * k + ROWS]
                a = dict(start=(j == 0), stop=(j == NJ - 1))
                pe.matmul(s_ps[0][0:ROWS, :], q(j), kT[:, j % 2, 0:NEAR], **a)
                pe.matmul(s_ps[1][0:ROWS, 0:FARS], q(j), kT[:, j % 2, NEAR:], **a).then_inc(G["kT_used"], 1)
                if j == NJ - 1:
                    for k in range(NJ):
                        mm = pe.matmul(s_ps[1][0:ROWS, FARS:FARS + T], q(k), kw[:, k, :], start=(k == 0), stop=(k == NJ - 1))
                    mm.then_inc(G["scored"], 1)

            def turn_p(b):
                pe.wait_ge(G["normed"], b + 1)
                pe.wait_ge(G["o_picked"], b + 1)
                pe.sem_inc(G["seen"], 1)
                for k in range(9):
                    w, at = (P, P * k) if k < T else (FAR, NEAR + FAR * (k - T)) if k < 2 * T else (T, NEAR + FARS)
                    mm = pe.transpose(p_ps[0:w, ROWS * k:ROWS * k + ROWS], pr[:, at:at + w], ident[0:ROWS, 0:ROWS])
                mm.then_inc(G["pT_mm"], 1)

            def mix(b):
                pe.wait_ge(v_in, 48 * b + 48)
                pe.wait_ge(G["pT_out"], b + 1)
                pe.sem_inc(G["seen"], 1)
                for k in range(9):
                    v, w = (vn[:, k, :], P) if k < T else (vf[:, k - T, :], FAR) if k < 2 * T else (vnew[:], T)
                    mm = pe.matmul(s_ps[0][0:ROWS, :], pT[0:w, ROWS * k:ROWS * k + ROWS], v, start=(k == 0), stop=(k == 8))
                mm.then_inc(G["mixed"], 1)

            def turn_o(b):
                pe.wait_ge(G["o_out"], b + 1)
                pe.sem_inc(G["seen"], 1)
                for j in range(NJ):
                    mm = pe.transpose(p_ps[:, O_AT + ROWS * j:O_AT + ROWS * j + ROWS], o_sb[:, P * j:P * j + P], ident[0:ROWS, 0:ROWS])
                mm.then_inc(G["o_turned"], 1)

            with pe.Fori(0, DEC_BATCH) as b:
                turn(b, 0)
                turn(b, 1)
                half_tile(2 * b, 0, 0, P)
                score(b, 0)
                score(b, 1)
                turn(b, 2)
                turn(b, 3)
                half_tile(2 * b, 0, 1, P)
                score(b, 2)
                score(b, 3)
                half_tile(2 * b + 1, 1, 0, P, 0, 5)
                turn_p(b)
                half_tile(2 * b + 1, 1, 0, P, 5, KT)
                mix(b)
                half_tile(2 * b + 1, 1, 1, P)
                turn_o(b)
            for c in range(2):
                half_tile(NT, 0, c, NS)

        @block.scalar
        def _(act):
            act.sem_inc(G["kT_act"], 2)

            def high(n, u, i):
                act.wait_ge(m_in[u], 16 * i + 16)
                act.wait_ge(O["mm"], 2 * n + 2)
                act.activation(mh[:, u], mx[:, u], ACT.Copy).then_inc(O["hi"], 1)

            def square(n, u, rows):
                act.wait_ge(O["added"], 1 + 2 * n + 2)
                act.activation(xt[0:rows, u, :], yt[0:rows, u, :], ACT.Square, accum_out=st[0:rows, u, 0:1]).then_inc(O["squared"], 1)

            def turned(b, j):
                act.wait_ge(G["kT_used"], NJ * b + j + 1)
                act.wait_ge(G["near_mm"], NJ * b + j + 1)
                act.activation(kT[:, j % 2, 0:NEAR], near_ps[j % 2][:], ACT.Copy).then_inc(G["kT_act"], 1)

            def step(b, more):
                for j in range(NJ):
                    turned(b, j)
                if more:
                    high(2 * b + 2, 0, b + 1)
                act.wait_ge(G["max"], b + 1)
                act.activation(pr[:], pr[:], ACT.Exp, bias=snmax[:, 0:1], accum_out=slsum[:, 0:1]).then_inc(G["exped"], 1)
                square(2 * b, 0, P)
                act.wait_ge(G["pT_mm"], b + 1)
                for w, a, z in ((P, 0, T), (FAR, T, 2 * T), (T, 2 * T, 9)):
                    ins = act.activation(pT[0:w, ROWS * a:ROWS * z], p_ps[0:w, ROWS * a:ROWS * z], ACT.Copy)
                ins.then_inc(G["pT_out"], 1)
                act.wait_ge(G["mixed"], b + 1)
                act.activation(o_sb[:], s_ps[0][0:ROWS, :], ACT.Copy).then_inc(G["o_out"], 1)
                square(2 * b + 1, 1, P)
                if more:
                    high(2 * b + 3, 1, b + 1)

            high(0, 0, 0)
            high(1, 1, 0)
            with act.Fori(0, DEC_BATCH - 1) as b:
                step(b, True)
            step(DEC_BATCH - 1, False)
            act.wait_ge(G["o_picked"], 1 + DEC_BATCH)
            act.activation(mh[:, 0, :, 0:NS], E.mix_s[:], ACT.Copy).then_inc(O["hi"], 1)
            square(NT, 0, NS)

        @block.vector
        def _(dve):
            dve.sem_inc(G["kT_dve"], 2)
            dve.sem_inc(G["masked"], 2)
            dve.sem_inc(G["o_picked"], 1)
            dve.sem_inc(O["added"], 1)
            dve.wait_ge(O["const"], 16)
            dve.wait_ge(G["qw_zero"], 1)

            def pick_q(b):
                t = bass.ds(T * b, T)
                for e in range(2):
                    half = slice(HD * e, HD * e + HD)
                    dve.tensor_copy(qw[half, :].rearrange("p (j z) -> p j z", z=DIAG)[:, :, T * e:T * e + T], sam[half, KINDS.index("wq"), :, t])
                dve.tensor_copy(kw[:], sam[:, KINDS.index("wk"), :, t]).then_inc(G["q_picked"], 1)

            def turned(b, j):
                dve.wait_ge(G["kT_used"], NJ * b + j + 1)
                dve.wait_ge(G["far_mm"], NJ * b + j + 1)
                dve.tensor_copy(kT[:, j % 2, NEAR:], far_ps[j % 2][:, 0:FARS]).then_inc(G["kT_dve"], 1)

            def add(n, u, c, rows):
                cs = slice(CHUNK * c, CHUNK * (c + 1))
                dve.wait_ge(O["mm"], 4 + 2 * n + c + 1)
                dve.tensor_tensor(yt[0:rows, u, cs], y_ps[0:rows, :], xt[0:rows, u, cs], ALU.add).then_inc(O["added"], 1)

            def mean(n, u, rows):
                dve.wait_ge(O["squared"], n + 1)
                dve.tensor_scalar(st[0:rows, u, 1:2], st[0:rows, u, 0:1], 1.0 / D_MODEL, EPS, ALU.mult, ALU.add).then_inc(O["mean"], 1)

            def scale(n, u, rows):
                dve.wait_ge(O["inv"], n + 1)
                y = yt[0:rows, u, :]
                dve.scalar_tensor_tensor(out=y, in0=y, scalar=st[0:rows, u, 2:3], in1=gf[0:rows, :], op0=ALU.mult, op1=ALU.mult).then_inc(O["done"], 1)

            def ready(u, i, stored):
                dve.wait_ge(x_in[u], 16 * i + 16)
                if stored:
                    dve.wait_ge(out[u], 16 * i)

            def step(b, first):
                turned(b, 0)
                turned(b, 1)
                pick_q(b)
                ready(0, b, not first)
                add(2 * b, 0, 0, P)
                turned(b, 2)
                turned(b, 3)
                add(2 * b, 0, 1, P)
                dve.wait_ge(G["scored"], b + 1)
                dve.sem_inc(G["seen"], 1)
                for x, (a, z) in enumerate(((0, NEAR), (NEAR, KEYS))):
                    dve.tensor_tensor_reduce(pr[:, a:z], s_ps[x][0:ROWS, 0:z - a], tab[:, a:z], SCALE, -3.0e38, ALU.add, ALU.max,
                                             smax[:, x:x + 1]).then_inc(G["masked"], 1)
                dve.wait_ge(G["masked"], 2 * b + 4)
                dve.tensor_reduce(snmax[:], smax[:], AX.X, ALU.max, negate=True).then_inc(G["max"], 1)
                dve.wait_ge(G["exped"], b + 1)
                dve.reciprocal(slinv[:], slsum[:]).then_inc(G["lsum"], 1)
                dve.wait_ge(G["lsum"], b + 1)
                dve.tensor_scalar(pr[:], pr[:], slinv[:, 0:1], None, ALU.mult).then_inc(G["normed"], 1)
                ready(1, b, not first)
                add(2 * b + 1, 1, 0, P)
                mean(2 * b, 0, P)
                scale(2 * b, 0, P)
                add(2 * b + 1, 1, 1, P)
                mean(2 * b + 1, 1, P)
                scale(2 * b + 1, 1, P)
                dve.wait_ge(G["o_turned"], b + 1)
                t = bass.ds(T * b, T)
                for e in range(2):
                    half = slice(HD * e, HD * e + HD)
                    o = p_ps[half, O_AT:O_AT + NJ * DIAG].rearrange("p (j z) -> p j z", z=DIAG)[:, :, T * e:T * e + T]
                    ins = dve.tensor_tensor(E.mix_s[half, NJ:2 * NJ, t], o, sam[half, KINDS.index("zb"), :, t], ALU.mult)
                ins.then_inc(G["o_picked"], 1)

            step(0, True)
            with dve.Fori(1, DEC_BATCH) as b:
                step(b, False)
            ready(0, DEC_BATCH, True)
            for c in range(2):
                add(NT, 0, c, NS)
            mean(NT, 0, NS)
            scale(NT, 0, NS)


class Env:
    pass


class Dram:
    pass


def in_phase(nc, env, phase, D):
    mine = []

    def sem(name):
        mine.append(nc.alloc_semaphore(name=name))
        return mine[-1]

    env.sem = sem
    phase(nc, env, D)
    nc.all_engine_barrier()
    nc.clear_and_free_semaphores(mine)
    nc.all_engine_barrier()


def hybrid_step(nc, x_prompt, x_sample, state_conv, state_delta, cache_k_win, cache_v_win, norm_g, final_norm_g, w_in, conv_w,
                a_log, dt_bias, dn_norm_g, w_out, y_prompt, y_sample, new_conv_prompt, new_delta_prompt, new_k_prompt, new_v_prompt,
                new_conv_sample, new_delta_sample, new_k_sample, new_v_sample):
    env, D = Env(), Dram()
    D.x, D.y = x_prompt[0], y_prompt[0]
    D.x_sample, D.y_s = (t.rearrange("b t d -> (b t) d") for t in (x_sample, y_sample))
    D.state_conv, D.state_delta, D.new_conv_s, D.new_delta_s = state_conv[0], state_delta[0], new_conv_sample[0], new_delta_sample[0]
    D.cache_k, D.cache_v, D.out_k, D.out_v = (t[0].rearrange("b n h d -> b n (h d)") for t in (cache_k_win, cache_v_win, new_k_sample, new_v_sample))
    D.norm_g, D.final_norm_g, D.w_in, D.conv_w = norm_g[0], final_norm_g, w_in[0], conv_w[0]
    D.a_log, D.dt_bias, D.dn_norm_g, D.w_out = a_log[0], dt_bias[0], dn_norm_g[0], w_out[0]
    D.new_conv, D.new_delta = new_conv_prompt[0, 0], new_delta_prompt[0, 0]
    D.new_k, D.new_v = (t[0, 0].rearrange("n h d -> n (h d)") for t in (new_k_prompt, new_v_prompt))
    scratch = lambda n, s: nc.dram_tensor(n, s, F32, kind="Internal").ap()
    D.qk_ch, D.z_ch = scratch("qk_ch", [2, QK_W, SEQ]), scratch("z_ch", [2, QK_W, SEQ])
    D.k_tok, D.v_tok = scratch("k_tok", [SEQ, QK_W]), scratch("v_tok", [SEQ, QK_W])
    D.wqk, D.mix = scratch("wqk", [2, 2, SW_WIDTH, SEQ]), scratch("mix", [D_MODEL, SEQ])
    with ExitStack() as ctx:
        constants(nc, env, ctx)
        in_phase(nc, env, project, D)
        gate_tensors(nc, env, ctx)
        with ExitStack() as mine:
            mixer_operands(nc, env, mine)
            in_phase(nc, env, gates, D)
            in_phase(nc, env, mixers, D)
        tail_tensors(nc, env, ctx)
        in_phase(nc, env, sample, D)
        in_phase(nc, env, output, D)


_INS = ["x_prompt", "x_sample", "state_conv", "state_delta", "cache_k_win", "cache_v_win", "norm_g", "final_norm_g",
        "w_in", "conv_w", "a_log", "dt_bias", "dn_norm_g", "w_out"]
_OUTS = [(1, 2048, 1024), (8, 4, 1024), (1, 1, 3, 1536), (1, 1, 4, 128, 128), (1, 1, 2048, 8, 64), (1, 1, 2048, 8, 64),
         (1, 8, 3, 1536), (1, 8, 4, 128, 128), (1, 8, 2048, 8, 64), (1, 8, 2048, 8, 64)]


def kernel(**inputs):
    import numpy as _np
    import concourse.bacc as _bacc
    from concourse import mybir as _mybir
    from concourse.bass_utils import run_bass_kernel_spmd as _run

    nc = _bacc.Bacc("TRN2", target_bir_lowering=False, num_devices=1)
    arrays, args = {}, []
    for name in _INS:
        a = _np.ascontiguousarray(inputs[name])
        arrays[f"in_{name}_dram"] = a
        args.append(nc.dram_tensor(f"in_{name}_dram", a.shape, _mybir.dt.from_np(a.dtype), kind="ExternalInput").ap())
    for i, shape in enumerate(_OUTS):
        args.append(nc.dram_tensor(f"out_{i}_dram", shape, _mybir.dt.from_np(_np.dtype("float32")), kind="ExternalOutput").ap())
    hybrid_step(nc, *args)
    r = _run(nc, [arrays], core_ids=[0])
    return tuple(r.results[0][f"out_{i}_dram"] for i in range(len(_OUTS)))
```
